# Optimizing a Trainium2 kernel written in Bass

```python
import math
import jax, jax.numpy as jnp
from jax import lax
import numpy as np

D_MODEL = 1024
BATCH = 1
SEQ = 2048
DEPTH = 1
DEC_BATCH = 8
DEC_SEQ = 4
PAST_LEN = 8192
PAGE_SIZE = 128

HEAD_DIM = 64
MIX_WIDTH = D_MODEL
N_HEADS_SB = (MIX_WIDTH // HEAD_DIM) // 2
N_HEADS_DIL = MIX_WIDTH // HEAD_DIM - N_HEADS_SB
W_SB = N_HEADS_SB * HEAD_DIM
W_DIL = N_HEADS_DIL * HEAD_DIM
DILATIONS = ((128, 1), (512, 4), (2048, 16))
W_MAX = max(w for w, _ in DILATIONS)
ROT_DIM = HEAD_DIM // 4
ROPE_THETA = 500000.0
Q_BLOCK = 128
PLE_DIM = 256
SB_BIAS_INIT = -8.0
EPS = 1e-6

kernel_name = "hymba_stickbreak_dilated_decoder_step"

def _rmsnorm(x, g):
    xf = x.astype(jnp.float32)
    out = xf * lax.rsqrt(jnp.mean(xf * xf, axis=-1, keepdims=True) + EPS)
    return (out * g.astype(jnp.float32)).astype(x.dtype)

def _rope(x, pos):
    half = ROT_DIM // 2
    inv = jnp.power(ROPE_THETA, -(jnp.arange(half, dtype=jnp.float32) * 2.0 / ROT_DIM))
    ang = pos.astype(jnp.float32)[:, None] * inv[None, :]
    cos = jnp.cos(ang)[:, None, :]
    sin = jnp.sin(ang)[:, None, :]
    xf = x.astype(jnp.float32)
    x1 = xf[..., :half]
    x2 = xf[..., half:ROT_DIM]
    out = jnp.concatenate([x1 * cos - x2 * sin, x2 * cos + x1 * sin, xf[..., ROT_DIM:]], axis=-1)
    return out.astype(x.dtype)

def _heads(t):
    return t.reshape(t.shape[:-1] + (-1, HEAD_DIM))

def _project(x, attn_norm, w_in):
    h = _rmsnorm(x, attn_norm)
    proj = jnp.einsum('bsd,de->bse', h, w_in)
    q_sb, k_sb, v_sb, z_sb, q_dl, k_dl, v_dl, z_dl = jnp.split(proj, 8, axis=-1)
    return (_heads(q_sb), _heads(k_sb), _heads(v_sb), z_sb,
            _heads(q_dl), _heads(k_dl), _heads(v_dl), z_dl)

def _stick_breaking(q, k, v, q_pos, k_pos, bias):
    z = jnp.einsum('bqhd,bkhd->bhqk', q, k).astype(jnp.float32) / math.sqrt(HEAD_DIM)
    z = z + bias.astype(jnp.float32)[None, :, None, None]
    mask = (k_pos[None, :] < q_pos[:, None])[None, None]
    log_1m = jnp.where(mask, jax.nn.log_sigmoid(-z), 0.0)
    rest = lax.cumsum(log_1m, axis=3, reverse=True) - log_1m
    a = jnp.where(mask, jnp.exp(jax.nn.log_sigmoid(z) + rest), 0.0)
    return jnp.einsum('bhqk,bkhd->bqhd', a.astype(v.dtype), v)

def _stick_breaking_prompt(q, k, v, bias):
    b, s, h, dh = q.shape
    nb = s // Q_BLOCK
    qb = q.reshape(b, nb, Q_BLOCK, h, dh).transpose(1, 0, 2, 3, 4)
    qpos = jnp.arange(s, dtype=jnp.int32).reshape(nb, Q_BLOCK)
    kpos = jnp.arange(s, dtype=jnp.int32)
    out = lax.map(lambda a: _stick_breaking(a[0], k, v, a[1], kpos, bias), (qb, qpos))
    return out.transpose(1, 0, 2, 3, 4).reshape(b, s, h, dh)

def _dilated_prompt(q, k, v, window, dil):
    b, s, h, dh = q.shape
    n_keys = window // dil
    blk = n_keys
    L = s // dil
    nb = -(-L // blk)
    pad = nb * blk - L

    def sub(t):
        t = t.reshape(b, L, dil, h, dh).transpose(0, 2, 1, 3, 4)
        t = jnp.pad(t, ((0, 0), (0, 0), (0, pad), (0, 0), (0, 0)))
        return t.reshape(b, dil, nb, blk, h, dh)

    def band(t):
        prev = jnp.pad(t, ((0, 0), (0, 0), (1, 0), (0, 0), (0, 0), (0, 0)))[:, :, :-1]
        return jnp.concatenate([prev, t], axis=3)

    qs = sub(q)
    kb = band(sub(k))
    vb = band(sub(v))
    sc = jnp.einsum('bgnqhd,bgnkhd->bgnhqk', qs, kb).astype(jnp.float32) / math.sqrt(HEAD_DIM)
    i = jnp.arange(blk)[:, None]
    j = jnp.arange(2 * blk)[None, :]
    dist = blk + i - j
    in_win = (dist >= 0) & (dist <= n_keys)
    mask = in_win[None] & ((jnp.arange(nb)[:, None, None] > 0) | (j[None] >= blk))
    sc = jnp.where(mask[None, None, :, None], sc, -jnp.inf)
    m = jnp.max(sc, axis=-1, keepdims=True)
    pw = jnp.exp(sc - m)
    l = jnp.sum(pw, axis=-1, keepdims=True)
    o = jnp.einsum('bgnhqk,bgnkhd->bgnqhd', (pw / l).astype(v.dtype), vb)
    lse = (m + jnp.log(l))[..., 0]
    o = o.reshape(b, dil, nb * blk, h, dh)[:, :, :L].transpose(0, 2, 1, 3, 4).reshape(b, s, h, dh)
    lse = lse.transpose(0, 1, 2, 4, 3).reshape(b, dil, nb * blk, h)[:, :, :L]
    lse = lse.transpose(0, 2, 1, 3).reshape(b, s, h)
    return o, lse

def _dilated_sample(q, k_all, v_all, window, dil, n_buf):
    n_keys = window // dil
    t = q.shape[1]
    idx = n_buf + jnp.arange(t)[:, None] - dil * jnp.arange(n_keys + 1)[None, :]
    valid = idx >= 0
    idx = jnp.maximum(idx, 0)
    kg = k_all[:, idx]
    vg = v_all[:, idx]
    sc = jnp.einsum('bqhd,bqjhd->bhqj', q, kg).astype(jnp.float32) / math.sqrt(HEAD_DIM)
    sc = jnp.where(valid[None, None], sc, -jnp.inf)
    m = jnp.max(sc, axis=-1, keepdims=True)
    pw = jnp.exp(sc - m)
    l = jnp.sum(pw, axis=-1, keepdims=True)
    o = jnp.einsum('bhqj,bqjhd->bqhd', (pw / l).astype(v_all.dtype), vg)
    lse = (m + jnp.log(l))[..., 0].transpose(0, 2, 1)
    return o, lse

def _combine(outs, lses):
    w = jax.nn.softmax(jnp.stack(lses, axis=0), axis=0)
    o = jnp.sum(w[..., None] * jnp.stack(outs, axis=0).astype(jnp.float32), axis=0)
    return o.astype(outs[0].dtype)

def _qk_norm_rope(q, k, pos, q_norm, k_norm):
    return _rope(_rmsnorm(q, q_norm), pos), _rope(_rmsnorm(k, k_norm), pos)

def _merge(x, o_sb, z_sb, o_dl, z_dl, p, out_norm_sb, out_norm_dil, w_out, w_ple, w_ple_gate):
    b, s = x.shape[0], x.shape[1]
    y_sb = _rmsnorm(o_sb.reshape(b, s, W_SB), out_norm_sb) * jax.nn.silu(z_sb)
    y_dl = _rmsnorm(o_dl.reshape(b, s, W_DIL), out_norm_dil) * jax.nn.silu(z_dl)
    x = x + jnp.einsum('bse,ed->bsd', jnp.concatenate([y_sb, y_dl], axis=-1), w_out)
    gate = jax.nn.sigmoid(jnp.einsum('bsd,de->bse', x, w_ple_gate))
    return x + gate * jnp.einsum('bsp,pd->bsd', p, w_ple)

def setup_inputs(seed: int = 0) -> dict:
    key = jax.random.key(seed)
    ks = jax.random.split(key, 24)
    f32 = jnp.float32
    n_pages = PAST_LEN // PAGE_SIZE
    n_used = DEC_BATCH * n_pages
    n_phys = n_used + max(1, n_used // 4)
    n_buf = min(W_MAX, PAST_LEN)
    nrm = lambda k, shp, sc=1.0: jax.random.normal(k, shp, f32) * sc
    page_table = jax.random.permutation(ks[0], n_phys)[:n_used].reshape(DEC_BATCH, n_pages).astype(jnp.int32)
    return {
        "x_prompt": nrm(ks[1], (BATCH, SEQ, D_MODEL)),
        "x_sample": nrm(ks[2], (DEC_BATCH, DEC_SEQ, D_MODEL)),
        "cache_k_sb": nrm(ks[3], (DEPTH, n_phys, PAGE_SIZE, N_HEADS_SB, HEAD_DIM)),
        "cache_v_sb": nrm(ks[4], (DEPTH, n_phys, PAGE_SIZE, N_HEADS_SB, HEAD_DIM)),
        "cache_k_win": nrm(ks[5], (DEPTH, DEC_BATCH, n_buf, N_HEADS_DIL, HEAD_DIM)),
        "cache_v_win": nrm(ks[6], (DEPTH, DEC_BATCH, n_buf, N_HEADS_DIL, HEAD_DIM)),
        "page_table": page_table,
        "p_prompt": nrm(ks[7], (DEPTH, BATCH, SEQ, PLE_DIM)),
        "p_sample": nrm(ks[8], (DEPTH, DEC_BATCH, DEC_SEQ, PLE_DIM)),
        "attn_norm": 1.0 + nrm(ks[9], (DEPTH, D_MODEL), 0.02),
        "w_in": nrm(ks[10], (DEPTH, D_MODEL, 4 * MIX_WIDTH), D_MODEL ** -0.5),
        "sb_bias": SB_BIAS_INIT + nrm(ks[18], (DEPTH, N_HEADS_SB), 0.1),
        "q_norm_dil": 1.0 + nrm(ks[11], (DEPTH, HEAD_DIM), 0.02),
        "k_norm_dil": 1.0 + nrm(ks[12], (DEPTH, HEAD_DIM), 0.02),
        "out_norm_sb": 1.0 + nrm(ks[13], (DEPTH, W_SB), 0.02),
        "out_norm_dil": 1.0 + nrm(ks[14], (DEPTH, W_DIL), 0.02),
        "w_out": nrm(ks[15], (DEPTH, MIX_WIDTH, D_MODEL), MIX_WIDTH ** -0.5),
        "w_ple": nrm(ks[16], (DEPTH, PLE_DIM, D_MODEL), PLE_DIM ** -0.5),
        "w_ple_gate": nrm(ks[17], (DEPTH, D_MODEL, D_MODEL), D_MODEL ** -0.5),
    }

def reference(x_prompt, x_sample, cache_k_sb, cache_v_sb, cache_k_win, cache_v_win, page_table,
              p_prompt, p_sample, attn_norm, w_in, sb_bias, q_norm_dil, k_norm_dil, out_norm_sb,
              out_norm_dil, w_out, w_ple, w_ple_gate):
    seq = x_prompt.shape[1]
    dec_b, dec_s = x_sample.shape[0], x_sample.shape[1]
    n_pages = page_table.shape[1]
    past = n_pages * cache_k_sb.shape[2]
    pos_p = jnp.arange(seq, dtype=jnp.int32)
    pos_s = past + jnp.arange(dec_s, dtype=jnp.int32)
    kpos_s = jnp.arange(past + dec_s, dtype=jnp.int32)
    wp = min(W_MAX, seq)
    xp, xs = x_prompt, x_sample
    ksb_p, vsb_p, ksb_s, vsb_s = [], [], [], []
    kw_p, vw_p, kw_s, vw_s = [], [], [], []
    for i in range(DEPTH):
        qa, ka, va, za, qb, kb, vb, zb = _project(xp, attn_norm[i], w_in[i])
        o_sb = _stick_breaking_prompt(qa, ka, va, sb_bias[i])
        qb, kb = _qk_norm_rope(qb, kb, pos_p, q_norm_dil[i], k_norm_dil[i])
        outs, lses = [], []
        for (win, dil) in DILATIONS:
            o, l = _dilated_prompt(qb, kb, vb, win, dil)
            outs.append(o)
            lses.append(l)
        o_dl = _combine(outs, lses)
        xp = _merge(xp, o_sb, za, o_dl, zb, p_prompt[i], out_norm_sb[i], out_norm_dil[i],
                    w_out[i], w_ple[i], w_ple_gate[i])
        ksb_p.append(ka)
        vsb_p.append(va)
        kw_p.append(kb[:, seq - wp:])
        vw_p.append(vb[:, seq - wp:])
        qa, ka, va, za, qb, kb, vb, zb = _project(xs, attn_norm[i], w_in[i])
        k_past = cache_k_sb[i][page_table].reshape(dec_b, past, N_HEADS_SB, HEAD_DIM)
        v_past = cache_v_sb[i][page_table].reshape(dec_b, past, N_HEADS_SB, HEAD_DIM)
        k_all = jnp.concatenate([k_past.astype(ka.dtype), ka], axis=1)
        v_all = jnp.concatenate([v_past.astype(va.dtype), va], axis=1)
        o_sb = _stick_breaking(qa, k_all, v_all, pos_s, kpos_s, sb_bias[i])
        qb, kb = _qk_norm_rope(qb, kb, pos_s, q_norm_dil[i], k_norm_dil[i])
        n_buf = cache_k_win.shape[2]
        kw_all = jnp.concatenate([cache_k_win[i].astype(kb.dtype), kb], axis=1)
        vw_all = jnp.concatenate([cache_v_win[i].astype(vb.dtype), vb], axis=1)
        outs, lses = [], []
        for (win, dil) in DILATIONS:
            o, l = _dilated_sample(qb, kw_all, vw_all, win, dil, n_buf)
            outs.append(o)
            lses.append(l)
        o_dl = _combine(outs, lses)
        xs = _merge(xs, o_sb, za, o_dl, zb, p_sample[i], out_norm_sb[i], out_norm_dil[i],
                    w_out[i], w_ple[i], w_ple_gate[i])
        ksb_s.append(ka)
        vsb_s.append(va)
        kw_s.append(kw_all[:, dec_s:])
        vw_s.append(vw_all[:, dec_s:])
    return (xp, xs,
            jnp.stack(ksb_p), jnp.stack(vsb_p), jnp.stack(ksb_s), jnp.stack(vsb_s),
            jnp.stack(kw_p), jnp.stack(vw_p), jnp.stack(kw_s), jnp.stack(vw_s))


_drawn_inputs = setup_inputs


def setup_inputs(seed=0):
    import zlib

    import numpy as np

    out = dict(_drawn_inputs(seed))
    spreads = {}
    factors = {'attn_norm': 2.82,
     'q_norm_dil': 8.0,
     'k_norm_dil': 3.121,
     'out_norm_sb': 8.0,
     'out_norm_dil': 8.0}
    for name, (base, spread) in spreads.items():
        noise = np.random.default_rng([zlib.crc32(name.encode()), seed]).standard_normal(out[name].shape)
        drawn = base * np.exp(spread * noise) if base else spread * noise
        out[name] = __import__('jax').numpy.asarray(drawn.astype(out[name].dtype))
    for name, factor in factors.items():
        out[name] = (out[name] * factor).astype(out[name].dtype)
    return out
```

```python
import concourse.bass as bass
from concourse import mybir
from contextlib import ExitStack

F32 = mybir.dt.float32
F32R = mybir.dt.float32r
I32 = mybir.dt.int32
ALU = mybir.AluOpType
ACT = mybir.ActivationFunctionType
AX = mybir.AxisListType

P = 128
D = 1024
SEQ = 2048
DEC_B, DEC_S = 8, 4
NS = DEC_B * DEC_S
H, DH = 8, 64
W = H * DH
PAIRS = H // 2
PAGE, PAGES = 128, 64
WIN = 2048
PLE = 256
EPS = 1e-6
TILES = SEQ // P
KC = D // P
ROT = DH // 4
NEG = -3.0e38
BIG = 2.0 ** 60
LN_EXP_SET = 6


class Mem:

    def __init__(self, nc, ctx, tag):
        self.nc, self.ctx, self.tag = nc, ctx, tag
        self.used = []
        ctx.callback(self.clear)

    def clear(self):
        self.nc.clear_and_free_semaphores(self.used)
        self.nc.all_engine_barrier()

    def sb(self, name, shape, dt=F32):
        return self.ctx.enter_context(self.nc.sbuf_tensor(f"{self.tag}_{name}", shape, dt))

    def ps(self, name, shape):
        return self.ctx.enter_context(self.nc.psum_tensor(f"{self.tag}_{name}", shape, F32))

    def sem(self, name):
        self.used.append(self.nc.alloc_semaphore(name=f"{self.tag}_{name}"))
        return self.used[-1]

    def sems(self, name, n):
        return [self.sem(f"{name}{i}") for i in range(n)]


def load_exp_ln_table(nc, act):
    act.add_instruction(mybir.InstLoadActFuncSet(
        name=nc.get_next_instruction_name(), act_func_set_id=LN_EXP_SET,
        engine=mybir.EngineType.Activation, ins=[], outs=[]))


def flat(ap):
    n = len(ap.shape)
    if n == 5:
        return ap.rearrange("a b s h d -> (a b s) (h d)")
    return ap


def hold(eng, sem, value):
    eng.wait_ge(sem, value)
    if not isinstance(value, int):
        eng.sem_inc(TICK[0], 1)


TICK = [None]


def steps(eng, body):
    for item in (0, 1, 2):
        body(item, item % 2, item // 2)
    with eng.Fori(1, TILES // 2 - 1) as o:
        body(1 + 2 * o, 1, o)
        body(2 + 2 * o, 0, o + 1)
    for item in (TILES - 1, TILES):
        body(item, item % 2, item // 2)


def following(item, slot, use):
    return item + 1, 1 - slot, use + slot


def first(item):
    return isinstance(item, int) and item == 0


def last(item):
    return isinstance(item, int) and item == TILES


def project(nc, t, half):
    mixer_b = half == 1
    GROUPS = 4
    C0 = half * GROUPS * W
    QK_STEPS = 6
    ctx = ExitStack()
    with ctx:
        m = Mem(nc, ctx, f"proj{half}")
        w_hi = m.sb("w_hi", [P, KC, GROUPS * W], F32R)
        w_lo = m.sb("w_lo", [P, KC, GROUPS * W], F32R)
        x_in = m.sb("x_in", [P, 2, D])
        xT_hi = m.sb("xT_hi", [P, 2, KC, P], F32R)
        xT_lo = m.sb("xT_lo", [P, 2, KC, P], F32R)
        out = m.sb("out", [P, 2, GROUPS * W])
        junk = m.sb("junk", [P, D])
        g_attn = m.sb("g_attn", [P, KC])
        ident = m.sb("ident", [P, P])
        stat = m.sb("stat", [P, 2, 4])
        mhalf = m.sb("mhalf", [P, 2 * H])
        if mixer_b:
            qk_sq = m.sb("qk_sq", [P, 2 * W])
            g_qk = m.sb("g_qk", [P, 2, DH])
            rope = m.sb("rope", [P, TILES + 1, ROT])
            hstat = m.sb("hstat", [P, 2, 3, 2 * H])
            rt = m.sb("rt", [P, 4, 2 * H, ROT // 2])
        ps_T = m.ps("ps_T", [P, 2, 512])
        ps_G = m.ps("ps_G", [P, GROUPS, 512])

        w_loaded = m.sems("w_loaded", 2)
        w_hi_done = m.sem("w_hi_done")
        w_split = m.sem("w_split")
        consts = m.sem("consts")
        mhalf_set = m.sem("mhalf_set")
        x_loaded = m.sems("x_loaded", 2)
        x_squared = m.sem("x_squared")
        x_turned = m.sem("x_turned")
        hi_done = m.sem("hi_done")
        lo_done = m.sem("lo_done")
        mean_done = m.sem("mean_done")
        rms_done = m.sem("rms_done")
        grp_done = m.sem("grp_done")
        evacuated = m.sem("evacuated")
        stored = [m.sems(f"stored{g}_", 2) for g in range(GROUPS)]
        win_copied = m.sem("win_copied")
        if mixer_b:
            gq_set = m.sem("gq_set")
            sq_done = m.sem("sq_done")
            ssum_done = m.sem("ssum_done")
            hmean_done = m.sem("hmean_done")
            hrms_done = m.sem("hrms_done")
            qk_step = m.sem("qk_step")

        def rows_of(item):
            return NS if first(item) else P

        w_rows = t["w_in"][0].rearrange("(c p) e -> p c e", p=P)
        x_p, x_s = t["x_prompt"][0], t["x_sample"].rearrange("b s d -> (b s) d")
        if mixer_b:
            dst_p = [t["q_dl"], flat(t["k_win_p"]), flat(t["v_win_p"]), t["z_dl"]]
            win_rows = [t[n][0].rearrange("b s h d -> b s (h d)")[:, WIN - DEC_S:WIN, :]
                        for n in ("k_win_s", "v_win_s")]
            dst_s = [t["q_dl_s"], win_rows[0], win_rows[1], t["z_dl_s"]]
        else:
            dst_p = [t["q_sb"], flat(t["k_sb_p"]), flat(t["v_sb_p"]), t["z_sb"]]
            dst_s = [t["q_sb_s"], flat(t["k_sb_s"]), flat(t["v_sb_s"]), t["z_sb_s"]]
        old_win = t["cache_v_win" if mixer_b else "cache_k_win"][0].rearrange("b s h d -> b s (h d)")
        new_win = t["v_win_s" if mixer_b else "k_win_s"][0].rearrange("b s h d -> b s (h d)")
        HALF_WIN = (WIN - DEC_S) // 2
        block = ctx.enter_context(nc.Block())

        @block.sync
        def _(sp):
            sp.dma_start(ident[:, :], t["ident"][:, :]).then_inc(consts, 16)
            with nc.allow_non_contiguous_dma(reason="the 1024 weights of the norm, once"):
                sp.dma_start(g_attn[:, :], t["attn_norm"][0].rearrange("(c p) -> p c", p=P)).then_inc(consts, 16)
            if mixer_b:
                for i, n in enumerate(("q_norm_dil", "k_norm_dil")):
                    sp.dma_start(g_qk[:, i, :], t[n][0:1, :].to_broadcast([P, DH])).then_inc(consts, 16)
                sp.dma_start(rope[:, :, :], t["rope"].rearrange("n p r -> p n r")).then_inc(consts, 16)
            for c in range(2 * KC):
                if c >= 2:
                    hold(sp, w_split, c - 1)
                sp.dma_start(x_in[:, c % 2, :], w_rows[:, c // 2, C0 + (c % 2) * D:C0 + (c % 2 + 1) * D]) \
                    .then_inc(w_loaded[c % 2], 16)
            hold(sp, w_split, 2 * KC)

            def load(item, slot):
                n = rows_of(item)
                src = x_s if first(item) else x_p[bass.ts(item - 1, P), :]
                sp.dma_start(x_in[0:n, slot, :], src).then_inc(x_loaded[slot], 16)

            def body(item, slot, use):
                n = rows_of(item)
                if not last(item):
                    if not first(item):
                        hold(sp, x_squared, item)
                        hold(sp, x_turned, 2 * item)
                    load(item + 1, 1 - slot)
                for g in range(GROUPS):
                    if mixer_b and g < 2:
                        hold(sp, qk_step, QK_STEPS * item + QK_STEPS)
                    else:
                        hold(sp, evacuated, GROUPS * item + g + 1)
                    dst = dst_s[g] if first(item) else dst_p[g][bass.ts(item - 1, P), :]
                    sp.dma_start(dst, out[0:n, slot, g * W:(g + 1) * W]).then_inc(stored[g][slot], 16)

            load(0, 0)
            steps(sp, body)
            for g in range(GROUPS):
                hold(sp, stored[g][0], 16 * (TILES // 2 + 1))
                hold(sp, stored[g][1], 16 * (TILES // 2))

        @block.gpsimd
        def _(pool):
            nc.gpsimd.memset(mhalf[:, :], -0.5).then_inc(mhalf_set, 1)
            hold(pool, mhalf_set, 1)

            def rms(item, slot, use):
                n = rows_of(item)
                hold(pool, x_squared, item + 1)
                if not (isinstance(item, int) and item < 2):
                    hold(pool, evacuated, GROUPS * item - GROUPS)
                nc.gpsimd.tensor_scalar(stat[0:n, slot, 1:2], stat[0:n, slot, 0:1], 1.0 / D, EPS,
                                        ALU.mult, ALU.add).then_inc(mean_done, 1)
                hold(pool, mean_done, item + 1)
                nc.gpsimd.tensor_tensor(stat[0:n, slot, 2:3], stat[0:n, slot, 1:2], mhalf[0:n, 0:1], ALU.pow) \
                    .then_inc(rms_done, 1)
                hold(pool, rms_done, 2 * item + 1)
                nc.gpsimd.tensor_scalar(stat[0:n, slot, 3:4], stat[0:n, slot, 2:3], 1.0 / 8, None, ALU.mult) \
                    .then_inc(rms_done, 1)

            def body(item, slot, use):
                n = rows_of(item)
                if not last(item):
                    rms(*following(item, slot, use))
                if not first(item):
                    b, j = (item - 1) // 2 if isinstance(item, int) else (use if slot else use - 1), 1 - slot
                    pool.dma_start(new_win[bass.ds(b, 1), j * HALF_WIN:(j + 1) * HALF_WIN, :],
                                   old_win[bass.ds(b, 1), DEC_S + j * HALF_WIN:DEC_S + (j + 1) * HALF_WIN, :]) \
                        .then_inc(win_copied, 16)
                if mixer_b:
                    hold(pool, ssum_done, item + 1)
                    nc.gpsimd.tensor_scalar(hstat[0:n, slot, 1, :], hstat[0:n, slot, 0, :], 1.0 / DH, EPS,
                                            ALU.mult, ALU.add).then_inc(hmean_done, 1)
                    hold(pool, hmean_done, item + 1)
                    nc.gpsimd.tensor_tensor(hstat[0:n, slot, 2, :], hstat[0:n, slot, 1, :], mhalf[0:n, :], ALU.pow) \
                        .then_inc(hrms_done, 1)

            rms(0, 0, 0)
            steps(pool, body)
            hold(pool, win_copied, 16 * 2 * DEC_B)

        @block.vector
        def _(dve):
            dve.wait_ge(consts, 80 if mixer_b else 32)
            if mixer_b:
                nc.vector.tensor_scalar(g_qk[:, 0, :], g_qk[:, 0, :], 1.0 / 8, None, ALU.mult).then_inc(gq_set, 1)
                dve.wait_ge(gq_set, 1)
            for c in range(2 * KC):
                k, cols = c // 2, slice((c % 2) * D, (c % 2 + 1) * D)
                dve.wait_ge(w_loaded[c % 2], 16 * (c // 2 + 1))
                nc.vector.tensor_scalar(w_hi[:, k, cols], x_in[:, c % 2, :], g_attn[:, k:k + 1], None, ALU.mult) \
                    .then_inc(w_hi_done, 1)
                dve.wait_ge(w_hi_done, c + 1)
                nc.vector.scalar_tensor_tensor(out=w_lo[:, k, cols], in0=x_in[:, c % 2, :], scalar=g_attn[:, k:k + 1],
                                               in1=w_hi[:, k, cols].bitcast(F32), op0=ALU.mult,
                                               op1=ALU.subtract).then_inc(w_split, 1)

            def low_parts(item, slot, use):
                n = rows_of(item)
                for b in range(2):
                    dve.wait_ge(hi_done, 2 * item + b + 1)
                    src = ps_T[:, b, :].rearrange("p (c r) -> p c r", r=P)[:, :, 0:n]
                    nc.vector.tensor_tensor(xT_lo[:, slot, 4 * b:4 * b + 4, 0:n], src,
                                            xT_hi[:, slot, 4 * b:4 * b + 4, 0:n].bitcast(F32),
                                            ALU.subtract).then_inc(lo_done, 1)

            def norm_rotate(item, slot, use):
                n = rows_of(item)
                dve.wait_ge(sq_done, item + 1)
                nc.vector.tensor_reduce(hstat[0:n, slot, 0, :], qk_sq[0:n, :].rearrange("p (h d) -> p h d", d=DH),
                                        AX.X, ALU.add).then_inc(ssum_done, 1)
                qk = out[0:n, slot, 0:2 * W].rearrange("p (h d) -> p h d", d=DH)
                dve.wait_ge(hrms_done, item + 1)
                base = QK_STEPS * item
                nc.vector.tensor_tensor(qk, qk, hstat[0:n, slot, 2, :].unsqueeze(2).to_broadcast([n, 2 * H, DH]),
                                        ALU.mult).then_inc(qk_step, 1)
                dve.wait_ge(qk_step, base + 1)
                for i in range(2):
                    part = qk[:, i * H:(i + 1) * H, :]
                    nc.vector.tensor_tensor(part, part, g_qk[0:n, i:i + 1, :].to_broadcast([n, H, DH]),
                                            ALU.mult).then_inc(qk_step, 1)
                dve.wait_ge(qk_step, base + 3)
                x1, x2 = qk[:, :, 0:8], qk[:, :, 8:16]
                cos = rope[0:n, bass.ds(item, 1), 0:8].to_broadcast([n, 2 * H, 8])
                sin = rope[0:n, bass.ds(item, 1), 8:16].to_broadcast([n, 2 * H, 8])
                for i, (x, f) in enumerate(((x1, cos), (x2, sin), (x2, cos), (x1, sin))):
                    rot = nc.vector.tensor_tensor(rt[0:n, i], x, f, ALU.mult)
                rot.then_inc(qk_step, 1)
                dve.wait_ge(qk_step, base + 4)
                nc.vector.tensor_tensor(x1, rt[0:n, 0], rt[0:n, 1], ALU.subtract).then_inc(qk_step, 1)
                nc.vector.tensor_tensor(x2, rt[0:n, 2], rt[0:n, 3], ALU.add).then_inc(qk_step, 1)

            def body(item, slot, use):
                if not last(item):
                    low_parts(*following(item, slot, use))
                if mixer_b:
                    norm_rotate(item, slot, use)

            low_parts(0, 0, 0)
            steps(dve, body)

        @block.scalar
        def _(act):
            load_exp_ln_table(nc, act)

            def high_parts(item, slot, use):
                n = rows_of(item)
                act.wait_ge(x_loaded[slot], 16 * use + 16)
                nc.scalar.activation(junk[0:n, :], x_in[0:n, slot, :], ACT.Square,
                                     accum_out=stat[0:n, slot, 0:1]).then_inc(x_squared, 1)
                for b in range(2):
                    act.wait_ge(x_turned, 2 * item + b + 1)
                    src = ps_T[:, b, :].rearrange("p (c r) -> p c r", r=P)[:, :, 0:n]
                    nc.scalar.activation(xT_hi[:, slot, 4 * b:4 * b + 4, 0:n], src, ACT.Copy).then_inc(hi_done, 1)

            def body(item, slot, use):
                n = rows_of(item)
                act.wait_ge(rms_done, 2 * item + 2)
                for g in range(GROUPS):
                    act.wait_ge(grp_done, GROUPS * item + g + 1)
                    if not (isinstance(item, int) and item < 2):
                        act.wait_ge(stored[g][slot], 16 * use)
                    r = 3 if (g == 0 and not mixer_b) else 2
                    nc.scalar.activation(out[0:n, slot, g * W:(g + 1) * W], ps_G[0:n, g, :], ACT.Copy,
                                         scale=stat[0:n, slot, r:r + 1]).then_inc(evacuated, 1)
                    if g == 1:
                        if mixer_b:
                            act.wait_ge(evacuated, GROUPS * item + 2)
                            if not first(item):
                                act.wait_ge(ssum_done, item)
                            nc.scalar.activation(qk_sq[0:n, :], out[0:n, slot, 0:2 * W], ACT.Square) \
                                .then_inc(sq_done, 1)
                        if not last(item):
                            high_parts(*following(item, slot, use))

            high_parts(0, 0, 0)
            steps(act, body)

        @block.tensor
        def _(pe):
            def turn(item, slot, use):
                n = rows_of(item)
                pe.wait_ge(x_loaded[slot], 16 * use + 16)
                for b in range(2):
                    if not first(item):
                        pe.wait_ge(lo_done, 2 * item - 1 + b)
                    for c in range(4):
                        k = 4 * b + c
                        last_t = nc.tensor.transpose(ps_T[:, b, c * P:c * P + n], x_in[0:n, slot, k * P:(k + 1) * P],
                                                     ident[0:n, 0:n])
                    last_t.then_inc(x_turned, 1)

            def body(item, slot, use):
                n = rows_of(item)
                pe.wait_ge(lo_done, 2 * item + 2)
                for g in range(GROUPS):
                    if not first(item):
                        pe.wait_ge(evacuated, GROUPS * item - GROUPS + g + 1)
                    for k in range(KC):
                        cols = slice(g * W, (g + 1) * W)
                        nc.tensor.matmul(ps_G[0:n, g, :], xT_hi[:, slot, k, 0:n], w_hi[:, k, cols],
                                         start=(k == 0), stop=False)
                        nc.tensor.matmul(ps_G[0:n, g, :], xT_hi[:, slot, k, 0:n], w_lo[:, k, cols],
                                         start=False, stop=False)
                        mm = nc.tensor.matmul(ps_G[0:n, g, :], xT_lo[:, slot, k, 0:n], w_hi[:, k, cols],
                                              start=False, stop=(k == KC - 1))
                    mm.then_inc(grp_done, 1)
                    if g == 1 and not last(item):
                        turn(*following(item, slot, use))

            pe.wait_ge(consts, 80 if mixer_b else 32)
            turn(0, 0, 0)
            pe.wait_ge(w_split, 2 * KC)
            steps(pe, body)


def stick_breaking_prompt(nc, t):
    QT = 512 // P
    NQ = TILES // QT
    ITEMS = []
    for Q in range(NQ):
        for s in range(QT * Q + QT):
            for h in range(2):
                ITEMS.append((Q, QT * Q + QT - 1 - s, h, s))
    NI = len(ITEMS)
    FILLS = 2 * NQ
    ZB = 6

    def first_col(i):
        Q, j, h, s = ITEMS[i]
        return max(0, j - QT * Q) * P

    def diagonal(i):
        return ITEMS[i][1] >= QT * ITEMS[i][0]

    def closes(i):
        return ITEMS[i][1] == 0

    DIAGS = sum(diagonal(i) for i in range(NI))
    CLOSES = sum(closes(i) for i in range(NI))

    def diags_to(i):
        return sum(diagonal(x) for x in range(i + 1))

    def closes_to(i):
        return sum(closes(x) for x in range(i + 1))

    ctx = ExitStack()
    with ctx:
        m = Mem(nc, ctx, "sbp")
        ident = m.sb("ident", [P, P])
        suffix = m.sb("suffix", [P, 2, P])
        suf_r = m.sb("suf_r", [P, P], F32R)
        bias = m.sb("bias", [P, H])
        bias_pair = m.sb("bias_pair", [P, 2])
        qk_in = m.sb("qk_in", [P, 2, TILES, P])
        v_all = m.sb("v_all", [P, TILES, W])
        T_hi = m.sb("T_hi", [P, 2, SEQ], F32R)
        T_lo = m.sb("T_lo", [P, 2, SEQ], F32R)
        el = m.sb("el", [P, 4, 512])
        sp_ = m.sb("sp", [P, 4, 512])
        sp_hi = m.sb("sp_hi", [P, 4, 512], F32R)
        sp_lo = m.sb("sp_lo", [P, 4, 512], F32R)
        S = m.sb("S", [P, 2, 2, 512])
        a = m.sb("a", [P, 4, 512])
        o_out = m.sb("o_out", [P, TILES, P])
        Z = m.ps("Z", [P, ZB, 512])
        O = m.ps("O", [P, 2, 512])

        consts = m.sem("consts")
        suf_done = m.sem("suf_done")
        v_loaded = m.sem("v_loaded")
        qk_loaded = m.sem("qk_loaded")
        turned = m.sem("turned")
        turn_hi = m.sem("turn_hi")
        turn_lo = m.sem("turn_lo")
        bias_set = m.sem("bias_set")
        z_done = m.sem("z_done")
        exp_done = m.sem("exp_done")
        cut_done = m.sem("cut_done")
        ln_done = m.sem("ln_done")
        sp_done = m.sem("sp_done")
        sp_masked = m.sem("sp_masked")
        hi_done = m.sem("hi_done")
        lo_done = m.sem("lo_done")
        S_done = m.sem("S_done")
        sum_done = m.sem("sum_done")
        a_done = m.sem("a_done")
        a_masked = m.sem("a_masked")
        av_done = m.sem("av_done")
        o_copied = m.sem("o_copied")
        o_stored = m.sem("o_stored")
        o_free = m.sem("o_free")

        q_rows = t["q_sb"].rearrange("(n p) c -> p n c", p=P)
        k_rows = flat(t["k_sb_p"]).rearrange("(n p) c -> p n c", p=P)
        v_rows = flat(t["v_sb_p"]).rearrange("(n p) c -> p n c", p=P)
        o_rows = t["o_sb"].rearrange("(n p) c -> p n c", p=P)
        block = ctx.enter_context(nc.Block())

        @block.sync
        def _(sp):
            sp.dma_start(ident[:, :], t["ident"][:, :]).then_inc(consts, 16)
            sp.dma_start(suffix[:, :, :], t["suffix"].rearrange("a p c -> p a c")).then_inc(consts, 16)
            sp.dma_start(bias[:, :], t["sb_bias"][0:1, :].to_broadcast([P, H])).then_inc(consts, 16)

            def load(p):
                sp.dma_start(qk_in[:, 0, :, :], q_rows[:, :, bass.ts(p, P)]).then_inc(qk_loaded, 16)
                sp.dma_start(qk_in[:, 1, :, :], k_rows[:, :, bass.ts(p, P)]).then_inc(qk_loaded, 16)

            def store(p):
                hold(sp, o_copied, CLOSES * p + CLOSES)
                sp.dma_start(o_rows[:, :, bass.ts(p, P)], o_out[:, :, :]).then_inc(o_stored, 16)
                hold(sp, o_stored, 16 * p + 16)
                sp.sem_inc(o_free, 1)

            sp.sem_inc(o_free, 1)
            load(0)
            sp.dma_start(v_all[:, :, :], v_rows).then_inc(v_loaded, 16)
            with sp.Fori(0, PAIRS - 1) as p:
                hold(sp, turned, FILLS * p + FILLS)
                load(p + 1)
                store(p)
            store(PAIRS - 1)
            sp.wait_ge(o_stored, 16 * PAIRS)

        @block.gpsimd
        def _(pool):
            with pool.Fori(0, PAIRS) as p:
                B, BD = NI * p, DIAGS * p
                for T in range(-2, NI + 2):
                    i = T + 2
                    if i < NI:
                        c = first_col(i)
                        hold(pool, sp_done, B + i + 1)
                        if diagonal(i):
                            blk = sp_[:, i % 4, c:c + P]
                            nc.gpsimd.affine_select(out=blk, in_=blk, compare_op=ALU.is_gt, fill=0.0, base=0,
                                                    pattern=[[1, P]], channel_multiplier=-1).then_inc(sp_masked, 1)
                            hold(pool, sp_masked, BD + diags_to(i))
                        if i >= 4:
                            hold(pool, sum_done, B + i - 3)
                        nc.gpsimd.tensor_copy(sp_hi[:, i % 4, c:512], sp_[:, i % 4, c:512]).then_inc(hi_done, 1)
                    i = T - 1
                    if 0 <= i < NI and diagonal(i):
                        c = first_col(i)
                        hold(pool, a_done, B + i + 1)
                        blk = a[:, i % 4, c:c + P]
                        nc.gpsimd.affine_select(out=blk, in_=blk, compare_op=ALU.is_gt, fill=0.0, base=0,
                                                pattern=[[1, P]], channel_multiplier=-1).then_inc(a_masked, 1)

        @block.vector
        def _(dve):
            dve.wait_ge(consts, 48)
            nc.vector.tensor_copy(suf_r[:, :], suffix[:, 0, :]).then_inc(suf_done, 1)
            with dve.Fori(0, PAIRS) as p:
                B, BF = NI * p, FILLS * p
                for f in range(FILLS):
                    dve.wait_ge(turn_hi, BF + f + 1)
                    if f == 0:
                        nc.vector.tensor_copy(bias_pair[:, :], bias[:, bass.ts(p, 2)]).then_inc(bias_set, 1)
                    cols = slice((f % NQ) * 512, (f % NQ + 1) * 512)
                    nc.vector.tensor_tensor(T_lo[:, f // NQ, cols], Z[:, f % ZB, :],
                                            T_hi[:, f // NQ, cols].bitcast(F32), ALU.subtract).then_inc(turn_lo, 1)
                for T in range(-4, NI):
                    i = T + 4
                    if i < NI:
                        dve.wait_ge(exp_done, B + i + 1)
                        c = first_col(i)
                        nc.vector.tensor_scalar(el[:, i % 4, c:512], el[:, i % 4, c:512], BIG, None, ALU.min) \
                            .then_inc(cut_done, 1)
                    i = T + 2
                    if 0 <= i < NI:
                        c, h = first_col(i), ITEMS[i][2]
                        dve.wait_ge(ln_done, B + i + 1)
                        nc.vector.scalar_tensor_tensor(out=sp_[:, i % 4, c:512], in0=Z[:, i % ZB, c:512],
                                                       scalar=bias_pair[:, h:h + 1], in1=el[:, i % 4, c:512],
                                                       op0=ALU.add, op1=ALU.max).then_inc(sp_done, 1)
                    i = T + 1
                    if 0 <= i < NI:
                        c, (Q, j, h, s) = first_col(i), ITEMS[i]
                        dve.wait_ge(hi_done, B + i + 1)
                        if i >= 4:
                            dve.wait_ge(sum_done, B + i - 3)
                        nc.vector.tensor_tensor(sp_lo[:, i % 4, c:512], sp_[:, i % 4, c:512],
                                                sp_hi[:, i % 4, c:512].bitcast(F32), ALU.subtract).then_inc(lo_done, 1)
                        if i >= 2:
                            dve.wait_ge(sum_done, B + i - 1)
                            dve.wait_ge(S_done, B + i - 1)
                        c0 = 512 if s == 0 else first_col(i - 2)
                        if c < c0:
                            op = nc.vector.tensor_copy(S[:, h, (s + 1) % 2, c:c0], sp_[:, i % 4, c:c0])
                        if c0 < 512:
                            op = nc.vector.tensor_tensor(S[:, h, (s + 1) % 2, c0:512], S[:, h, s % 2, c0:512],
                                                         sp_[:, i % 4, c0:512], ALU.add)
                        op.then_inc(S_done, 1)

        @block.scalar
        def _(act):
            load_exp_ln_table(nc, act)
            with act.Fori(0, PAIRS) as p:
                B, BF, BC = NI * p, FILLS * p, CLOSES * p
                for f in range(FILLS):
                    act.wait_ge(turned, BF + f + 1)
                    nc.scalar.activation(T_hi[:, f // NQ, (f % NQ) * 512:(f % NQ + 1) * 512], Z[:, f % ZB, :],
                                         ACT.Copy).then_inc(turn_hi, 1)
                for T in range(-4, NI + 4):
                    i = T + 4
                    if i < NI:
                        c, h = first_col(i), ITEMS[i][2]
                        act.wait_ge(z_done, B + i + 1)
                        if i >= 4:
                            act.wait_ge(sp_done, B + i - 3)
                        nc.scalar.activation(el[:, i % 4, c:512], Z[:, i % ZB, c:512], ACT.Exp,
                                             bias=bias_pair[:, h:h + 1]).then_inc(exp_done, 1)
                    i = T + 3
                    if 0 <= i < NI:
                        c = first_col(i)
                        act.wait_ge(cut_done, B + i + 1)
                        nc.scalar.activation(el[:, i % 4, c:512], el[:, i % 4, c:512], ACT.Ln, bias=1.0) \
                            .then_inc(ln_done, 1)
                    i = T - 1
                    if 0 <= i < NI:
                        c, h = first_col(i), ITEMS[i][2]
                        act.wait_ge(sum_done, B + i + 1)
                        if i >= 4:
                            act.wait_ge(av_done, B + i - 3 + 1)
                        nc.scalar.activation(a[:, i % 4, c:512], Z[:, i % ZB, c:512], ACT.Exp,
                                             bias=bias_pair[:, h:h + 1]).then_inc(a_done, 1)
                    i = T - 3
                    if 0 <= i < NI and closes(i):
                        Q, j, h, s = ITEMS[i]
                        act.wait_ge(av_done, B + i + 2)
                        if closes_to(i) == 1:
                            act.wait_ge(o_free, p + 1)
                        nc.scalar.activation(o_out[:, QT * Q:QT * Q + QT, h * DH:(h + 1) * DH],
                                             O[:, h, 0:QT * DH].rearrange("p (n d) -> p n d", d=DH), ACT.Copy) \
                            .then_inc(o_copied, 1)

        @block.tensor
        def _(pe):
            pe.wait_ge(consts, 48)
            pe.wait_ge(suf_done, 1)
            pe.wait_ge(v_loaded, 16)
            pe.sem_inc(av_done, 1)
            with pe.Fori(0, PAIRS) as p:
                B, BD, BF, BC = NI * p, DIAGS * p, FILLS * p, CLOSES * p
                pe.wait_ge(qk_loaded, 32 * p + 32)
                pe.wait_ge(av_done, B + 1)
                for f in range(FILLS):
                    if f >= ZB:
                        pe.wait_ge(turn_lo, BF + f - ZB + 1)
                    for n in range(4):
                        tr = nc.tensor.transpose(Z[:, f % ZB, n * P:(n + 1) * P], qk_in[:, f // NQ, 4 * (f % NQ) + n, :],
                                                 ident[:, :])
                    tr.then_inc(turned, 1)
                pe.wait_ge(turn_lo, BF + FILLS)
                for T in range(-4, NI + 2):
                    i = T + 4
                    if i < NI:
                        c, (Q, j, h, s) = first_col(i), ITEMS[i]
                        if i >= ZB:
                            pe.wait_ge(a_done, B + i - ZB + 1)
                        r, keys, qs = slice(h * DH, (h + 1) * DH), slice(j * P, (j + 1) * P), slice(Q * 512 + c, Q * 512 + 512)
                        for n, (kt, qt) in enumerate(((T_hi, T_hi), (T_lo, T_hi), (T_hi, T_lo))):
                            mm = nc.tensor.matmul(Z[:, i % ZB, c:512], kt[r, 1, keys], qt[r, 0, qs], start=(n == 0),
                                                  stop=(n == 2), skip_group_check=True)
                        mm.then_inc(z_done, 1)
                    i = T
                    if 0 <= i < NI:
                        c, (Q, j, h, s) = first_col(i), ITEMS[i]
                        if s > 0:
                            pe.wait_ge(S_done, B + i - 1)
                            c0 = first_col(i - 2)
                            nc.tensor.matmul(Z[:, i % ZB, c0:512], suffix[:, 1, :], S[:, h, s % 2, c0:512], start=False,
                                             stop=False, skip_group_check=True)
                        pe.wait_ge(lo_done, B + i + 1)
                        nc.tensor.matmul(Z[:, i % ZB, c:512], suf_r[:, :], sp_hi[:, i % 4, c:512], start=False, stop=False,
                                         skip_group_check=True)
                        nc.tensor.matmul(Z[:, i % ZB, c:512], suf_r[:, :], sp_lo[:, i % 4, c:512], start=False, stop=True,
                                         skip_group_check=True).then_inc(sum_done, 1)
                    i = T - 2
                    if 0 <= i < NI:
                        c, (Q, j, h, s) = first_col(i), ITEMS[i]
                        if diagonal(i):
                            pe.wait_ge(a_masked, BD + diags_to(i))
                        else:
                            pe.wait_ge(a_done, B + i + 1)
                        if s == 0 and Q > 0:
                            pe.wait_ge(o_copied, BC + 2 * Q - 1 + h)
                        for b in range(c // P, QT):
                            mm = nc.tensor.matmul(O[:, h, b * DH:(b + 1) * DH], a[:, i % 4, b * P:(b + 1) * P],
                                                  v_all[:, j, bass.ds(p * P + h * DH, DH)],
                                                  start=(s == 0 and b == QT - 1), stop=closes(i), skip_group_check=True)
                        mm.then_inc(av_done, 1)


def dilated_prompt(nc, t):
    DILS = (1, 4, 16)
    ITEMS = []
    for br, dil in enumerate(DILS):
        per = 4 if dil == 16 else 2
        for T in range(0, TILES, per):
            for h in range(2):
                ITEMS.append((br, T, h))
    NI = len(ITEMS)
    FILLS, FB = 8, 4

    def tiles(i):
        br, T, h = ITEMS[i]
        dil = DILS[br]
        runs = TILES // dil
        out = []
        for x in range(T, T + (4 if dil == 16 else 2)):
            g, n = x // runs, x % runs
            out.append((x, g + dil * P * n, n == 0))
        return out

    def blocks(i):
        return 1 if ITEMS[i][0] == 2 else 2

    def closes(i):
        return i + 1 == NI or (ITEMS[i + 1][0] != ITEMS[i][0])

    def branch_items_to(br):
        return sum(1 for x in ITEMS if x[0] <= br)

    ctx = ExitStack()
    with ctx:
        m = Mem(nc, ctx, "dil")
        ident = m.sb("ident", [P, P])
        masks = m.sb("masks", [P, 3, 512])
        qk_in = m.sb("qk_in", [P, 2, TILES, P])
        v_br = m.sb("v_br", [P, 2, TILES, P])
        T_hi = m.sb("T_hi", [P, 2, SEQ], F32R)
        T_lo = m.sb("T_lo", [P, 2, SEQ], F32R)
        sc = m.sb("sc", [P, 4, 512])
        pT = m.sb("pT", [P, 3, 512])
        nmax = m.sb("nmax", [P, 4, 4])
        rsum = m.sb("rsum", [P, 4, 4])
        inv = m.sb("inv", [P, 4, 4])
        keep = m.sb("keep", [P, 2, 2, TILES, 2])
        lse = m.sb("lse", [P, 2, TILES, 2])
        o_out = m.sb("o_out", [P, 2, TILES, P])
        Z = m.ps("Z", [P, 4, 512])
        ps_T = m.ps("ps_T", [P, 2, 512])
        O = m.ps("O", [P, 2, 512])

        consts = m.sem("consts")
        v_loaded = m.sems("v_loaded", 2)
        qk_loaded = m.sem("qk_loaded")
        turned = m.sem("turned")
        turn_hi = m.sem("turn_hi")
        turn_lo = m.sem("turn_lo")
        z_done = m.sem("z_done")
        masked = m.sem("masked")
        max_done = m.sem("max_done")
        exp_done = m.sem("exp_done")
        pt_done = m.sem("pt_done")
        pt_copied = m.sem("pt_copied")
        inv_done = m.sem("inv_done")
        av_done = m.sem("av_done")
        o_scaled = m.sem("o_scaled")
        kept = m.sem("kept")
        ln_done = m.sem("ln_done")
        lse_done = m.sem("lse_done")
        br_free = m.sem("br_free")
        stored = m.sems("stored", 2)

        q_rows = t["q_dl"].rearrange("(n p) c -> p n c", p=P)
        k_rows = flat(t["k_win_p"]).rearrange("(n p) c -> p n c", p=P)

        def run_rows(rows, br, g):
            dil = DILS[br]
            return rows.rearrange("(n p g) c -> g p n c", p=P, g=dil)[g]

        NB = 3

        def per_pairs(eng, body):
            with eng.Fori(0, PAIRS // 2) as pp:
                for u in range(2):
                    body(pp, u, 2 * pp + u)

        def bslot(u, br):
            return (NB * u + br) % 2

        def slot_dmas(pp, u, br):
            seen = [DILS[b] for v in range(2) for b in range(NB)
                    if bslot(v, b) == bslot(u, br) and (v, b) <= (u, br)]
            return sum(DILS) * pp + sum(seen)

        block = ctx.enter_context(nc.Block())

        @block.sync
        def _(sp):
            sp.dma_start(ident[:, :], t["ident"][:, :]).then_inc(consts, 16)
            sp.dma_start(masks[:, :, :], t["masks"].rearrange("a p c -> p a c")).then_inc(consts, 16)
            sp.sem_inc(br_free, 2)

            def body(pp, u, p):
                cols = bass.ts(p, P)
                hold(sp, av_done, NI * p + 1)
                sp.dma_start(qk_in[:, 0, :, :], q_rows[:, :, cols]).then_inc(qk_loaded, 16)
                sp.dma_start(qk_in[:, 1, :, :], k_rows[:, :, cols]).then_inc(qk_loaded, 16)
                for br, dil in enumerate(DILS):
                    s, runs = bslot(u, br), TILES // dil
                    if br == 2:
                        hold(sp, av_done, NI * p + 1 + branch_items_to(0))
                    for g in range(dil):
                        sp.dma_start(v_br[:, s, g * runs:(g + 1) * runs, :], run_rows(flat(t["v_win_p"]), br, g)[:, :, cols]) \
                            .then_inc(v_loaded[s], 16)
                for br, dil in enumerate(DILS):
                    s, runs = bslot(u, br), TILES // dil
                    hold(sp, o_scaled, NI * p + branch_items_to(br))
                    for g in range(dil):
                        sp.dma_start(run_rows(t["o_dil"][br], br, g)[:, :, cols], o_out[:, s, g * runs:(g + 1) * runs, :]) \
                            .then_inc(stored[s], 16)
                    hold(sp, lse_done, NB * p + br + 1)
                    for g in range(dil):
                        sp.dma_start(run_rows(t["lse_dil"][br], br, g)[:, :, bass.ts(p, 2)], lse[:, s, g * runs:(g + 1) * runs, :]) \
                            .then_inc(stored[s], 16)
                    hold(sp, stored[s], 2 * 16 * slot_dmas(pp, u, br))
                    sp.sem_inc(br_free, 1)

            per_pairs(sp, body)

        @block.vector
        def _(dve):
            dve.wait_ge(consts, 32)

            def body(pp, u, p):
                B, BF = NI * p, FILLS * p
                for f in range(FILLS):
                    dve.wait_ge(turn_hi, BF + f + 1)
                    cols = slice((f % 4) * 512, (f % 4 + 1) * 512)
                    nc.vector.tensor_tensor(T_lo[:, f // 4, cols], Z[:, f % FB, :],
                                            T_hi[:, f // 4, cols].bitcast(F32), ALU.subtract).then_inc(turn_lo, 1)
                for T in range(-1, NI + 3):
                    i = T + 1
                    if i < NI:
                        br, x, h = ITEMS[i]
                        kind = 2 if br == 2 else (0 if tiles(i)[0][2] else 1)
                        nt = len(tiles(i))
                        dve.wait_ge(z_done, B + i + 1)
                        if i >= 4:
                            dve.wait_ge(pt_done, B + i - 3)
                        nc.vector.tensor_tensor(sc[:, i % 4, :], Z[:, i % 4, :], masks[:, kind, :], ALU.add) \
                            .then_inc(masked, 1)
                        dve.wait_ge(masked, B + i + 1)
                        nc.vector.tensor_reduce(nmax[:, i % 4, 0:nt], sc[:, i % 4, :].rearrange("p (n k) -> p n k", n=nt),
                                                AX.X, ALU.max, negate=True).then_inc(max_done, 1)
                    i = T - 1
                    if 0 <= i < NI:
                        nt = len(tiles(i))
                        dve.wait_ge(exp_done, B + i + 1)
                        if i >= 4:
                            dve.wait_ge(o_scaled, B + i - 3)
                        nc.vector.reciprocal(inv[:, i % 4, 0:nt], rsum[:, i % 4, 0:nt]).then_inc(inv_done, 1)
                        br, x, h = ITEMS[i]
                        s = bslot(u, br)
                        if x == 0 and h == 0:
                            dve.wait_ge(br_free, NB * p + br + 1)
                        nc.vector.tensor_copy(keep[:, s, 0, x:x + nt, h], nmax[:, i % 4, 0:nt])
                        nc.vector.tensor_copy(keep[:, s, 1, x:x + nt, h], rsum[:, i % 4, 0:nt]).then_inc(kept, 1)
                    i = T - 3
                    if 0 <= i < NI:
                        br, x, h = ITEMS[i]
                        nt, s = len(tiles(i)), bslot(u, br)
                        dve.wait_ge(av_done, B + i + 2)
                        dve.wait_ge(inv_done, B + i + 1)
                        nc.vector.tensor_tensor(o_out[:, s, x:x + nt, h * DH:(h + 1) * DH],
                                                O[:, i % 2, 0:nt * DH].rearrange("p (n d) -> p n d", d=DH),
                                                inv[:, i % 4, 0:nt].unsqueeze(2).to_broadcast([P, nt, DH]), ALU.mult) \
                            .then_inc(o_scaled, 1)
                        if closes(i):
                            dve.wait_ge(ln_done, NB * p + br + 1)
                            nc.vector.tensor_tensor(lse[:, s, :, :], keep[:, s, 1, :, :], keep[:, s, 0, :, :],
                                                    ALU.subtract).then_inc(lse_done, 1)
                dve.wait_ge(o_scaled, B + NI)

            per_pairs(dve, body)

        @block.scalar
        def _(act):
            load_exp_ln_table(nc, act)

            def body(pp, u, p):
                B, BF = NI * p, FILLS * p
                for f in range(FILLS):
                    act.wait_ge(turned, BF + f + 1)
                    nc.scalar.activation(T_hi[:, f // 4, (f % 4) * 512:(f % 4 + 1) * 512], Z[:, f % FB, :],
                                         ACT.Copy).then_inc(turn_hi, 1)
                for T in range(0, NI + 2):
                    i = T
                    if i < NI:
                        nt = len(tiles(i))
                        w = 512 // nt
                        act.wait_ge(max_done, B + i + 1)
                        if i >= 4:
                            act.wait_ge(kept, B + i - 3)
                        for n in range(nt):
                            e = nc.scalar.activation(sc[:, i % 4, n * w:(n + 1) * w], sc[:, i % 4, n * w:(n + 1) * w],
                                                     ACT.Exp, bias=nmax[:, i % 4, n:n + 1],
                                                     accum_out=rsum[:, i % 4, n:n + 1])
                        e.then_inc(exp_done, 1)
                    i = T - 1
                    if 0 <= i < NI:
                        act.wait_ge(pt_done, B + i + 1)
                        if i >= 3:
                            act.wait_ge(av_done, B + i - 2 + 1)
                        nc.scalar.activation(pT[:, i % 3, :], ps_T[:, i % 2, :], ACT.Copy).then_inc(pt_copied, 1)
                    i = T - 2
                    if 0 <= i < NI and closes(i):
                        br = ITEMS[i][0]
                        s = bslot(u, br)
                        act.wait_ge(kept, B + i + 1)
                        nc.scalar.activation(keep[:, s, 1, :, :], keep[:, s, 1, :, :], ACT.Ln).then_inc(ln_done, 1)

            per_pairs(act, body)

        @block.tensor
        def _(pe):
            pe.wait_ge(consts, 32)
            pe.sem_inc(av_done, 1)

            def body(pp, u, p):
                B, BF = NI * p, FILLS * p
                pe.wait_ge(qk_loaded, 32 * p + 32)
                for f in range(FILLS):
                    if f >= FB:
                        pe.wait_ge(turn_lo, BF + f - FB + 1)
                    for n in range(4):
                        tr = nc.tensor.transpose(Z[:, f % FB, n * P:(n + 1) * P], qk_in[:, f // 4, 4 * (f % 4) + n, :],
                                                 ident[:, :])
                    tr.then_inc(turned, 1)
                pe.wait_ge(turn_lo, BF + FILLS)
                for T in range(-2, NI + 2):
                    i = T + 2
                    if i < NI:
                        br, x0, h = ITEMS[i]
                        dil = DILS[br]
                        if i >= 4:
                            pe.wait_ge(masked, B + i - 3)
                        r = slice(h * DH, (h + 1) * DH)
                        first_mm = True
                        nt, w = len(tiles(i)), blocks(i) * P
                        for n, (x, pos, head) in enumerate(tiles(i)):
                            kpos = pos - dil * P if (w == 2 * P and not head) else pos
                            own = slice(pos, pos + dil * (P - 1) + 1, dil)
                            ks = slice(kpos, kpos + dil * (w - 1) + 1, dil)
                            for c, (qt, kt) in enumerate(((T_hi, T_hi), (T_lo, T_hi), (T_hi, T_lo))):
                                mm = nc.tensor.matmul(Z[:, i % 4, n * w:(n + 1) * w], qt[r, 0, own], kt[r, 1, ks],
                                                      start=first_mm, stop=(c == 2), skip_group_check=True)
                                first_mm = False
                        mm.then_inc(z_done, 1)
                    i = T
                    if 0 <= i < NI:
                        pe.wait_ge(exp_done, B + i + 1)
                        if i >= 2:
                            pe.wait_ge(pt_copied, B + i - 1)
                        for n in range(4):
                            tr = nc.tensor.transpose(ps_T[:, i % 2, n * P:(n + 1) * P], sc[:, i % 4, n * P:(n + 1) * P],
                                                     ident[:, :])
                        tr.then_inc(pt_done, 1)
                    i = T - 2
                    if 0 <= i < NI:
                        br, x0, h = ITEMS[i]
                        s = bslot(u, br)
                        pe.wait_ge(pt_copied, B + i + 1)
                        if i >= 2:
                            pe.wait_ge(o_scaled, B + i - 1)
                        if x0 == 0 and h == 0:
                            pe.wait_ge(v_loaded[s], 16 * slot_dmas(pp, u, br))
                        first_mm = True
                        bl = blocks(i)
                        for n, (x, pos, head) in enumerate(tiles(i)):
                            kt = [x] if bl == 1 else ([x, x + 1] if head else [x - 1, x])
                            for b in range(bl):
                                mm = nc.tensor.matmul(O[:, i % 2, n * DH:(n + 1) * DH],
                                                      pT[:, i % 3, (n * bl + b) * P:(n * bl + b + 1) * P],
                                                      v_br[:, s, kt[b], h * DH:(h + 1) * DH],
                                                      start=first_mm, stop=(b == bl - 1), skip_group_check=True)
                                first_mm = False
                        mm.then_inc(av_done, 1)

            per_pairs(pe, body)


def spread_queries(copy, dst, src):
    for h in range(2):
        r = slice(h * DH, (h + 1) * DH)
        for pr in range(PAIRS):
            c = (2 * pr + h) * DEC_S
            last = copy(dst[r, :, c:c + DEC_S], src[r, pr, :].rearrange("p (b s) -> p b s", s=DEC_S))
    return last


def stick_breaking_sample(nc, t):
    C = PAIRS * 2 * DEC_S
    GP = 8
    NG = PAGES // GP
    RING = 4
    CH = 4
    PC = PAGES // CH
    ctx = ExitStack()
    with ctx:
        m = Mem(nc, ctx, "sbs")
        ident = m.sb("ident", [P, P])
        suffix = m.sb("suffix", [P, 2, P])
        table = m.sb("table", [1, DEC_B * PAGES], I32)
        bias = m.sb("bias", [P, H])
        biasC = m.sb("biasC", [P, C])
        valid = m.sb("valid", [NS, DEC_B, C])
        new_in = m.sb("new_in", [NS, 3, W])
        q_bd = m.sb("q_bd", [P, DEC_B, C])
        kT_new = m.sb("kT_new", [P, PAIRS, NS])
        z_new = m.sb("z_new", [NS, DEC_B, C])
        e_new = m.sb("e_new", [NS, DEC_B, C])
        a_new = m.sb("a_new", [NS, DEC_B, C])
        carry0 = m.sb("carry0", [P, DEC_B, C])
        k_ring = m.sb("k_ring", [P, RING, GP, W])
        v_ring = m.sb("v_ring", [P, RING, GP, W])
        kT = m.sb("kT", [P, 2, W])
        z = m.sb("z", [P, PAGES, C])
        el = m.sb("el", [P, PAGES * C])
        sp_ = m.sb("sp", [P, PAGES * C])
        tot = m.sb("tot", [P, C, PAGES])
        run = m.sb("run", [P, C, PAGES])
        a = m.sb("a", [P, PAGES, C])
        oT = m.sb("oT", [P, PAIRS, NS])
        o_rows = m.sb("o_rows", [NS, W])
        ps_T = m.ps("ps_T", [P, 2, 512])
        Zg = m.ps("Zg", [P, 2, 512])
        M = m.ps("M", [P, 3, 512])
        O = m.ps("O", [P, 512])

        consts = m.sem("consts")
        const_set = m.sem("const_set")
        biasC_set = m.sem("biasC_set")
        new_turned = m.sem("new_turned")
        new_spread = m.sem("new_spread")
        z_new_done = m.sem("z_new_done")
        new_step = m.sem("new_step")
        new_exp = m.sem("new_exp")
        new_sum = m.sem("new_sum")
        k_loaded = m.sems("k_loaded", RING)
        v_loaded = m.sems("v_loaded", RING)
        k_turned = m.sem("k_turned")
        kT_even = m.sem("kT_even")
        kT_odd = m.sem("kT_odd")
        qk_done = m.sem("qk_done")
        z_copied = m.sem("z_copied")
        v_used = m.sem("v_used")
        exp_done = m.sem("exp_done")
        cut_done = m.sem("cut_done")
        ln_done = m.sem("ln_done")
        sp_done = m.sem("sp_done")
        tot_done = m.sem("tot_done")
        tot_copied = m.sem("tot_copied")
        scanned = m.sem("scanned")
        suf_done = m.sem("suf_done")
        suf_added = m.sem("suf_added")
        carry_added = m.sem("carry_added")
        a_done = m.sem("a_done")
        o_copied = m.sem("o_copied")
        o_turned = m.sem("o_turned")
        o_rows_copied = m.sem("o_rows_copied")
        o_stored = m.sem("o_stored")

        def entries(eng, body):
            body(0)
            with eng.Fori(1, DEC_B) as b:
                body(b)

        def stream(eng, keys, values):
            keys_only, both, values_only = (lambda k: keys(k, None)), (lambda k, v: keys(k, v)), values
            keys_only(0)
            both(1, 0)
            with eng.Fori(2, DEC_B) as b:
                both(b, b - 1)
            values_only(DEC_B - 1)

        def is0(b):
            return isinstance(b, int) and b == 0

        block = ctx.enter_context(nc.Block())

        def load_pages(eng, pages, ring, loaded, used):
            cache = pages[0].rearrange("n s h d -> n s (h d)")

            def body(b):
                for g in range(NG):
                    if not (is0(b) and g < RING):
                        hold(eng, used, PAGES * b + GP * (g - RING + 1))
                    for i in range(GP):
                        r = GP * g + i
                        n = eng.value_load(table[0:1, bass.ds(PAGES * b + PAGES - 1 - r, 1)], min_val=0,
                                           max_val=pages.shape[1] - 1)
                        eng.dma_start(ring[:, g % RING, i, :], cache[bass.ds(n, 1), :, :].rearrange("a s c -> (a s) c")) \
                            .then_inc(loaded[g % RING], 16)
            return body

        @block.sync
        def _(sp):
            sp.dma_start(table[:, :], t["page_table"].rearrange("b n -> (b n)").rearrange("(a n) -> a n", a=1)) \
                .then_inc(consts, 16)
            sp.dma_start(ident[:, :], t["ident"][:, :]).then_inc(consts, 16)
            sp.dma_start(suffix[:, :, :], t["suffix"].rearrange("a p c -> p a c")).then_inc(consts, 16)
            sp.dma_start(bias[:, :], t["sb_bias"][0:1, :].to_broadcast([P, H])).then_inc(consts, 16)
            sp.dma_start(valid[:, :, :], t["valid_new"][:, :, :]).then_inc(consts, 16)
            for i, src in enumerate((t["q_sb_s"], flat(t["k_sb_s"]), flat(t["v_sb_s"]))):
                sp.dma_start(new_in[:, i, :], src).then_inc(consts, 16)
            sp.wait_ge(consts, 128)
            entries(sp, load_pages(sp, t["cache_k_sb"], k_ring, k_loaded, k_turned))
            sp.wait_ge(o_rows_copied, 1)
            sp.dma_start(t["o_sb_s"], o_rows[:, :]).then_inc(o_stored, 16)
            sp.wait_ge(o_stored, 16)

        @block.gpsimd
        def _(pool):
            nc.gpsimd.memset(q_bd[:, :, :], 0.0).then_inc(const_set, 1)
            nc.gpsimd.memset(run[:, :, :], 1.0).then_inc(const_set, 1)
            pool.wait_ge(const_set, 2)
            nc.gpsimd.memset(run[:, :, 0:1], 0.0).then_inc(const_set, 1)
            pool.wait_ge(consts, 128)
            entries(pool, load_pages(pool, t["cache_v_sb"], v_ring, v_loaded, v_used))

        @block.vector
        def _(dve):
            dve.wait_ge(consts, 128)
            nc.vector.tensor_copy(biasC[:, :].rearrange("p (h s) -> p h s", s=DEC_S),
                                  bias[:, :].unsqueeze(2).to_broadcast([P, H, DEC_S])).then_inc(biasC_set, 1)
            dve.wait_ge(const_set, 3)
            dve.wait_ge(new_turned, 1)
            spread_queries(nc.vector.tensor_copy, q_bd, ps_T[:, 0, 0:PAIRS * NS].rearrange("p (a n) -> p a n", n=NS))
            nc.vector.tensor_copy(kT_new[:, :, :], ps_T[:, 1, 0:PAIRS * NS].rearrange("p (a n) -> p a n", n=NS)) \
                .then_inc(new_spread, 1)
            dve.wait_ge(z_new_done, 1)
            dve.wait_ge(biasC_set, 1)
            for pr in range(PAIRS):
                cols = slice(pr * 2 * DEC_S, (pr + 1) * 2 * DEC_S)
                z_ev = nc.vector.tensor_tensor(z_new[:, :, cols],
                                               Zg[0:NS, 0, pr * 64:(pr + 1) * 64].rearrange("p (b c) -> p b c", b=DEC_B),
                                               biasC[0:NS, cols].unsqueeze(1).to_broadcast([NS, DEC_B, 2 * DEC_S]), ALU.add)
            z_ev.then_inc(new_step, 1)
            dve.wait_ge(new_exp, 1)
            nc.vector.tensor_scalar(e_new[:, :, :], e_new[:, :, :], BIG, None, ALU.min).then_inc(new_step, 1)
            dve.wait_ge(new_exp, 2)
            nc.vector.tensor_tensor(e_new[:, :, :], e_new[:, :, :], z_new[:, :, :], ALU.max).then_inc(new_step, 1)
            dve.wait_ge(new_step, 3)
            nc.vector.tensor_tensor(e_new[:, :, :], e_new[:, :, :], valid[:, :, :], ALU.mult).then_inc(new_step, 1)
            dve.wait_ge(new_sum, 1)
            flat_bc = "p b c -> p (b c)"
            nc.vector.tensor_tensor(z_new[:, :, :].rearrange(flat_bc), z_new[:, :, :].rearrange(flat_bc),
                                    M[0:NS, 0, 0:DEC_B * C], ALU.add).then_inc(new_step, 1)
            nc.vector.tensor_copy(carry0[:, :, :].rearrange(flat_bc), M[:, 1, 0:DEC_B * C]).then_inc(new_step, 1)
            dve.wait_ge(new_step, 6)
            nc.vector.tensor_scalar(z_new[:, :, :], z_new[:, :, :], 0.0, None, ALU.min).then_inc(new_step, 1)
            dve.wait_ge(new_exp, 3)
            nc.vector.tensor_tensor(a_new[:, :, :], e_new[:, :, :], valid[:, :, :], ALU.mult).then_inc(new_step, 1)

            def keys(b, _):
                def z_out(g):
                    dve.wait_ge(qk_done, PAGES * b + GP * (g + 1))
                    if g == 0 and not is0(b):
                        dve.wait_ge(a_done, CH * b)
                    nc.vector.tensor_tensor(z[:, g * GP:(g + 1) * GP, :],
                                            Zg[:, g % 2, 0:GP * C].rearrange("p (n c) -> p n c", c=C),
                                            biasC[:, :].unsqueeze(1).to_broadcast([P, GP, C]), ALU.add).then_inc(z_copied, 1)

                for r in range(1, PAGES, 2):
                    dve.wait_ge(k_turned, PAGES * b + r + 1)
                    if not (is0(b) and r < 2):
                        dve.wait_ge(qk_done, PAGES * b + r - 1)
                    nc.vector.tensor_copy(kT[:, 1, :], ps_T[:, 1, :]).then_inc(kT_odd, 1)
                    if r % GP == 1 and r > GP:
                        z_out(r // GP - 1)
                z_out(NG - 1)
                zf = z[:, :, :].rearrange("p n c -> p (n c)")
                for q in range(CH):
                    cols = slice(q * 512, (q + 1) * 512)
                    dve.wait_ge(exp_done, CH * b + q + 1)
                    nc.vector.tensor_scalar(el[:, cols], el[:, cols], BIG, None, ALU.min).then_inc(cut_done, 1)
                for q in range(CH):
                    cols = slice(q * 512, (q + 1) * 512)
                    dve.wait_ge(ln_done, CH * b + q + 1)
                    nc.vector.tensor_tensor(sp_[:, cols], zf[:, cols], el[:, cols], ALU.max).then_inc(sp_done, 1)
                    if q == 0:
                        nc.vector.tensor_copy(tot[:, :, 0:1], carry0[:, bass.ds(b, 1), :].rearrange("p a c -> p c a"))
                for q in range(CH):
                    n = PC if q < CH - 1 else PC - 1
                    dve.wait_ge(tot_done, CH * b + q + 1)
                    nc.vector.tensor_copy(tot[:, :, q * PC + 1:q * PC + 1 + n],
                                          M[:, q % 3, 0:n * C].rearrange("p (n c) -> p c n", c=C)).then_inc(tot_copied, 1)
                dve.wait_ge(tot_copied, CH * b + CH)
                nc.vector.tensor_tensor_scan(el[:, :], run[:, :, :].rearrange("p c n -> p (c n)"),
                                             tot[:, :, :].rearrange("p c n -> p (c n)"), 0.0, ALU.mult, ALU.add) \
                    .then_inc(scanned, 1)
                for q in range(CH):
                    cols = slice(q * 512, (q + 1) * 512)
                    dve.wait_ge(suf_done, CH * b + q + 1)
                    nc.vector.tensor_tensor(zf[:, cols], zf[:, cols], M[:, (CH + q) % 3, :], ALU.add).then_inc(suf_added, 1)
                dve.wait_ge(scanned, b + 1)
                for q in range(CH):
                    dve.wait_ge(suf_added, CH * b + q + 1)
                    part = z[:, q * PC:(q + 1) * PC, :]
                    carry = el[:, :].rearrange("p (c n) -> p n c", c=C)[:, q * PC:(q + 1) * PC, :]
                    nc.vector.tensor_tensor(part, part, carry, ALU.add).then_inc(carry_added, 1)

            stream(dve, keys, lambda b: None)

        @block.scalar
        def _(act):
            load_exp_ln_table(nc, act)
            act.wait_ge(new_step, 1)
            nc.scalar.activation(e_new[:, :, :], z_new[:, :, :], ACT.Exp).then_inc(new_exp, 1)
            act.wait_ge(new_step, 2)
            nc.scalar.activation(e_new[:, :, :], e_new[:, :, :], ACT.Ln, bias=1.0).then_inc(new_exp, 1)
            act.wait_ge(new_step, 7)
            nc.scalar.activation(e_new[:, :, :], z_new[:, :, :], ACT.Exp).then_inc(new_exp, 1)

            def values(b):
                act.wait_ge(v_used, PAGES * b + PAGES)
                for h in range(2):
                    r = slice(h * DH, (h + 1) * DH)
                    src = O[r, 0:C].rearrange("p (a x) -> p a x", a=PAIRS)[:, :, h * DEC_S:(h + 1) * DEC_S]
                    nc.scalar.activation(oT[r, :, bass.ds(b * DEC_S, DEC_S)], src, ACT.Copy).then_inc(o_copied, 1)

            def keys(b, bv):
                for r in range(0, PAGES, 2):
                    act.wait_ge(k_turned, PAGES * b + r + 1)
                    if not (is0(b) and r < 2):
                        act.wait_ge(qk_done, PAGES * b + r - 1)
                    nc.scalar.activation(kT[:, 0, :], ps_T[:, 0, :], ACT.Copy).then_inc(kT_even, 1)
                if bv is not None:
                    values(bv)
                zf = z[:, :, :].rearrange("p n c -> p (n c)")
                for q in range(CH):
                    cols = slice(q * 512, (q + 1) * 512)
                    act.wait_ge(z_copied, NG * b + 2 * q + 2)
                    if q == 0 and not is0(b):
                        act.wait_ge(carry_added, CH * b)
                    nc.scalar.activation(el[:, cols], zf[:, cols], ACT.Exp).then_inc(exp_done, 1)
                for q in range(CH):
                    cols = slice(q * 512, (q + 1) * 512)
                    act.wait_ge(cut_done, CH * b + q + 1)
                    nc.scalar.activation(el[:, cols], el[:, cols], ACT.Ln, bias=1.0).then_inc(ln_done, 1)
                for q in range(CH):
                    act.wait_ge(carry_added, CH * b + q + 1)
                    nc.scalar.activation(a[:, q * PC:(q + 1) * PC, :], z[:, q * PC:(q + 1) * PC, :], ACT.Exp) \
                        .then_inc(a_done, 1)

            stream(act, keys, values)
            act.wait_ge(o_turned, 1)
            nc.scalar.activation(o_rows[:, :], M[0:NS, 0, :], ACT.Copy).then_inc(o_rows_copied, 1)

        @block.tensor
        def _(pe):
            pe.wait_ge(consts, 128)
            for i in range(2):
                for pr in range(PAIRS):
                    tr = nc.tensor.transpose(ps_T[:, i, pr * NS:(pr + 1) * NS], new_in[:, i, pr * P:(pr + 1) * P],
                                             ident[0:NS, 0:NS])
            tr.then_inc(new_turned, 1)
            pe.wait_ge(new_spread, 1)
            for pr in range(PAIRS):
                mm = nc.tensor.matmul(Zg[0:NS, 0, pr * 64:(pr + 1) * 64], kT_new[:, pr, :],
                                      q_bd[:, :, pr * 2 * DEC_S:(pr + 1) * 2 * DEC_S], start=True, stop=True)
            mm.then_inc(z_new_done, 1)
            pe.wait_ge(new_step, 4)
            e_flat = e_new[:, :, :].rearrange("p b c -> p (b c)")
            nc.tensor.matmul(M[0:NS, 0, 0:DEC_B * C], suffix[0:NS, 0, 0:NS], e_flat, start=True, stop=True)
            nc.tensor.matmul(M[:, 1, 0:DEC_B * C], suffix[0:NS, 1, :], e_flat, start=True, stop=True).then_inc(new_sum, 1)
            pe.wait_ge(new_step, 8)

            def turn(b, r):
                g = r // GP
                if r % GP == 0:
                    pe.wait_ge(k_loaded[g % RING], 16 * GP * (2 * b + g // RING + 1))
                if not (is0(b) and r < 2):
                    pe.wait_ge(kT_odd if r % 2 else kT_even, (PAGES // 2) * b + r // 2)
                for pr in range(PAIRS):
                    tr = nc.tensor.transpose(ps_T[:, r % 2, pr * P:(pr + 1) * P], k_ring[:, g % RING, r % GP, pr * P:(pr + 1) * P],
                                             ident[:, :])
                tr.then_inc(k_turned, 1)

            def score(b, r):
                g = r // GP
                if r % GP == 0 and not (is0(b) and g < 2):
                    pe.wait_ge(z_copied, NG * b + g - 1)
                pe.wait_ge(kT_odd if r % 2 else kT_even, (PAGES // 2) * b + r // 2 + 1)
                for pr in range(PAIRS):
                    c = pr * 2 * DEC_S
                    mm = nc.tensor.matmul(Zg[:, g % 2, (r % GP) * C + c:(r % GP) * C + c + 2 * DEC_S],
                                          kT[:, r % 2, pr * P:(pr + 1) * P], q_bd[:, bass.ds(b, 1), c:c + 2 * DEC_S].rearrange("p a c -> p (a c)"),
                                          start=True, stop=True)
                mm.then_inc(qk_done, 1)

            def weigh(b, r):
                g = r // GP
                if r % GP == 0:
                    pe.wait_ge(v_loaded[g % RING], 16 * GP * (2 * b + g // RING + 1))
                if r == 0:
                    pe.wait_ge(a_done, CH * b + CH)
                    if not is0(b):
                        pe.wait_ge(o_copied, 2 * b)
                for pr in range(PAIRS):
                    c = pr * 2 * DEC_S
                    if r == 0:
                        nc.tensor.matmul(O[:, c:c + 2 * DEC_S], new_in[:, 2, pr * P:(pr + 1) * P],
                                         a_new[:, bass.ds(b, 1), c:c + 2 * DEC_S].rearrange("p a c -> p (a c)"), start=(pr == 0), stop=False,
                                         skip_group_check=True)
                for pr in range(PAIRS):
                    c = pr * 2 * DEC_S
                    mm = nc.tensor.matmul(O[:, c:c + 2 * DEC_S], v_ring[:, g % RING, r % GP, pr * P:(pr + 1) * P],
                                          a[:, r, c:c + 2 * DEC_S], start=False, stop=(r == PAGES - 1), skip_group_check=True)
                mm.then_inc(v_used, 1)

            def keys(b, bv):
                for r in range(PAGES + 1):
                    if r < PAGES:
                        turn(b, r)
                        if bv is not None:
                            weigh(bv, r)
                    if r >= 1:
                        score(b, r - 1)
                for q in range(CH):
                    pe.wait_ge(sp_done, CH * b + q + 1)
                    if q == 3:
                        pe.wait_ge(tot_copied, CH * b + 1)
                    if q < 3 and not is0(b):
                        pe.wait_ge(suf_added, CH * b)
                    nc.tensor.matmul(M[:, q % 3, :], suffix[:, 1, :], sp_[:, q * 512:(q + 1) * 512], start=True, stop=True) \
                        .then_inc(tot_done, 1)
                for q in range(CH):
                    pe.wait_ge(tot_copied, CH * b + min(q + 2, CH))
                    if q == 3:
                        pe.wait_ge(suf_added, CH * b + 1)
                    nc.tensor.matmul(M[:, (CH + q) % 3, :], suffix[:, 0, :], sp_[:, q * 512:(q + 1) * 512], start=True,
                                     stop=True).then_inc(suf_done, 1)

            def values(b):
                for r in range(PAGES):
                    weigh(b, r)

            stream(pe, keys, values)
            pe.wait_ge(o_copied, 2 * DEC_B)
            pe.wait_ge(suf_added, CH * DEC_B)
            for pr in range(PAIRS):
                tr = nc.tensor.transpose(M[0:NS, 0, pr * P:(pr + 1) * P], oT[:, pr, :], ident[:, :])
            tr.then_inc(o_turned, 1)


def dilated_sample(nc, t):
    C = H * DEC_S
    NA = 512 // P
    NT = NA + DEC_S
    KEYS = 2 * 512 + DEC_S
    ctx = ExitStack()
    with ctx:
        m = Mem(nc, ctx, "dls")
        ident = m.sb("ident", [P, P])
        mask = m.sb("mask", [C, KEYS])
        count = m.sb("count", [C, KEYS])
        own = m.sb("own", [C, W])
        pick = m.sb("pick", [C, DEC_S])
        qk_new = m.sb("qk_new", [NS, 2, W])
        q_pad = m.sb("q_pad", [P, 2, PAIRS * (C + 8)])
        qT = m.sb("qT", [P, PAIRS, NS])
        kT_new = m.sb("kT_new", [P, PAIRS, NS])
        k_in = m.sb("k_in", [P, 2, NT, W])
        v_in = m.sb("v_in", [P, 2, NT, W])
        v_new = m.sb("v_new", [DEC_S, 2, W])
        kT = m.sb("kT", [P, PAIRS, NT * P])
        s = m.sb("s", [C, 2, KEYS])
        stat = m.sb("stat", [C, 2, 4])
        pT = m.sb("pT", [P, 2, NT + 1, C])
        o_own = m.sb("o_own", [C, 2, W])
        o_row = m.sb("o_row", [DEC_S, 2, W])
        ps_T = m.ps("ps_T", [P, 2, 512])
        Sc = m.ps("Sc", [P, 3, 512])
        O = m.ps("O", [P, 2, 512])
        R = m.ps("R", [P, 512])

        consts = m.sem("consts")
        zeroed = m.sem("zeroed")
        q_turned = m.sem("q_turned")
        q_copied = m.sem("q_copied")
        k_loaded = m.sems("k_loaded", 2)
        v_loaded = m.sems("v_loaded", 2)
        padded = m.sem("padded")
        turned = m.sem("turned")
        copied = m.sems("copied", 2)
        scored = m.sem("scored")
        masked = m.sem("masked")
        max_done = m.sem("max_done")
        exp_done = m.sem("exp_done")
        counted = m.sem("counted")
        summed = m.sem("summed")
        inv_done = m.sem("inv_done")
        p_turned = m.sem("p_turned")
        p_copied = m.sem("p_copied")
        av_done = m.sem("av_done")
        o_masked = m.sem("o_masked")
        picked = m.sem("picked")
        row_copied = m.sem("row_copied")
        stored = m.sems("stored", 2)

        def entries(eng, scores, output):
            scores(0, 0, 0)
            scores(1, 1, 0)
            output(0, 0, 0)
            with eng.Fori(1, DEC_B // 2) as o:
                scores(2 * o, 0, o)
                output(2 * o - 1, 1, o - 1)
                scores(2 * o + 1, 1, o)
                output(2 * o, 0, o)
            output(DEC_B - 1, 1, DEC_B // 2 - 1)

        def early(b, n):
            return isinstance(b, int) and b < n

        k_c, v_c = (t[n][0].rearrange("b s h d -> b s (h d)") for n in ("cache_k_win", "cache_v_win"))
        k_new, v_new_d = (t[n][0].rearrange("b s h d -> b s (h d)")[:, WIN - DEC_S:WIN, :] for n in ("k_win_s", "v_win_s"))
        block = ctx.enter_context(nc.Block())

        @block.sync
        def _(sp):
            sp.dma_start(ident[:, :], t["ident"][:, :]).then_inc(consts, 16)
            for buf, n in ((mask, "win_mask"), (count, "win_count"), (own, "own_head"), (pick, "pick")):
                sp.dma_start(buf[:, :], t[n][:, :]).then_inc(consts, 16)
            sp.dma_start(qk_new[:, 0, :], t["q_dl_s"]).then_inc(consts, 16)
            sp.dma_start(qk_new[:, 1, :], k_new).then_inc(consts, 16)

            def rows(src, b):
                return src[bass.ds(b, 1), :, :].rearrange("a s c -> (a s) c")

            def load(b, slot, use):
                if not early(b, 2):
                    hold(sp, turned, NT * (b - 2) + NT)
                for buf, src, sem in ((k_in, k_c, k_loaded), (v_in, v_c, v_loaded)):
                    if buf is v_in and not early(b, 2):
                        hold(sp, av_done, b - 1)
                    sp.dma_start(buf[:, slot, 0:NA, :], rows(src, b)[WIN - 512:WIN, :].rearrange("(n p) c -> p n c", p=P)) \
                        .then_inc(sem[slot], 16)
                    sp.dma_start(buf[:, slot, NA:NT, :], rows(src, b).rearrange("(p r) c -> p r c", r=16)[:, 0:DEC_S, :]) \
                        .then_inc(sem[slot], 16)
                sp.dma_start(v_new[:, slot, :], rows(v_new_d, b)).then_inc(v_loaded[slot], 16)

            def store(b, slot, use):
                hold(sp, row_copied, b + 1)
                sp.dma_start(t["o_dl_s"][bass.ds(b * DEC_S, DEC_S), :], o_row[:, slot, :]).then_inc(stored[slot], 16)

            entries(sp, load, store)
            for slot in range(2):
                sp.wait_ge(stored[slot], 16 * (DEC_B // 2))

        @block.vector
        def _(dve):
            nc.vector.memset(q_pad[:, :, :], 0.0).then_inc(zeroed, 1)
            dve.wait_ge(consts, 16 * 7)
            dve.wait_ge(q_turned, 1)
            nc.vector.tensor_copy(qT[:, :, :], ps_T[:, 0, 0:PAIRS * NS].rearrange("p (a n) -> p a n", n=NS)).then_inc(q_copied, 1)
            nc.vector.tensor_copy(kT_new[:, :, :], ps_T[:, 1, 0:PAIRS * NS].rearrange("p (a n) -> p a n", n=NS)) \
                .then_inc(q_copied, 1)
            dve.wait_ge(zeroed, 1)
            dve.wait_ge(q_copied, 2)

            def scores(b, slot, use):
                if not early(b, 2):
                    dve.wait_ge(scored, b - 1)
                for h in range(2):
                    r = slice(h * DH, (h + 1) * DH)
                    dst = q_pad[r, slot, :].rearrange("p (a x) -> p a x", a=PAIRS)[:, :, h * DEC_S:(h + 1) * DEC_S]
                    pd = nc.vector.tensor_copy(dst, qT[r, :, bass.ds(b * DEC_S, DEC_S)])
                pd.then_inc(padded, 1)
                for x in range(1, NT, 2):
                    dve.wait_ge(turned, NT * b + x + 1)
                    if not early(b, 1):
                        dve.wait_ge(scored, b)
                    nc.vector.tensor_copy(kT[:, :, x * P:(x + 1) * P], ps_T[:, 1, :].rearrange("p (a n) -> p a n", a=PAIRS)) \
                        .then_inc(copied[1], 1)
                dve.wait_ge(scored, b + 1)
                if not early(b, 2):
                    dve.wait_ge(p_turned, b - 1)
                for x in range(2):
                    cols = slice(x * 512, (x + 1) * 512)
                    nc.vector.tensor_tensor(s[:, slot, cols], Sc[0:C, x, :], mask[:, cols], ALU.add)
                nc.vector.tensor_tensor(s[:, slot, 1024:KEYS], Sc[0:C, 2, 0:DEC_S], mask[:, 1024:KEYS], ALU.add).then_inc(masked, 1)
                dve.wait_ge(masked, b + 1)
                nc.vector.tensor_reduce(stat[:, slot, 0:1], s[:, slot, :], AX.X, ALU.max, negate=True).then_inc(max_done, 1)
                dve.wait_ge(exp_done, b + 1)
                nc.vector.tensor_tensor(s[:, slot, :], s[:, slot, :], count[:, :], ALU.mult).then_inc(counted, 1)
                dve.wait_ge(counted, b + 1)
                nc.vector.tensor_reduce(stat[:, slot, 1:2], s[:, slot, :], AX.X, ALU.add).then_inc(summed, 1)
                dve.wait_ge(summed, b + 1)
                nc.vector.reciprocal(stat[:, slot, 2:3], stat[:, slot, 1:2]).then_inc(inv_done, 1)

            def output(b, slot, use):
                dve.wait_ge(av_done, b + 1)
                dve.wait_ge(inv_done, b + 1)
                if not early(b, 2):
                    dve.wait_ge(picked, b - 1)
                nc.vector.scalar_tensor_tensor(out=o_own[:, slot, :], in0=O[0:C, slot, :], scalar=stat[:, slot, 2:3],
                                               in1=own[:, :], op0=ALU.mult, op1=ALU.mult).then_inc(o_masked, 1)

            entries(dve, scores, output)

        @block.scalar
        def _(act):
            load_exp_ln_table(nc, act)

            def scores(b, slot, use):
                for x in range(0, NT, 2):
                    act.wait_ge(turned, NT * b + x + 1)
                    if not early(b, 1):
                        act.wait_ge(scored, b)
                    nc.scalar.activation(kT[:, :, x * P:(x + 1) * P], ps_T[:, 0, :].rearrange("p (a n) -> p a n", a=PAIRS),
                                         ACT.Copy).then_inc(copied[0], 1)
                act.wait_ge(max_done, b + 1)
                nc.scalar.activation(s[:, slot, :], s[:, slot, :], ACT.Exp, bias=stat[:, slot, 0:1]).then_inc(exp_done, 1)

            def output(b, slot, use):
                act.wait_ge(p_turned, b + 1)
                nc.scalar.activation(pT[:, slot, 0:NT, :], ps_T[:, 0, 0:NT * C].rearrange("p (n c) -> p n c", c=C), ACT.Copy)
                nc.scalar.activation(pT[0:DEC_S, slot, NT, :], ps_T[0:DEC_S, 1, 0:C], ACT.Copy).then_inc(p_copied, 1)
                act.wait_ge(picked, b + 1)
                if not early(b, 2):
                    act.wait_ge(stored[slot], 16 * use)
                nc.scalar.activation(o_row[:, slot, :], R[0:DEC_S, :], ACT.Copy).then_inc(row_copied, 1)

            entries(act, scores, output)

        @block.tensor
        def _(pe):
            pe.wait_ge(consts, 16 * 7)
            for i in range(2):
                for pr in range(PAIRS):
                    tr = nc.tensor.transpose(ps_T[:, i, pr * NS:(pr + 1) * NS], qk_new[:, i, pr * P:(pr + 1) * P],
                                             ident[0:NS, 0:NS])
            tr.then_inc(q_turned, 1)
            pe.wait_ge(q_copied, 2)

            def scores(b, slot, use):
                pe.wait_ge(k_loaded[slot], 32 * use + 32)
                if not early(b, 2):
                    pe.wait_ge(p_copied, b - 1)
                for x in range(NT):
                    if not (early(b, 1) and x < 2):
                        pe.wait_ge(copied[x % 2], (NT // 2) * b + x // 2)
                    for pr in range(PAIRS):
                        tr = nc.tensor.transpose(ps_T[:, x % 2, pr * P:(pr + 1) * P], k_in[:, slot, x, pr * P:(pr + 1) * P],
                                                 ident[:, :])
                    tr.then_inc(turned, 1)
                for x in range(2):
                    pe.wait_ge(copied[x], (NT // 2) * b + NT // 2)
                pe.wait_ge(padded, b + 1)
                if not early(b, 1):
                    pe.wait_ge(masked, b)
                for x in range(2):
                    for pr in range(PAIRS):
                        nc.tensor.matmul(Sc[0:C, x, :], q_pad[:, slot, pr * C:(pr + 1) * C], kT[:, pr, x * 512:(x + 1) * 512],
                                         start=(pr == 0), stop=(pr == PAIRS - 1))
                for pr in range(PAIRS):
                    mm = nc.tensor.matmul(Sc[0:C, 2, 0:DEC_S], q_pad[:, slot, pr * C:(pr + 1) * C],
                                          kT_new[:, pr, bass.ds(b * DEC_S, DEC_S)], start=(pr == 0), stop=(pr == PAIRS - 1))
                mm.then_inc(scored, 1)

            def output(b, slot, use):
                hold(pe, summed, b + 1)
                for x in range(NT):
                    nc.tensor.transpose(ps_T[:, 0, x * C:(x + 1) * C], s[:, slot, x * P:(x + 1) * P], ident[0:C, 0:C])
                nc.tensor.transpose(ps_T[0:DEC_S, 1, 0:C], s[:, slot, 1024:KEYS], ident[0:C, 0:C]).then_inc(p_turned, 1)
                hold(pe, v_loaded[slot], 48 * use + 48)
                hold(pe, p_copied, b + 1)
                if not early(b, 2):
                    hold(pe, o_masked, b - 1)
                nc.tensor.matmul(O[0:C, slot, :], pT[0:DEC_S, slot, NT, :], v_new[:, slot, :], start=True, stop=False)
                for x in range(NT):
                    mm = nc.tensor.matmul(O[0:C, slot, :], pT[:, slot, x, :], v_in[:, slot, x, :], start=False,
                                          stop=(x == NT - 1))
                mm.then_inc(av_done, 1)
                hold(pe, o_masked, b + 1)
                if not early(b, 1):
                    hold(pe, row_copied, b)
                nc.tensor.matmul(R[0:DEC_S, :], pick[:, :], o_own[:, slot, :], start=True, stop=True).then_inc(picked, 1)

            entries(pe, scores, output)


def merge(nc, t):
    PC = PLE // P
    ctx = ExitStack()
    with ctx:
        m = Mem(nc, ctx, "merge")
        wo_hi, wo_lo = (m.sb(f"wo_{x}", [P, KC, D], F32R) for x in ("hi", "lo"))
        wg_hi, wg_lo = (m.sb(f"wg_{x}", [P, KC, D], F32R) for x in ("hi", "lo"))
        wp_hi, wp_lo = (m.sb(f"wp_{x}", [P, PC, D], F32R) for x in ("hi", "lo"))
        yT_hi, yT_lo = (m.sb(f"yT_{x}", [P, KC, P], F32R) for x in ("hi", "lo"))
        xT_hi, xT_lo = (m.sb(f"xT_{x}", [P, KC, P], F32R) for x in ("hi", "lo"))
        pT_hi, pT_lo = (m.sb(f"pT_{x}", [P, PC, P], F32R) for x in ("hi", "lo"))
        x = m.sb("x", [P, 2, D])
        work = m.sb("work", [P, 2, D])
        z = m.sb("z", [P, D])
        o = m.sb("o", [P, 4, W])
        lse = m.sb("lse", [P, 3, H])
        top = m.sb("top", [P, H])
        share = m.sb("share", [P, 3, H])
        total = m.sb("total", [P, H])
        p_in = m.sb("p_in", [P, PLE])
        junk = m.sb("junk", [P, W])
        stat = m.sb("stat", [P, 3, 2])
        mhalf = m.sb("mhalf", [P, 2])
        g_out = m.sb("g_out", [P, KC])
        ident = m.sb("ident", [P, P])
        T = m.ps("T", [P, 2, 512])
        Out = m.ps("Out", [P, 2, 512])
        Gate = m.ps("Gate", [P, 2, 512])
        Ple = m.ps("Ple", [P, 2, 512])

        consts = m.sem("consts")
        mhalf_set = m.sem("mhalf_set")
        w_loaded = m.sems("w_loaded", 2)
        w_hi_done = m.sem("w_hi_done")
        w_split = m.sem("w_split")
        in_loaded = m.sem("in_loaded")
        x_loaded = m.sems("x_loaded", 2)
        p_loaded = m.sem("p_loaded")
        share_step = m.sem("share_step")
        share_exp = m.sem("share_exp")
        z_exp = m.sem("z_exp")
        silu_step = m.sem("silu_step")
        squared = m.sem("squared")
        mean_done = m.sem("mean_done")
        rms_done = m.sem("rms_done")
        y_done = m.sem("y_done")
        y_turned, y_hi, y_split = m.sem("y_turned"), m.sem("y_hi"), m.sem("y_split")
        x1_turned, x1_hi, x1_split = m.sem("x1_turned"), m.sem("x1_hi"), m.sem("x1_split")
        p_turned, p_hi, p_split = m.sem("p_turned"), m.sem("p_hi"), m.sem("p_split")
        out_done = m.sem("out_done")
        x1_done = m.sem("x1_done")
        gate_done = m.sem("gate_done")
        gate_exp = m.sem("gate_exp")
        ple_done = m.sem("ple_done")
        final_step = m.sem("final_step")
        stored = m.sem("stored")

        SH, FS = 10, 4

        def rows_of(item):
            return NS if first(item) else P

        def before(item, slot, use):
            return item - 1, 1 - slot, use - (1 - slot)

        def pipeline(eng, enter, body, leave):
            enter()
            steps(eng, body)
            leave()

        sets = [(t["w_out"][0], wo_hi, wo_lo, k) for k in range(KC)] \
            + [(t["w_ple"][0], wp_hi, wp_lo, k) for k in range(PC)] \
            + [(t["w_ple_gate"][0], wg_hi, wg_lo, k) for k in range(KC)]
        NW = len(sets)
        x_s, p_s = t["x_sample"].rearrange("b s d -> (b s) d"), t["p_sample"][0].rearrange("b s d -> (b s) d")
        y_s = t["y_sample"].rearrange("b s d -> (b s) d")
        block = ctx.enter_context(nc.Block())

        @block.sync
        def _(sp):
            sp.dma_start(ident[:, :], t["ident"][:, :]).then_inc(consts, 16)
            with nc.allow_non_contiguous_dma(reason="the 1024 weights of the norms, once"):
                for i, n in enumerate(("out_norm_sb", "out_norm_dil")):
                    sp.dma_start(g_out[:, 4 * i:4 * i + 4], t[n][0].rearrange("(c p) -> p c", p=P)).then_inc(consts, 16)

            def load_in(item):
                n = rows_of(item)
                rows = slice(0, NS) if first(item) else bass.ts(item - 1, P)
                if first(item):
                    srcs = [t["o_sb_s"]] + [t["o_dl_s"]] * 3
                    zs, ls = [t["z_sb_s"], t["z_dl_s"]], t["lse_one"].rearrange("n (b h) -> n b h", h=H)
                else:
                    srcs = [t["o_sb"][rows, :]] + [t["o_dil"][br][rows, :] for br in range(3)]
                    zs = [t["z_sb"][rows, :], t["z_dl"][rows, :]]
                    ls = t["lse_dil"][:, rows, :].rearrange("b n h -> n b h")
                sp.dma_start(lse[0:n], ls).then_inc(in_loaded, 16)
                for i, src in enumerate(zs):
                    sp.dma_start(z[0:n, i * W:(i + 1) * W], src).then_inc(in_loaded, 16)
                for i, src in enumerate(srcs):
                    sp.dma_start(o[0:n, i, :], src).then_inc(in_loaded, 16)

            def load_x(item, slot):
                n = rows_of(item)
                sp.dma_start(x[0:n, slot, :], x_s if first(item) else t["x_prompt"][0][bass.ts(item - 1, P), :]) \
                    .then_inc(x_loaded[slot], 16)

            def load_p(item):
                n = rows_of(item)
                sp.dma_start(p_in[0:n, :], p_s if first(item) else t["p_prompt"][0, 0][bass.ts(item - 1, P), :]) \
                    .then_inc(p_loaded, 16)

            def store(item):
                n = rows_of(item)
                hold(sp, final_step, FS * item + FS)
                dst = y_s if first(item) else t["y_prompt"][0][bass.ts(item - 1, P), :]
                sp.dma_start(dst, work[0:n, 1, :]).then_inc(stored, 16)

            def enter():
                for c, (src, hi, lo, k) in enumerate(sets):
                    if c >= 2:
                        sp.wait_ge(w_split, c - 1)
                    sp.dma_start(work[:, c % 2, :], src[k * P:(k + 1) * P, :]).then_inc(w_loaded[c % 2], 16)
                    if c == 1:
                        load_in(0)
                        load_x(0, 0)
                        load_p(0)
                hold(sp, y_done, 2)
                load_in(1)

            def body(item, slot, use):
                if not last(item):
                    if not (isinstance(item, int) and item == 0):
                        hold(sp, final_step, FS * item)
                    load_x(item + 1, 1 - slot)
                if not (isinstance(item, int) and item >= TILES - 1):
                    hold(sp, y_done, 2 * item + 4)
                    load_in(item + 2)
                if not first(item):
                    hold(sp, p_turned, item)
                    load_p(item)
                    store(item - 1)

            pipeline(sp, enter, body, lambda: store(TILES))
            sp.wait_ge(stored, 16 * (TILES + 1))

        @block.gpsimd
        def _(pool):
            nc.gpsimd.memset(mhalf[:, :], -0.5).then_inc(mhalf_set, 1)
            hold(pool, mhalf_set, 1)

            def rms(item):
                n = rows_of(item)
                hold(pool, squared, 2 * item + 2)
                if not first(item):
                    hold(pool, y_done, 2 * item)
                nc.gpsimd.tensor_scalar(stat[0:n, 1, :], stat[0:n, 0, :], 1.0 / W, EPS, ALU.mult, ALU.add) \
                    .then_inc(mean_done, 1)
                hold(pool, mean_done, item + 1)
                nc.gpsimd.tensor_tensor(stat[0:n, 2, :], stat[0:n, 1, :], mhalf[0:n, :], ALU.pow).then_inc(rms_done, 1)

            def body(item, slot, use):
                if not last(item):
                    rms(item + 1)

            rms(0)
            steps(pool, body)

        @block.vector
        def _(dve):
            def enter():
                for c, (src, hi, lo, k) in enumerate(sets):
                    dve.wait_ge(w_hi_done, c + 1)
                    if c < KC:
                        nc.vector.scalar_tensor_tensor(out=lo[:, k, :], in0=work[:, c % 2, :], scalar=g_out[:, k:k + 1],
                                                       in1=hi[:, k, :].bitcast(F32), op0=ALU.mult, op1=ALU.subtract) \
                            .then_inc(w_split, 1)
                    else:
                        nc.vector.tensor_tensor(lo[:, k, :], work[:, c % 2, :], hi[:, k, :].bitcast(F32), ALU.subtract) \
                            .then_inc(w_split, 1)
                prepare(0)
                low(0, "y")

            def prepare(item):
                n = rows_of(item)
                s = SH * item
                dve.wait_ge(in_loaded, 16 * 7 * item + 16 * 7)
                nc.vector.tensor_tensor(top[0:n], lse[0:n, 0], lse[0:n, 1], ALU.max).then_inc(share_step, 1)
                dve.wait_ge(share_step, s + 1)
                nc.vector.tensor_tensor(top[0:n], top[0:n], lse[0:n, 2], ALU.max).then_inc(share_step, 1)
                dve.wait_ge(share_step, s + 2)
                nc.vector.tensor_tensor(share[0:n], lse[0:n], top[0:n].unsqueeze(1).to_broadcast([n, 3, H]), ALU.subtract) \
                    .then_inc(share_step, 1)
                dve.wait_ge(z_exp, item + 1)
                nc.vector.tensor_scalar(work[0:n, 0, :], work[0:n, 0, :], 1.0, None, ALU.add).then_inc(silu_step, 1)
                dve.wait_ge(share_exp, item + 1)
                nc.vector.tensor_tensor(total[0:n], share[0:n, 0], share[0:n, 1], ALU.add).then_inc(share_step, 1)
                dve.wait_ge(share_step, s + 4)
                nc.vector.tensor_tensor(total[0:n], total[0:n], share[0:n, 2], ALU.add).then_inc(share_step, 1)
                dve.wait_ge(share_step, s + 5)
                nc.vector.reciprocal(total[0:n], total[0:n]).then_inc(share_step, 1)
                dve.wait_ge(share_step, s + 6)
                nc.vector.tensor_tensor(share[0:n], share[0:n], total[0:n].unsqueeze(1).to_broadcast([n, 3, H]), ALU.mult) \
                    .then_inc(share_step, 1)
                dve.wait_ge(share_step, s + 7)
                nc.vector.tensor_tensor(o[0:n, 1:4, :].rearrange("p b (h d) -> p (b h) d", d=DH),
                                        o[0:n, 1:4, :].rearrange("p b (h d) -> p (b h) d", d=DH),
                                        share[0:n].rearrange("p b h -> p (b h)").unsqueeze(2).to_broadcast([n, 3 * H, DH]),
                                        ALU.mult).then_inc(share_step, 1)
                dve.wait_ge(share_step, s + 8)
                nc.vector.tensor_tensor(o[0:n, 1, :], o[0:n, 1, :], o[0:n, 2, :], ALU.add).then_inc(share_step, 1)
                dve.wait_ge(share_step, s + 9)
                nc.vector.tensor_tensor(o[0:n, 1, :], o[0:n, 1, :], o[0:n, 3, :], ALU.add).then_inc(share_step, 1)
                dve.wait_ge(silu_step, 3 * item + 1)
                nc.vector.reciprocal(work[0:n, 0, :], work[0:n, 0, :]).then_inc(silu_step, 1)
                dve.wait_ge(silu_step, 3 * item + 2)
                nc.vector.tensor_tensor(work[0:n, 0, :], work[0:n, 0, :], z[0:n, :], ALU.mult).then_inc(silu_step, 1)
                dve.wait_ge(rms_done, item + 1)
                dve.wait_ge(silu_step, 3 * item + 3)
                for i in range(2):
                    cols = slice(i * W, (i + 1) * W)
                    nc.vector.scalar_tensor_tensor(out=work[0:n, 0, cols], in0=o[0:n, i, :], scalar=stat[0:n, 2, i:i + 1],
                                                   in1=work[0:n, 0, cols], op0=ALU.mult, op1=ALU.mult).then_inc(y_done, 1)

            def low(item, what):
                n = rows_of(item)
                hi, lo, hi_done, split = {"y": (yT_hi, yT_lo, y_hi, y_split), "x1": (xT_hi, xT_lo, x1_hi, x1_split)}[what]
                for b in range(2):
                    dve.wait_ge(hi_done, 2 * item + b + 1)
                    src = T[:, b, :].rearrange("p (c r) -> p c r", r=P)[:, :, 0:n]
                    nc.vector.tensor_tensor(lo[:, 4 * b:4 * b + 4, 0:n], src, hi[:, 4 * b:4 * b + 4, 0:n].bitcast(F32),
                                            ALU.subtract).then_inc(split, 1)

            def low_p(item):
                n = rows_of(item)
                dve.wait_ge(p_hi, item + 1)
                src = T[:, 0, 0:PC * P].rearrange("p (c r) -> p c r", r=P)[:, :, 0:n]
                nc.vector.tensor_tensor(pT_lo[:, :, 0:n], src, pT_hi[:, :, 0:n].bitcast(F32), ALU.subtract).then_inc(p_split, 1)

            def residual(item, slot, use):
                n = rows_of(item)
                dve.wait_ge(x_loaded[slot], 16 * use + 16)
                for g in range(2):
                    dve.wait_ge(out_done, 2 * item + g + 1)
                    cols = slice(g * 512, (g + 1) * 512)
                    nc.vector.tensor_tensor(x[0:n, slot, cols], x[0:n, slot, cols], Out[0:n, g, :], ALU.add) \
                        .then_inc(x1_done, 1)

            def final(item, slot, use):
                n = rows_of(item)
                f = FS * item
                out = work[0:n, 1, :]
                dve.wait_ge(gate_exp, 2 * item + 2)
                nc.vector.tensor_scalar(out, out, 1.0, None, ALU.add).then_inc(final_step, 1)
                dve.wait_ge(final_step, f + 1)
                nc.vector.reciprocal(out, out).then_inc(final_step, 1)
                dve.wait_ge(ple_done, item + 1)
                dve.wait_ge(final_step, f + 2)
                nc.vector.tensor_tensor(out, out, Ple[0:n, :, :].rearrange("p a c -> p (a c)"), ALU.mult).then_inc(final_step, 1)
                dve.wait_ge(final_step, f + 3)
                nc.vector.tensor_tensor(out, out, x[0:n, slot, :], ALU.add).then_inc(final_step, 1)

            def body(item, slot, use):
                if not first(item):
                    low(item - 1, "x1")
                if not last(item):
                    prepare(item + 1)
                if not first(item):
                    low_p(item - 1)
                residual(item, slot, use)
                if not last(item):
                    low(item + 1, "y")
                if not first(item):
                    final(*before(item, slot, use))

            def leave():
                low(TILES, "x1")
                low_p(TILES)
                final(TILES, 0, TILES // 2)

            pipeline(dve, enter, body, leave)

        @block.scalar
        def _(act):
            load_exp_ln_table(nc, act)

            def enter():
                act.wait_ge(consts, 48)
                for c, (src, hi, lo, k) in enumerate(sets):
                    act.wait_ge(w_loaded[c % 2], 16 * (c // 2 + 1))
                    nc.scalar.activation(hi[:, k, :], work[:, c % 2, :], ACT.Copy,
                                         scale=g_out[:, k:k + 1] if c < KC else 1.0).then_inc(w_hi_done, 1)
                act.wait_ge(w_split, NW)
                prepare(0)
                high(0, "y")

            def prepare(item):
                n = rows_of(item)
                act.wait_ge(in_loaded, 16 * 7 * item + 16 * 7)
                if not first(item):
                    act.wait_ge(y_turned, 2 * item)
                    act.wait_ge(squared, 2 * item)
                    act.wait_ge(mean_done, item)
                nc.scalar.activation(work[0:n, 0, :], z[0:n, :], ACT.Exp, scale=-1.0).then_inc(z_exp, 1)
                nc.scalar.activation(junk[0:n, :], o[0:n, 0, :], ACT.Square, accum_out=stat[0:n, 0, 0:1]).then_inc(squared, 1)
                act.wait_ge(share_step, SH * item + 3)
                nc.scalar.activation(share[0:n], share[0:n], ACT.Exp).then_inc(share_exp, 1)
                act.wait_ge(share_step, SH * item + 10)
                act.wait_ge(squared, 2 * item + 1)
                nc.scalar.activation(junk[0:n, :], o[0:n, 1, :], ACT.Square, accum_out=stat[0:n, 0, 1:2]).then_inc(squared, 1)

            def high(item, what):
                n = rows_of(item)
                hi, hi_done, turned = {"y": (yT_hi, y_hi, y_turned), "x1": (xT_hi, x1_hi, x1_turned)}[what]
                for b in range(2):
                    act.wait_ge(turned, 2 * item + b + 1)
                    src = T[:, b, :].rearrange("p (c r) -> p c r", r=P)[:, :, 0:n]
                    nc.scalar.activation(hi[:, 4 * b:4 * b + 4, 0:n], src, ACT.Copy).then_inc(hi_done, 1)

            def high_p(item):
                n = rows_of(item)
                act.wait_ge(p_turned, item + 1)
                src = T[:, 0, 0:PC * P].rearrange("p (c r) -> p c r", r=P)[:, :, 0:n]
                nc.scalar.activation(pT_hi[:, :, 0:n], src, ACT.Copy).then_inc(p_hi, 1)

            def gate(item):
                n = rows_of(item)
                if first(item):
                    act.wait_ge(w_split, NW)
                else:
                    act.wait_ge(stored, 16 * item)
                for g in range(2):
                    act.wait_ge(gate_done, 2 * item + g + 1)
                    nc.scalar.activation(work[0:n, 1, g * 512:(g + 1) * 512], Gate[0:n, g, :], ACT.Exp, scale=-1.0) \
                        .then_inc(gate_exp, 1)

            def body(item, slot, use):
                if not first(item):
                    high(item - 1, "x1")
                if not last(item):
                    prepare(item + 1)
                if not first(item):
                    high_p(item - 1)
                if not last(item):
                    high(item + 1, "y")
                if not first(item):
                    gate(item - 1)

            def leave():
                high(TILES, "x1")
                high_p(TILES)
                gate(TILES)

            pipeline(act, enter, body, leave)

        @block.tensor
        def _(pe):
            def split_product(dst, n, xh, xl, wh, wl, chunks, g):
                cols = slice(g * 512, (g + 1) * 512)
                for k in range(chunks):
                    nc.tensor.matmul(dst[0:n, g, :], xh[:, k, 0:n], wh[:, k, cols], start=(k == 0), stop=False)
                    nc.tensor.matmul(dst[0:n, g, :], xh[:, k, 0:n], wl[:, k, cols], start=False, stop=False)
                    mm = nc.tensor.matmul(dst[0:n, g, :], xl[:, k, 0:n], wh[:, k, cols], start=False, stop=(k == chunks - 1))
                return mm

            def turn(src, n, b, chunks, turned):
                for c in range(chunks):
                    k = 4 * b + c
                    tr = nc.tensor.transpose(T[:, b, c * P:c * P + n], src[:, k * P:(k + 1) * P], ident[0:n, 0:n])
                tr.then_inc(turned, 1)

            def turn_y(item):
                n = rows_of(item)
                for b in range(2):
                    pe.wait_ge(y_done, 2 * item + b + 1)
                    if not first(item):
                        if isinstance(item, int) and item == 1:
                            pe.wait_ge(y_split, b + 1)
                        elif b == 0:
                            pe.wait_ge(p_split, item - 1)
                        else:
                            pe.wait_ge(x1_split, 2 * item - 2)
                    turn(work[0:n, 0, :], n, b, 4, y_turned)

            def turn_x1(item, slot, use):
                n = rows_of(item)
                pe.wait_ge(x1_done, 2 * item + 2)
                for b in range(2):
                    if not last(item):
                        pe.wait_ge(y_split, 2 * item + 3 + b)
                    elif b == 0:
                        pe.wait_ge(p_split, item)
                    else:
                        pe.wait_ge(x1_split, 2 * item)
                    turn(x[0:n, slot, :], n, b, 4, x1_turned)

            def turn_p(item):
                n = rows_of(item)
                pe.wait_ge(p_loaded, 16 * item + 16)
                pe.wait_ge(x1_split, 2 * item + 1)
                turn(p_in[0:n, :], n, 0, PC, p_turned)

            def project_out(item, g):
                n = rows_of(item)
                if g == 0:
                    pe.wait_ge(y_split, 2 * item + 2)
                if not first(item):
                    pe.wait_ge(x1_done, 2 * item - 1 + g)
                split_product(Out, n, yT_hi, yT_lo, wo_hi, wo_lo, KC, g).then_inc(out_done, 1)

            def gate_ple(item):
                n = rows_of(item)
                pe.wait_ge(x1_split, 2 * item + 2)
                for g in range(2):
                    if not first(item):
                        pe.wait_ge(gate_exp, 2 * item - 1 + g)
                    split_product(Gate, n, xT_hi, xT_lo, wg_hi, wg_lo, KC, g).then_inc(gate_done, 1)
                pe.wait_ge(p_split, item + 1)
                if not first(item):
                    pe.wait_ge(final_step, FS * item - 1)
                for g in range(2):
                    mm = split_product(Ple, n, pT_hi, pT_lo, wp_hi, wp_lo, PC, g)
                mm.then_inc(ple_done, 1)

            def enter():
                pe.wait_ge(consts, 48)
                turn_y(0)

            def body(item, slot, use):
                if not first(item):
                    turn_x1(*before(item, slot, use))
                project_out(item, 0)
                if not first(item):
                    turn_p(item - 1)
                project_out(item, 1)
                if not last(item):
                    turn_y(item + 1)
                if not first(item):
                    gate_ple(item - 1)

            def leave():
                turn_x1(TILES, 0, TILES // 2)
                turn_p(TILES)
                gate_ple(TILES)

            pipeline(pe, enter, body, leave)


def build(nc, t):
    for name, shape in (("q_sb", [SEQ, W]), ("z_sb", [SEQ, W]), ("q_dl", [SEQ, W]), ("z_dl", [SEQ, W]),
                        ("q_sb_s", [NS, W]), ("z_sb_s", [NS, W]), ("q_dl_s", [NS, W]), ("z_dl_s", [NS, W]),
                        ("o_sb", [SEQ, W]), ("o_dil", [3, SEQ, W]), ("lse_dil", [3, SEQ, H]),
                        ("o_sb_s", [NS, W]), ("o_dl_s", [NS, W])):
        t[name] = nc.dram_tensor(f"scratch_{name}", shape, F32).ap()
    with nc.semaphore("tick") as tick:
        TICK[0] = tick
        project(nc, t, 0)
        project(nc, t, 1)
        stick_breaking_prompt(nc, t)
        dilated_prompt(nc, t)
        stick_breaking_sample(nc, t)
        dilated_sample(nc, t)
        merge(nc, t)


INPUTS = ["x_prompt", "x_sample", "cache_k_sb", "cache_v_sb", "cache_k_win", "cache_v_win", "page_table",
          "p_prompt", "p_sample", "attn_norm", "w_in", "sb_bias", "q_norm_dil", "k_norm_dil", "out_norm_sb",
          "out_norm_dil", "w_out", "w_ple", "w_ple_gate"]
OUTPUTS = [("y_prompt", (1, SEQ, D)), ("y_sample", (DEC_B, DEC_S, D)),
           ("k_sb_p", (1, 1, SEQ, H, DH)), ("v_sb_p", (1, 1, SEQ, H, DH)),
           ("k_sb_s", (1, DEC_B, DEC_S, H, DH)), ("v_sb_s", (1, DEC_B, DEC_S, H, DH)),
           ("k_win_p", (1, 1, SEQ, H, DH)), ("v_win_p", (1, 1, SEQ, H, DH)),
           ("k_win_s", (1, DEC_B, WIN, H, DH)), ("v_win_s", (1, DEC_B, WIN, H, DH))]


def shape_constants():
    import numpy as np
    f32 = np.float32
    k, q = np.arange(P)[:, None], np.arange(P)[None, :]
    inv = np.power(f32(500000.0), -(np.arange(ROT // 2, dtype=f32) * f32(2.0) / f32(ROT))).astype(f32)
    pos = np.concatenate([np.resize(PAGES * PAGE + np.arange(DEC_S), P), np.arange(SEQ)]).astype(f32)
    ang = (pos[:, None] * inv[None, :]).astype(f32)
    rope = np.concatenate([np.cos(ang), np.sin(ang)], 1).astype(f32).reshape(TILES + 1, P, ROT)
    out = {"ident": np.eye(P, dtype=f32), "rope": rope}
    out["suffix"] = np.stack([-(k >= q).astype(f32), -np.ones((P, P), f32)])
    q, k = np.arange(P)[:, None], np.arange(P)[None, :]
    own = np.where(k <= q, 0.0, NEG)
    before = np.where(k >= q, 0.0, NEG)
    never = np.full((P, P), NEG)
    out["masks"] = np.stack([np.concatenate([own, never, before, own], 1),
                             np.concatenate([before, own, before, own], 1),
                             np.concatenate([own, own, own, own], 1)]).astype(f32)
    new, s = np.arange(NS), np.arange(PAIRS * 2 * DEC_S) % DEC_S
    out["valid_new"] = ((new[:, None, None] // DEC_S == np.arange(DEC_B)[None, :, None])
                        & (new[:, None, None] % DEC_S < s[None, None, :])).astype(f32)
    tok = (np.arange(H * DEC_S) % DEC_S)[:, None]
    dist = 512 + tok - np.arange(512)[None, :]
    recent = (dist <= 128).astype(f32) + ((dist % 4 == 0) & (dist <= 512))
    strided = np.broadcast_to(tok == np.repeat(np.arange(DEC_S), P)[None, :], (H * DEC_S, 512))
    fresh = (np.arange(DEC_S)[None, :] <= tok) + 2 * (np.arange(DEC_S)[None, :] == tok)
    out["win_count"] = np.concatenate([recent, strided, fresh], 1).astype(f32)
    out["win_mask"] = np.where(out["win_count"] > 0, 0.0, NEG).astype(f32)
    out["own_head"] = (np.arange(H * DEC_S)[:, None] // DEC_S == np.arange(W)[None, :] // DH).astype(f32)
    out["pick"] = (tok == np.arange(DEC_S)[None, :]).astype(f32)
    out["lse_one"] = np.repeat(np.array([[0.0, -1e30, -1e30]]), NS, 0).repeat(H, 1).astype(f32)
    return out


def kernel(**inputs):
    import numpy as np
    import concourse.bacc as bacc
    from concourse.bass_utils import run_bass_kernel_spmd as run

    nc = bacc.Bacc("TRN2", target_bir_lowering=False, num_devices=1)
    arrays, t = {}, {}
    for name in INPUTS:
        arrays[f"in_{name}"] = np.ascontiguousarray(inputs[name])
    for name, a in shape_constants().items():
        arrays[f"in_{name}"] = a
    for name, a in arrays.items():
        t[name[3:]] = nc.dram_tensor(name, a.shape, mybir.dt.from_np(a.dtype), kind="ExternalInput").ap()
    for name, shape in OUTPUTS:
        t[name] = nc.dram_tensor(f"out_{name}", shape, F32, kind="ExternalOutput").ap()
    build(nc, t)
    r = run(nc, [arrays], core_ids=[0])
    return tuple(r.results[0][f"out_{name}"] for name, _ in OUTPUTS)
```

```python
import concourse.bass as bass
from concourse import mybir
from contextlib import ExitStack

F32 = mybir.dt.float32
F32R = mybir.dt.float32r
I32 = mybir.dt.int32
ALU = mybir.AluOpType
ACT = mybir.ActivationFunctionType
AX = mybir.AxisListType

P = 128
D = 1024
SEQ = 2048
DEC_B, DEC_S = 8, 4
NS = DEC_B * DEC_S
H, DH = 8, 64
W = H * DH
PAIRS = H // 2
PAGE, PAGES = 128, 64
WIN = 2048
PLE = 256
EPS = 1e-6
TILES = SEQ // P
KC = D // P
ROT = DH // 4
NEG = -3.0e38
BIG = 2.0 ** 60
LN_EXP_SET = 6


class Mem:

    def __init__(self, nc, ctx, tag):
        self.nc, self.ctx, self.tag = nc, ctx, tag
        self.used = []
        ctx.callback(self.clear)

    def clear(self):
        self.nc.clear_and_free_semaphores(self.used)
        self.nc.all_engine_barrier()

    def sb(self, name, shape, dt=F32):
        return self.ctx.enter_context(self.nc.sbuf_tensor(f"{self.tag}_{name}", shape, dt))

    def ps(self, name, shape):
        return self.ctx.enter_context(self.nc.psum_tensor(f"{self.tag}_{name}", shape, F32))

    def sem(self, name):
        self.used.append(self.nc.alloc_semaphore(name=f"{self.tag}_{name}"))
        return self.used[-1]

    def sems(self, name, n):
        return [self.sem(f"{name}{i}") for i in range(n)]


def load_exp_ln_table(nc, act):
    act.add_instruction(mybir.InstLoadActFuncSet(
        name=nc.get_next_instruction_name(), act_func_set_id=LN_EXP_SET,
        engine=mybir.EngineType.Activation, ins=[], outs=[]))


def flat(ap):
    n = len(ap.shape)
    if n == 5:
        return ap.rearrange("a b s h d -> (a b s) (h d)")
    return ap


def hold(eng, sem, value):
    eng.wait_ge(sem, value)
    if not isinstance(value, int):
        eng.sem_inc(TICK[0], 1)


TICK = [None]


def steps(eng, body):
    for item in (0, 1, 2):
        body(item, item % 2, item // 2)
    with eng.Fori(1, TILES // 2 - 1) as o:
        body(1 + 2 * o, 1, o)
        body(2 + 2 * o, 0, o + 1)
    for item in (TILES - 1, TILES):
        body(item, item % 2, item // 2)


def following(item, slot, use):
    return item + 1, 1 - slot, use + slot


def first(item):
    return isinstance(item, int) and item == 0


def last(item):
    return isinstance(item, int) and item == TILES


def project(nc, t, half):
    mixer_b = half == 1
    GROUPS = 4
    C0 = half * GROUPS * W
    QK_STEPS = 6
    ctx = ExitStack()
    with ctx:
        m = Mem(nc, ctx, f"proj{half}")
        w_hi = m.sb("w_hi", [P, KC, GROUPS * W], F32R)
        w_lo = m.sb("w_lo", [P, KC, GROUPS * W], F32R)
        x_in = m.sb("x_in", [P, 2, D])
        xT_hi = m.sb("xT_hi", [P, 2, KC, P], F32R)
        xT_lo = m.sb("xT_lo", [P, 2, KC, P], F32R)
        out = m.sb("out", [P, 2, GROUPS * W])
        junk = m.sb("junk", [P, D])
        g_attn = m.sb("g_attn", [P, KC])
        ident = m.sb("ident", [P, P])
        stat = m.sb("stat", [P, 2, 4])
        mhalf = m.sb("mhalf", [P, 2 * H])
        if mixer_b:
            qk_sq = m.sb("qk_sq", [P, 2 * W])
            g_qk = m.sb("g_qk", [P, 2, DH])
            rope = m.sb("rope", [P, TILES + 1, ROT])
            hstat = m.sb("hstat", [P, 2, 3, 2 * H])
            rt = m.sb("rt", [P, 4, 2 * H, ROT // 2])
        ps_T = m.ps("ps_T", [P, 2, 512])
        ps_G = m.ps("ps_G", [P, GROUPS, 512])

        w_loaded = m.sems("w_loaded", 2)
        w_hi_done = m.sem("w_hi_done")
        w_split = m.sem("w_split")
        consts = m.sem("consts")
        mhalf_set = m.sem("mhalf_set")
        x_loaded = m.sems("x_loaded", 2)
        x_squared = m.sem("x_squared")
        x_turned = m.sem("x_turned")
        hi_done = m.sem("hi_done")
        lo_done = m.sem("lo_done")
        mean_done = m.sem("mean_done")
        rms_done = m.sem("rms_done")
        grp_done = m.sem("grp_done")
        evacuated = m.sem("evacuated")
        stored = [m.sems(f"stored{g}_", 2) for g in range(GROUPS)]
        win_copied = m.sem("win_copied")
        if mixer_b:
            gq_set = m.sem("gq_set")
            sq_done = m.sem("sq_done")
            ssum_done = m.sem("ssum_done")
            hmean_done = m.sem("hmean_done")
            hrms_done = m.sem("hrms_done")
            qk_step = m.sem("qk_step")

        def rows_of(item):
            return NS if first(item) else P

        w_rows = t["w_in"][0].rearrange("(c p) e -> p c e", p=P)
        x_p, x_s = t["x_prompt"][0], t["x_sample"].rearrange("b s d -> (b s) d")
        if mixer_b:
            dst_p = [t["q_dl"], flat(t["k_win_p"]), flat(t["v_win_p"]), t["z_dl"]]
            win_rows = [t[n][0].rearrange("b s h d -> b s (h d)")[:, WIN - DEC_S:WIN, :]
                        for n in ("k_win_s", "v_win_s")]
            dst_s = [t["q_dl_s"], win_rows[0], win_rows[1], t["z_dl_s"]]
        else:
            dst_p = [t["q_sb"], flat(t["k_sb_p"]), flat(t["v_sb_p"]), t["z_sb"]]
            dst_s = [t["q_sb_s"], flat(t["k_sb_s"]), flat(t["v_sb_s"]), t["z_sb_s"]]
        old_win = t["cache_v_win" if mixer_b else "cache_k_win"][0].rearrange("b s h d -> b s (h d)")
        new_win = t["v_win_s" if mixer_b else "k_win_s"][0].rearrange("b s h d -> b s (h d)")
        HALF_WIN = (WIN - DEC_S) // 2
        block = ctx.enter_context(nc.Block())

        @block.sync
        def _(sp):
            sp.dma_start(ident[:, :], t["ident"][:, :]).then_inc(consts, 16)
            with nc.allow_non_contiguous_dma(reason="the 1024 weights of the norm, once"):
                sp.dma_start(g_attn[:, :], t["attn_norm"][0].rearrange("(c p) -> p c", p=P)).then_inc(consts, 16)
            if mixer_b:
                for i, n in enumerate(("q_norm_dil", "k_norm_dil")):
                    sp.dma_start(g_qk[:, i, :], t[n][0:1, :].to_broadcast([P, DH])).then_inc(consts, 16)
                sp.dma_start(rope[:, :, :], t["rope"].rearrange("n p r -> p n r")).then_inc(consts, 16)
            for c in range(2 * KC):
                if c >= 2:
                    hold(sp, w_split, c - 1)
                sp.dma_start(x_in[:, c % 2, :], w_rows[:, c // 2, C0 + (c % 2) * D:C0 + (c % 2 + 1) * D]) \
                    .then_inc(w_loaded[c % 2], 16)
            hold(sp, w_split, 2 * KC)

            def load(item, slot):
                n = rows_of(item)
                src = x_s if first(item) else x_p[bass.ts(item - 1, P), :]
                sp.dma_start(x_in[0:n, slot, :], src).then_inc(x_loaded[slot], 16)

            def body(item, slot, use):
                n = rows_of(item)
                if not last(item):
                    if not first(item):
                        hold(sp, x_squared, item)
                        hold(sp, x_turned, 2 * item)
                    load(item + 1, 1 - slot)
                for g in range(GROUPS):
                    if mixer_b and g < 2:
                        hold(sp, qk_step, QK_STEPS * item + QK_STEPS)
                    else:
                        hold(sp, evacuated, GROUPS * item + g + 1)
                    dst = dst_s[g] if first(item) else dst_p[g][bass.ts(item - 1, P), :]
                    sp.dma_start(dst, out[0:n, slot, g * W:(g + 1) * W]).then_inc(stored[g][slot], 16)

            load(0, 0)
            steps(sp, body)
            for g in range(GROUPS):
                hold(sp, stored[g][0], 16 * (TILES // 2 + 1))
                hold(sp, stored[g][1], 16 * (TILES // 2))

        @block.gpsimd
        def _(pool):
            nc.gpsimd.memset(mhalf[:, :], -0.5).then_inc(mhalf_set, 1)
            hold(pool, mhalf_set, 1)

            def rms(item, slot, use):
                n = rows_of(item)
                hold(pool, x_squared, item + 1)
                if not (isinstance(item, int) and item < 2):
                    hold(pool, evacuated, GROUPS * item - GROUPS)
                nc.gpsimd.tensor_scalar(stat[0:n, slot, 1:2], stat[0:n, slot, 0:1], 1.0 / D, EPS,
                                        ALU.mult, ALU.add).then_inc(mean_done, 1)
                hold(pool, mean_done, item + 1)
                nc.gpsimd.tensor_tensor(stat[0:n, slot, 2:3], stat[0:n, slot, 1:2], mhalf[0:n, 0:1], ALU.pow) \
                    .then_inc(rms_done, 1)
                hold(pool, rms_done, 2 * item + 1)
                nc.gpsimd.tensor_scalar(stat[0:n, slot, 3:4], stat[0:n, slot, 2:3], 1.0 / 8, None, ALU.mult) \
                    .then_inc(rms_done, 1)

            def body(item, slot, use):
                n = rows_of(item)
                if not last(item):
                    rms(*following(item, slot, use))
                if not first(item):
                    b, j = (item - 1) // 2 if isinstance(item, int) else (use if slot else use - 1), 1 - slot
                    pool.dma_start(new_win[bass.ds(b, 1), j * HALF_WIN:(j + 1) * HALF_WIN, :],
                                   old_win[bass.ds(b, 1), DEC_S + j * HALF_WIN:DEC_S + (j + 1) * HALF_WIN, :]) \
                        .then_inc(win_copied, 16)
                if mixer_b:
                    hold(pool, ssum_done, item + 1)
                    nc.gpsimd.tensor_scalar(hstat[0:n, slot, 1, :], hstat[0:n, slot, 0, :], 1.0 / DH, EPS,
                                            ALU.mult, ALU.add).then_inc(hmean_done, 1)
                    hold(pool, hmean_done, item + 1)
                    nc.gpsimd.tensor_tensor(hstat[0:n, slot, 2, :], hstat[0:n, slot, 1, :], mhalf[0:n, :], ALU.pow) \
                        .then_inc(hrms_done, 1)

            rms(0, 0, 0)
            steps(pool, body)
            hold(pool, win_copied, 16 * 2 * DEC_B)

        @block.vector
        def _(dve):
            dve.wait_ge(consts, 80 if mixer_b else 32)
            if mixer_b:
                nc.vector.tensor_scalar(g_qk[:, 0, :], g_qk[:, 0, :], 1.0 / 8, None, ALU.mult).then_inc(gq_set, 1)
                dve.wait_ge(gq_set, 1)
            for c in range(2 * KC):
                k, cols = c // 2, slice((c % 2) * D, (c % 2 + 1) * D)
                dve.wait_ge(w_loaded[c % 2], 16 * (c // 2 + 1))
                nc.vector.tensor_scalar(w_hi[:, k, cols], x_in[:, c % 2, :], g_attn[:, k:k + 1], None, ALU.mult) \
                    .then_inc(w_hi_done, 1)
                dve.wait_ge(w_hi_done, c + 1)
                nc.vector.scalar_tensor_tensor(out=w_lo[:, k, cols], in0=x_in[:, c % 2, :], scalar=g_attn[:, k:k + 1],
                                               in1=w_hi[:, k, cols].bitcast(F32), op0=ALU.mult,
                                               op1=ALU.subtract).then_inc(w_split, 1)

            def low_parts(item, slot, use):
                n = rows_of(item)
                for b in range(2):
                    dve.wait_ge(hi_done, 2 * item + b + 1)
                    src = ps_T[:, b, :].rearrange("p (c r) -> p c r", r=P)[:, :, 0:n]
                    nc.vector.tensor_tensor(xT_lo[:, slot, 4 * b:4 * b + 4, 0:n], src,
                                            xT_hi[:, slot, 4 * b:4 * b + 4, 0:n].bitcast(F32),
                                            ALU.subtract).then_inc(lo_done, 1)

            def norm_rotate(item, slot, use):
                n = rows_of(item)
                dve.wait_ge(sq_done, item + 1)
                nc.vector.tensor_reduce(hstat[0:n, slot, 0, :], qk_sq[0:n, :].rearrange("p (h d) -> p h d", d=DH),
                                        AX.X, ALU.add).then_inc(ssum_done, 1)
                qk = out[0:n, slot, 0:2 * W].rearrange("p (h d) -> p h d", d=DH)
                dve.wait_ge(hrms_done, item + 1)
                base = QK_STEPS * item
                nc.vector.tensor_tensor(qk, qk, hstat[0:n, slot, 2, :].unsqueeze(2).to_broadcast([n, 2 * H, DH]),
                                        ALU.mult).then_inc(qk_step, 1)
                dve.wait_ge(qk_step, base + 1)
                for i in range(2):
                    part = qk[:, i * H:(i + 1) * H, :]
                    nc.vector.tensor_tensor(part, part, g_qk[0:n, i:i + 1, :].to_broadcast([n, H, DH]),
                                            ALU.mult).then_inc(qk_step, 1)
                dve.wait_ge(qk_step, base + 3)
                x1, x2 = qk[:, :, 0:8], qk[:, :, 8:16]
                cos = rope[0:n, bass.ds(item, 1), 0:8].to_broadcast([n, 2 * H, 8])
                sin = rope[0:n, bass.ds(item, 1), 8:16].to_broadcast([n, 2 * H, 8])
                for i, (x, f) in enumerate(((x1, cos), (x2, sin), (x2, cos), (x1, sin))):
                    rot = nc.vector.tensor_tensor(rt[0:n, i], x, f, ALU.mult)
                rot.then_inc(qk_step, 1)
                dve.wait_ge(qk_step, base + 4)
                nc.vector.tensor_tensor(x1, rt[0:n, 0], rt[0:n, 1], ALU.subtract).then_inc(qk_step, 1)
                nc.vector.tensor_tensor(x2, rt[0:n, 2], rt[0:n, 3], ALU.add).then_inc(qk_step, 1)

            def body(item, slot, use):
                if not last(item):
                    low_parts(*following(item, slot, use))
                if mixer_b:
                    norm_rotate(item, slot, use)

            low_parts(0, 0, 0)
            steps(dve, body)

        @block.scalar
        def _(act):
            load_exp_ln_table(nc, act)

            def high_parts(item, slot, use):
                n = rows_of(item)
                act.wait_ge(x_loaded[slot], 16 * use + 16)
                nc.scalar.activation(junk[0:n, :], x_in[0:n, slot, :], ACT.Square,
                                     accum_out=stat[0:n, slot, 0:1]).then_inc(x_squared, 1)
                for b in range(2):
                    act.wait_ge(x_turned, 2 * item + b + 1)
                    src = ps_T[:, b, :].rearrange("p (c r) -> p c r", r=P)[:, :, 0:n]
                    nc.scalar.activation(xT_hi[:, slot, 4 * b:4 * b + 4, 0:n], src, ACT.Copy).then_inc(hi_done, 1)

            def body(item, slot, use):
                n = rows_of(item)
                act.wait_ge(rms_done, 2 * item + 2)
                for g in range(GROUPS):
                    act.wait_ge(grp_done, GROUPS * item + g + 1)
                    if not (isinstance(item, int) and item < 2):
                        act.wait_ge(stored[g][slot], 16 * use)
                    r = 3 if (g == 0 and not mixer_b) else 2
                    nc.scalar.activation(out[0:n, slot, g * W:(g + 1) * W], ps_G[0:n, g, :], ACT.Copy,
                                         scale=stat[0:n, slot, r:r + 1]).then_inc(evacuated, 1)
                    if g == 1:
                        if mixer_b:
                            act.wait_ge(evacuated, GROUPS * item + 2)
                            if not first(item):
                                act.wait_ge(ssum_done, item)
                            nc.scalar.activation(qk_sq[0:n, :], out[0:n, slot, 0:2 * W], ACT.Square) \
                                .then_inc(sq_done, 1)
                        if not last(item):
                            high_parts(*following(item, slot, use))

            high_parts(0, 0, 0)
            steps(act, body)

        @block.tensor
        def _(pe):
            def turn(item, slot, use):
                n = rows_of(item)
                pe.wait_ge(x_loaded[slot], 16 * use + 16)
                for b in range(2):
                    if not first(item):
                        pe.wait_ge(lo_done, 2 * item - 1 + b)
                    for c in range(4):
                        k = 4 * b + c
                        last_t = nc.tensor.transpose(ps_T[:, b, c * P:c * P + n], x_in[0:n, slot, k * P:(k + 1) * P],
                                                     ident[0:n, 0:n])
                    last_t.then_inc(x_turned, 1)

            def body(item, slot, use):
                n = rows_of(item)
                pe.wait_ge(lo_done, 2 * item + 2)
                for g in range(GROUPS):
                    if not first(item):
                        pe.wait_ge(evacuated, GROUPS * item - GROUPS + g + 1)
                    for k in range(KC):
                        cols = slice(g * W, (g + 1) * W)
                        nc.tensor.matmul(ps_G[0:n, g, :], xT_hi[:, slot, k, 0:n], w_hi[:, k, cols],
                                         start=(k == 0), stop=False)
                        nc.tensor.matmul(ps_G[0:n, g, :], xT_hi[:, slot, k, 0:n], w_lo[:, k, cols],
                                         start=False, stop=False)
                        mm = nc.tensor.matmul(ps_G[0:n, g, :], xT_lo[:, slot, k, 0:n], w_hi[:, k, cols],
                                              start=False, stop=(k == KC - 1))
                    mm.then_inc(grp_done, 1)
                    if g == 1 and not last(item):
                        turn(*following(item, slot, use))

            pe.wait_ge(consts, 80 if mixer_b else 32)
            turn(0, 0, 0)
            pe.wait_ge(w_split, 2 * KC)
            steps(pe, body)


def stick_breaking_prompt(nc, t):
    QT = 512 // P
    NQ = TILES // QT
    ITEMS = []
    for Q in range(NQ):
        for s in range(QT * Q + QT):
            for h in range(2):
                ITEMS.append((Q, QT * Q + QT - 1 - s, h, s))
    NI = len(ITEMS)
    FILLS = 2 * NQ
    ZB = 6

    def first_col(i):
        Q, j, h, s = ITEMS[i]
        return max(0, j - QT * Q) * P

    def diagonal(i):
        return ITEMS[i][1] >= QT * ITEMS[i][0]

    def closes(i):
        return ITEMS[i][1] == 0

    DIAGS = sum(diagonal(i) for i in range(NI))
    CLOSES = sum(closes(i) for i in range(NI))

    def diags_to(i):
        return sum(diagonal(x) for x in range(i + 1))

    def closes_to(i):
        return sum(closes(x) for x in range(i + 1))

    ctx = ExitStack()
    with ctx:
        m = Mem(nc, ctx, "sbp")
        ident = m.sb("ident", [P, P])
        suffix = m.sb("suffix", [P, 2, P])
        suf_r = m.sb("suf_r", [P, P], F32R)
        bias = m.sb("bias", [P, H])
        bias_pair = m.sb("bias_pair", [P, 2])
        qk_in = m.sb("qk_in", [P, 2, TILES, P])
        v_all = m.sb("v_all", [P, TILES, W])
        T_hi = m.sb("T_hi", [P, 2, SEQ], F32R)
        T_lo = m.sb("T_lo", [P, 2, SEQ], F32R)
        el = m.sb("el", [P, 4, 512])
        sp_ = m.sb("sp", [P, 4, 512])
        sp_hi = m.sb("sp_hi", [P, 4, 512], F32R)
        sp_lo = m.sb("sp_lo", [P, 4, 512], F32R)
        S = m.sb("S", [P, 2, 2, 512])
        a = m.sb("a", [P, 4, 512])
        o_out = m.sb("o_out", [P, TILES, P])
        Z = m.ps("Z", [P, ZB, 512])
        O = m.ps("O", [P, 2, 512])

        consts = m.sem("consts")
        suf_done = m.sem("suf_done")
        v_loaded = m.sem("v_loaded")
        qk_loaded = m.sem("qk_loaded")
        turned = m.sem("turned")
        turn_hi = m.sem("turn_hi")
        turn_lo = m.sem("turn_lo")
        bias_set = m.sem("bias_set")
        z_done = m.sem("z_done")
        exp_done = m.sem("exp_done")
        cut_done = m.sem("cut_done")
        ln_done = m.sem("ln_done")
        sp_done = m.sem("sp_done")
        sp_masked = m.sem("sp_masked")
        hi_done = m.sem("hi_done")
        lo_done = m.sem("lo_done")
        S_done = m.sem("S_done")
        sum_done = m.sem("sum_done")
        a_done = m.sem("a_done")
        a_masked = m.sem("a_masked")
        av_done = m.sem("av_done")
        o_copied = m.sem("o_copied")
        o_stored = m.sem("o_stored")
        o_free = m.sem("o_free")

        q_rows = t["q_sb"].rearrange("(n p) c -> p n c", p=P)
        k_rows = flat(t["k_sb_p"]).rearrange("(n p) c -> p n c", p=P)
        v_rows = flat(t["v_sb_p"]).rearrange("(n p) c -> p n c", p=P)
        o_rows = t["o_sb"].rearrange("(n p) c -> p n c", p=P)
        block = ctx.enter_context(nc.Block())

        @block.sync
        def _(sp):
            sp.dma_start(ident[:, :], t["ident"][:, :]).then_inc(consts, 16)
            sp.dma_start(suffix[:, :, :], t["suffix"].rearrange("a p c -> p a c")).then_inc(consts, 16)
            sp.dma_start(bias[:, :], t["sb_bias"][0:1, :].to_broadcast([P, H])).then_inc(consts, 16)

            def load(p):
                sp.dma_start(qk_in[:, 0, :, :], q_rows[:, :, bass.ts(p, P)]).then_inc(qk_loaded, 16)
                sp.dma_start(qk_in[:, 1, :, :], k_rows[:, :, bass.ts(p, P)]).then_inc(qk_loaded, 16)

            def store(p):
                hold(sp, o_copied, CLOSES * p + CLOSES)
                sp.dma_start(o_rows[:, :, bass.ts(p, P)], o_out[:, :, :]).then_inc(o_stored, 16)
                hold(sp, o_stored, 16 * p + 16)
                sp.sem_inc(o_free, 1)

            sp.sem_inc(o_free, 1)
            load(0)
            sp.dma_start(v_all[:, :, :], v_rows).then_inc(v_loaded, 16)
            with sp.Fori(0, PAIRS - 1) as p:
                hold(sp, turned, FILLS * p + FILLS)
                load(p + 1)
                store(p)
            store(PAIRS - 1)
            sp.wait_ge(o_stored, 16 * PAIRS)

        @block.gpsimd
        def _(pool):
            with pool.Fori(0, PAIRS) as p:
                B, BD = NI * p, DIAGS * p
                for T in range(-2, NI + 2):
                    i = T + 2
                    if i < NI:
                        c = first_col(i)
                        hold(pool, sp_done, B + i + 1)
                        if diagonal(i):
                            blk = sp_[:, i % 4, c:c + P]
                            nc.gpsimd.affine_select(out=blk, in_=blk, compare_op=ALU.is_gt, fill=0.0, base=0,
                                                    pattern=[[1, P]], channel_multiplier=-1).then_inc(sp_masked, 1)
                            hold(pool, sp_masked, BD + diags_to(i))
                        if i >= 4:
                            hold(pool, sum_done, B + i - 3)
                        nc.gpsimd.tensor_copy(sp_hi[:, i % 4, c:512], sp_[:, i % 4, c:512]).then_inc(hi_done, 1)
                    i = T - 1
                    if 0 <= i < NI and diagonal(i):
                        c = first_col(i)
                        hold(pool, a_done, B + i + 1)
                        blk = a[:, i % 4, c:c + P]
                        nc.gpsimd.affine_select(out=blk, in_=blk, compare_op=ALU.is_gt, fill=0.0, base=0,
                                                pattern=[[1, P]], channel_multiplier=-1).then_inc(a_masked, 1)

        @block.vector
        def _(dve):
            dve.wait_ge(consts, 48)
            nc.vector.tensor_copy(suf_r[:, :], suffix[:, 0, :]).then_inc(suf_done, 1)
            with dve.Fori(0, PAIRS) as p:
                B, BF = NI * p, FILLS * p
                for f in range(FILLS):
                    dve.wait_ge(turn_hi, BF + f + 1)
                    if f == 0:
                        nc.vector.tensor_copy(bias_pair[:, :], bias[:, bass.ts(p, 2)]).then_inc(bias_set, 1)
                    cols = slice((f % NQ) * 512, (f % NQ + 1) * 512)
                    nc.vector.tensor_tensor(T_lo[:, f // NQ, cols], Z[:, f % ZB, :],
                                            T_hi[:, f // NQ, cols].bitcast(F32), ALU.subtract).then_inc(turn_lo, 1)
                for T in range(-4, NI):
                    i = T + 4
                    if i < NI:
                        dve.wait_ge(exp_done, B + i + 1)
                        c = first_col(i)
                        nc.vector.tensor_scalar(el[:, i % 4, c:512], el[:, i % 4, c:512], BIG, None, ALU.min) \
                            .then_inc(cut_done, 1)
                    i = T + 2
                    if 0 <= i < NI:
                        c, h = first_col(i), ITEMS[i][2]
                        dve.wait_ge(ln_done, B + i + 1)
                        nc.vector.scalar_tensor_tensor(out=sp_[:, i % 4, c:512], in0=Z[:, i % ZB, c:512],
                                                       scalar=bias_pair[:, h:h + 1], in1=el[:, i % 4, c:512],
                                                       op0=ALU.add, op1=ALU.max).then_inc(sp_done, 1)
                    i = T + 1
                    if 0 <= i < NI:
                        c, (Q, j, h, s) = first_col(i), ITEMS[i]
                        dve.wait_ge(hi_done, B + i + 1)
                        if i >= 4:
                            dve.wait_ge(sum_done, B + i - 3)
                        nc.vector.tensor_tensor(sp_lo[:, i % 4, c:512], sp_[:, i % 4, c:512],
                                                sp_hi[:, i % 4, c:512].bitcast(F32), ALU.subtract).then_inc(lo_done, 1)
                        if i >= 2:
                            dve.wait_ge(sum_done, B + i - 1)
                            dve.wait_ge(S_done, B + i - 1)
                        c0 = 512 if s == 0 else first_col(i - 2)
                        if c < c0:
                            op = nc.vector.tensor_copy(S[:, h, (s + 1) % 2, c:c0], sp_[:, i % 4, c:c0])
                        if c0 < 512:
                            op = nc.vector.tensor_tensor(S[:, h, (s + 1) % 2, c0:512], S[:, h, s % 2, c0:512],
                                                         sp_[:, i % 4, c0:512], ALU.add)
                        op.then_inc(S_done, 1)

        @block.scalar
        def _(act):
            load_exp_ln_table(nc, act)
            with act.Fori(0, PAIRS) as p:
                B, BF, BC = NI * p, FILLS * p, CLOSES * p
                for f in range(FILLS):
                    act.wait_ge(turned, BF + f + 1)
                    nc.scalar.activation(T_hi[:, f // NQ, (f % NQ) * 512:(f % NQ + 1) * 512], Z[:, f % ZB, :],
                                         ACT.Copy).then_inc(turn_hi, 1)
                for T in range(-4, NI + 4):
                    i = T + 4
                    if i < NI:
                        c, h = first_col(i), ITEMS[i][2]
                        act.wait_ge(z_done, B + i + 1)
                        if i >= 4:
                            act.wait_ge(sp_done, B + i - 3)
                        nc.scalar.activation(el[:, i % 4, c:512], Z[:, i % ZB, c:512], ACT.Exp,
                                             bias=bias_pair[:, h:h + 1]).then_inc(exp_done, 1)
                    i = T + 3
                    if 0 <= i < NI:
                        c = first_col(i)
                        act.wait_ge(cut_done, B + i + 1)
                        nc.scalar.activation(el[:, i % 4, c:512], el[:, i % 4, c:512], ACT.Ln, bias=1.0) \
                            .then_inc(ln_done, 1)
                    i = T - 1
                    if 0 <= i < NI:
                        c, h = first_col(i), ITEMS[i][2]
                        act.wait_ge(sum_done, B + i + 1)
                        if i >= 4:
                            act.wait_ge(av_done, B + i - 3 + 1)
                        nc.scalar.activation(a[:, i % 4, c:512], Z[:, i % ZB, c:512], ACT.Exp,
                                             bias=bias_pair[:, h:h + 1]).then_inc(a_done, 1)
                    i = T - 3
                    if 0 <= i < NI and closes(i):
                        Q, j, h, s = ITEMS[i]
                        act.wait_ge(av_done, B + i + 2)
                        if closes_to(i) == 1:
                            act.wait_ge(o_free, p + 1)
                        nc.scalar.activation(o_out[:, QT * Q:QT * Q + QT, h * DH:(h + 1) * DH],
                                             O[:, h, 0:QT * DH].rearrange("p (n d) -> p n d", d=DH), ACT.Copy) \
                            .then_inc(o_copied, 1)

        @block.tensor
        def _(pe):
            pe.wait_ge(consts, 48)
            pe.wait_ge(suf_done, 1)
            pe.wait_ge(v_loaded, 16)
            pe.sem_inc(av_done, 1)
            with pe.Fori(0, PAIRS) as p:
                B, BD, BF, BC = NI * p, DIAGS * p, FILLS * p, CLOSES * p
                pe.wait_ge(qk_loaded, 32 * p + 32)
                pe.wait_ge(av_done, B + 1)
                for f in range(FILLS):
                    if f >= ZB:
                        pe.wait_ge(turn_lo, BF + f - ZB + 1)
                    for n in range(4):
                        tr = nc.tensor.transpose(Z[:, f % ZB, n * P:(n + 1) * P], qk_in[:, f // NQ, 4 * (f % NQ) + n, :],
                                                 ident[:, :])
                    tr.then_inc(turned, 1)
                pe.wait_ge(turn_lo, BF + FILLS)
                for T in range(-4, NI + 2):
                    i = T + 4
                    if i < NI:
                        c, (Q, j, h, s) = first_col(i), ITEMS[i]
                        if i >= ZB:
                            pe.wait_ge(a_done, B + i - ZB + 1)
                        r, keys, qs = slice(h * DH, (h + 1) * DH), slice(j * P, (j + 1) * P), slice(Q * 512 + c, Q * 512 + 512)
                        for n, (kt, qt) in enumerate(((T_hi, T_hi), (T_lo, T_hi), (T_hi, T_lo))):
                            mm = nc.tensor.matmul(Z[:, i % ZB, c:512], kt[r, 1, keys], qt[r, 0, qs], start=(n == 0),
                                                  stop=(n == 2), skip_group_check=True)
                        mm.then_inc(z_done, 1)
                    i = T
                    if 0 <= i < NI:
                        c, (Q, j, h, s) = first_col(i), ITEMS[i]
                        if s > 0:
                            pe.wait_ge(S_done, B + i - 1)
                            c0 = first_col(i - 2)
                            nc.tensor.matmul(Z[:, i % ZB, c0:512], suffix[:, 1, :], S[:, h, s % 2, c0:512], start=False,
                                             stop=False, skip_group_check=True)
                        pe.wait_ge(lo_done, B + i + 1)
                        nc.tensor.matmul(Z[:, i % ZB, c:512], suf_r[:, :], sp_hi[:, i % 4, c:512], start=False, stop=False,
                                         skip_group_check=True)
                        nc.tensor.matmul(Z[:, i % ZB, c:512], suf_r[:, :], sp_lo[:, i % 4, c:512], start=False, stop=True,
                                         skip_group_check=True).then_inc(sum_done, 1)
                    i = T - 2
                    if 0 <= i < NI:
                        c, (Q, j, h, s) = first_col(i), ITEMS[i]
                        if diagonal(i):
                            pe.wait_ge(a_masked, BD + diags_to(i))
                        else:
                            pe.wait_ge(a_done, B + i + 1)
                        if s == 0 and Q > 0:
                            pe.wait_ge(o_copied, BC + 2 * Q - 1 + h)
                        for b in range(c // P, QT):
                            mm = nc.tensor.matmul(O[:, h, b * DH:(b + 1) * DH], a[:, i % 4, b * P:(b + 1) * P],
                                                  v_all[:, j, bass.ds(p * P + h * DH, DH)],
                                                  start=(s == 0 and b == QT - 1), stop=closes(i), skip_group_check=True)
                        mm.then_inc(av_done, 1)


def dilated_prompt(nc, t):
    DILS = (1, 4, 16)
    ITEMS = []
    for br, dil in enumerate(DILS):
        per = 4 if dil == 16 else 2
        for T in range(0, TILES, per):
            for h in range(2):
                ITEMS.append((br, T, h))
    NI = len(ITEMS)
    FILLS, FB = 8, 4

    def tiles(i):
        br, T, h = ITEMS[i]
        dil = DILS[br]
        runs = TILES // dil
        out = []
        for x in range(T, T + (4 if dil == 16 else 2)):
            g, n = x // runs, x % runs
            out.append((x, g + dil * P * n, n == 0))
        return out

    def blocks(i):
        return 1 if ITEMS[i][0] == 2 else 2

    def closes(i):
        return i + 1 == NI or (ITEMS[i + 1][0] != ITEMS[i][0])

    def branch_items_to(br):
        return sum(1 for x in ITEMS if x[0] <= br)

    ctx = ExitStack()
    with ctx:
        m = Mem(nc, ctx, "dil")
        ident = m.sb("ident", [P, P])
        masks = m.sb("masks", [P, 3, 512])
        qk_in = m.sb("qk_in", [P, 2, TILES, P])
        v_br = m.sb("v_br", [P, 2, TILES, P])
        T_hi = m.sb("T_hi", [P, 2, SEQ], F32R)
        T_lo = m.sb("T_lo", [P, 2, SEQ], F32R)
        sc = m.sb("sc", [P, 4, 512])
        pT = m.sb("pT", [P, 3, 512])
        nmax = m.sb("nmax", [P, 4, 4])
        rsum = m.sb("rsum", [P, 4, 4])
        inv = m.sb("inv", [P, 4, 4])
        keep = m.sb("keep", [P, 2, 2, TILES, 2])
        lse = m.sb("lse", [P, 2, TILES, 2])
        o_out = m.sb("o_out", [P, 2, TILES, P])
        Z = m.ps("Z", [P, 4, 512])
        ps_T = m.ps("ps_T", [P, 2, 512])
        O = m.ps("O", [P, 2, 512])

        consts = m.sem("consts")
        v_loaded = m.sems("v_loaded", 2)
        qk_loaded = m.sem("qk_loaded")
        turned = m.sem("turned")
        turn_hi = m.sem("turn_hi")
        turn_lo = m.sem("turn_lo")
        z_done = m.sem("z_done")
        masked = m.sem("masked")
        max_done = m.sem("max_done")
        exp_done = m.sem("exp_done")
        pt_done = m.sem("pt_done")
        pt_copied = m.sem("pt_copied")
        inv_done = m.sem("inv_done")
        av_done = m.sem("av_done")
        o_scaled = m.sem("o_scaled")
        kept = m.sem("kept")
        ln_done = m.sem("ln_done")
        lse_done = m.sem("lse_done")
        br_free = m.sem("br_free")
        stored = m.sems("stored", 2)

        q_rows = t["q_dl"].rearrange("(n p) c -> p n c", p=P)
        k_rows = flat(t["k_win_p"]).rearrange("(n p) c -> p n c", p=P)

        def run_rows(rows, br, g):
            dil = DILS[br]
            return rows.rearrange("(n p g) c -> g p n c", p=P, g=dil)[g]

        NB = 3

        def per_pairs(eng, body):
            with eng.Fori(0, PAIRS // 2) as pp:
                for u in range(2):
                    body(pp, u, 2 * pp + u)

        def bslot(u, br):
            return (NB * u + br) % 2

        def slot_dmas(pp, u, br):
            seen = [DILS[b] for v in range(2) for b in range(NB)
                    if bslot(v, b) == bslot(u, br) and (v, b) <= (u, br)]
            return sum(DILS) * pp + sum(seen)

        block = ctx.enter_context(nc.Block())

        @block.sync
        def _(sp):
            sp.dma_start(ident[:, :], t["ident"][:, :]).then_inc(consts, 16)
            sp.dma_start(masks[:, :, :], t["masks"].rearrange("a p c -> p a c")).then_inc(consts, 16)
            sp.sem_inc(br_free, 2)

            def body(pp, u, p):
                cols = bass.ts(p, P)
                hold(sp, av_done, NI * p + 1)
                sp.dma_start(qk_in[:, 0, :, :], q_rows[:, :, cols]).then_inc(qk_loaded, 16)
                sp.dma_start(qk_in[:, 1, :, :], k_rows[:, :, cols]).then_inc(qk_loaded, 16)
                for br, dil in enumerate(DILS):
                    s, runs = bslot(u, br), TILES // dil
                    if br == 2:
                        hold(sp, av_done, NI * p + 1 + branch_items_to(0))
                    for g in range(dil):
                        sp.dma_start(v_br[:, s, g * runs:(g + 1) * runs, :], run_rows(flat(t["v_win_p"]), br, g)[:, :, cols]) \
                            .then_inc(v_loaded[s], 16)
                for br, dil in enumerate(DILS):
                    s, runs = bslot(u, br), TILES // dil
                    hold(sp, o_scaled, NI * p + branch_items_to(br))
                    for g in range(dil):
                        sp.dma_start(run_rows(t["o_dil"][br], br, g)[:, :, cols], o_out[:, s, g * runs:(g + 1) * runs, :]) \
                            .then_inc(stored[s], 16)
                    hold(sp, lse_done, NB * p + br + 1)
                    for g in range(dil):
                        sp.dma_start(run_rows(t["lse_dil"][br], br, g)[:, :, bass.ts(p, 2)], lse[:, s, g * runs:(g + 1) * runs, :]) \
                            .then_inc(stored[s], 16)
                    hold(sp, stored[s], 2 * 16 * slot_dmas(pp, u, br))
                    sp.sem_inc(br_free, 1)

            per_pairs(sp, body)

        @block.vector
        def _(dve):
            dve.wait_ge(consts, 32)

            def body(pp, u, p):
                B, BF = NI * p, FILLS * p
                for f in range(FILLS):
                    dve.wait_ge(turn_hi, BF + f + 1)
                    cols = slice((f % 4) * 512, (f % 4 + 1) * 512)
                    nc.vector.tensor_tensor(T_lo[:, f // 4, cols], Z[:, f % FB, :],
                                            T_hi[:, f // 4, cols].bitcast(F32), ALU.subtract).then_inc(turn_lo, 1)
                for T in range(-1, NI + 3):
                    i = T + 1
                    if i < NI:
                        br, x, h = ITEMS[i]
                        kind = 2 if br == 2 else (0 if tiles(i)[0][2] else 1)
                        nt = len(tiles(i))
                        dve.wait_ge(z_done, B + i + 1)
                        if i >= 4:
                            dve.wait_ge(pt_done, B + i - 3)
                        nc.vector.tensor_tensor(sc[:, i % 4, :], Z[:, i % 4, :], masks[:, kind, :], ALU.add) \
                            .then_inc(masked, 1)
                        dve.wait_ge(masked, B + i + 1)
                        nc.vector.tensor_reduce(nmax[:, i % 4, 0:nt], sc[:, i % 4, :].rearrange("p (n k) -> p n k", n=nt),
                                                AX.X, ALU.max, negate=True).then_inc(max_done, 1)
                    i = T - 1
                    if 0 <= i < NI:
                        nt = len(tiles(i))
                        dve.wait_ge(exp_done, B + i + 1)
                        if i >= 4:
                            dve.wait_ge(o_scaled, B + i - 3)
                        nc.vector.reciprocal(inv[:, i % 4, 0:nt], rsum[:, i % 4, 0:nt]).then_inc(inv_done, 1)
                        br, x, h = ITEMS[i]
                        s = bslot(u, br)
                        if x == 0 and h == 0:
                            dve.wait_ge(br_free, NB * p + br + 1)
                        nc.vector.tensor_copy(keep[:, s, 0, x:x + nt, h], nmax[:, i % 4, 0:nt])
                        nc.vector.tensor_copy(keep[:, s, 1, x:x + nt, h], rsum[:, i % 4, 0:nt]).then_inc(kept, 1)
                    i = T - 3
                    if 0 <= i < NI:
                        br, x, h = ITEMS[i]
                        nt, s = len(tiles(i)), bslot(u, br)
                        dve.wait_ge(av_done, B + i + 2)
                        dve.wait_ge(inv_done, B + i + 1)
                        nc.vector.tensor_tensor(o_out[:, s, x:x + nt, h * DH:(h + 1) * DH],
                                                O[:, i % 2, 0:nt * DH].rearrange("p (n d) -> p n d", d=DH),
                                                inv[:, i % 4, 0:nt].unsqueeze(2).to_broadcast([P, nt, DH]), ALU.mult) \
                            .then_inc(o_scaled, 1)
                        if closes(i):
                            dve.wait_ge(ln_done, NB * p + br + 1)
                            nc.vector.tensor_tensor(lse[:, s, :, :], keep[:, s, 1, :, :], keep[:, s, 0, :, :],
                                                    ALU.subtract).then_inc(lse_done, 1)
                dve.wait_ge(o_scaled, B + NI)

            per_pairs(dve, body)

        @block.scalar
        def _(act):
            load_exp_ln_table(nc, act)

            def body(pp, u, p):
                B, BF = NI * p, FILLS * p
                for f in range(FILLS):
                    act.wait_ge(turned, BF + f + 1)
                    nc.scalar.activation(T_hi[:, f // 4, (f % 4) * 512:(f % 4 + 1) * 512], Z[:, f % FB, :],
                                         ACT.Copy).then_inc(turn_hi, 1)
                for T in range(0, NI + 2):
                    i = T
                    if i < NI:
                        nt = len(tiles(i))
                        w = 512 // nt
                        act.wait_ge(max_done, B + i + 1)
                        if i >= 4:
                            act.wait_ge(kept, B + i - 3)
                        for n in range(nt):
                            e = nc.scalar.activation(sc[:, i % 4, n * w:(n + 1) * w], sc[:, i % 4, n * w:(n + 1) * w],
                                                     ACT.Exp, bias=nmax[:, i % 4, n:n + 1],
                                                     accum_out=rsum[:, i % 4, n:n + 1])
                        e.then_inc(exp_done, 1)
                    i = T - 1
                    if 0 <= i < NI:
                        act.wait_ge(pt_done, B + i + 1)
                        if i >= 3:
                            act.wait_ge(av_done, B + i - 2 + 1)
                        nc.scalar.activation(pT[:, i % 3, :], ps_T[:, i % 2, :], ACT.Copy).then_inc(pt_copied, 1)
                    i = T - 2
                    if 0 <= i < NI and closes(i):
                        br = ITEMS[i][0]
                        s = bslot(u, br)
                        act.wait_ge(kept, B + i + 1)
                        nc.scalar.activation(keep[:, s, 1, :, :], keep[:, s, 1, :, :], ACT.Ln).then_inc(ln_done, 1)

            per_pairs(act, body)

        @block.tensor
        def _(pe):
            pe.wait_ge(consts, 32)
            pe.sem_inc(av_done, 1)

            def body(pp, u, p):
                B, BF = NI * p, FILLS * p
                pe.wait_ge(qk_loaded, 32 * p + 32)
                for f in range(FILLS):
                    if f >= FB:
                        pe.wait_ge(turn_lo, BF + f - FB + 1)
                    for n in range(4):
                        tr = nc.tensor.transpose(Z[:, f % FB, n * P:(n + 1) * P], qk_in[:, f // 4, 4 * (f % 4) + n, :],
                                                 ident[:, :])
                    tr.then_inc(turned, 1)
                pe.wait_ge(turn_lo, BF + FILLS)
                for T in range(-2, NI + 2):
                    i = T + 2
                    if i < NI:
                        br, x0, h = ITEMS[i]
                        dil = DILS[br]
                        if i >= 4:
                            pe.wait_ge(masked, B + i - 3)
                        r = slice(h * DH, (h + 1) * DH)
                        first_mm = True
                        nt, w = len(tiles(i)), blocks(i) * P
                        for n, (x, pos, head) in enumerate(tiles(i)):
                            kpos = pos - dil * P if (w == 2 * P and not head) else pos
                            own = slice(pos, pos + dil * (P - 1) + 1, dil)
                            ks = slice(kpos, kpos + dil * (w - 1) + 1, dil)
                            for c, (qt, kt) in enumerate(((T_hi, T_hi), (T_lo, T_hi), (T_hi, T_lo))):
                                mm = nc.tensor.matmul(Z[:, i % 4, n * w:(n + 1) * w], qt[r, 0, own], kt[r, 1, ks],
                                                      start=first_mm, stop=(c == 2), skip_group_check=True)
                                first_mm = False
                        mm.then_inc(z_done, 1)
                    i = T
                    if 0 <= i < NI:
                        pe.wait_ge(exp_done, B + i + 1)
                        if i >= 2:
                            pe.wait_ge(pt_copied, B + i - 1)
                        for n in range(4):
                            tr = nc.tensor.transpose(ps_T[:, i % 2, n * P:(n + 1) * P], sc[:, i % 4, n * P:(n + 1) * P],
                                                     ident[:, :])
                        tr.then_inc(pt_done, 1)
                    i = T - 2
                    if 0 <= i < NI:
                        br, x0, h = ITEMS[i]
                        s = bslot(u, br)
                        pe.wait_ge(pt_copied, B + i + 1)
                        if i >= 2:
                            pe.wait_ge(o_scaled, B + i - 1)
                        if x0 == 0 and h == 0:
                            pe.wait_ge(v_loaded[s], 16 * slot_dmas(pp, u, br))
                        first_mm = True
                        bl = blocks(i)
                        for n, (x, pos, head) in enumerate(tiles(i)):
                            kt = [x] if bl == 1 else ([x, x + 1] if head else [x - 1, x])
                            for b in range(bl):
                                mm = nc.tensor.matmul(O[:, i % 2, n * DH:(n + 1) * DH],
                                                      pT[:, i % 3, (n * bl + b) * P:(n * bl + b + 1) * P],
                                                      v_br[:, s, kt[b], h * DH:(h + 1) * DH],
                                                      start=first_mm, stop=(b == bl - 1), skip_group_check=True)
                                first_mm = False
                        mm.then_inc(av_done, 1)

            per_pairs(pe, body)


def stick_breaking_sample(nc, t):
    C = H * DEC_S
    GP = 4
    GK = GP * PAGE
    NG = PAGES // GP
    RING = 8
    ctx = ExitStack()
    with ctx:
        m = Mem(nc, ctx, "sbs")
        ident = m.sb("ident", [P, P])
        table = m.sb("table", [1, DEC_B * PAGES], I32)
        bias = m.sb("bias", [C, 1])
        valid = m.sb("valid", [C, DEC_S])
        own = m.sb("own", [C, W])
        pick = m.sb("pick", [C, DEC_S])
        ones = m.sb("ones", [C, DEC_S + GK])
        qk_new = m.sb("qk_new", [NS, 2, W])
        v_new = m.sb("v_new", [DEC_S, DEC_B, W])
        v_now = m.sb("v_now", [DEC_S, W])
        q_pad = m.sb("q_pad", [P, PAIRS * (C + 8)])
        qT = m.sb("qT", [P, PAIRS, NS])
        kT_new = m.sb("kT_new", [P, PAIRS, NS])
        k_ring = m.sb("k_ring", [P, RING, GP, W])
        v_ring = m.sb("v_ring", [P, RING, GP, W])
        kT = m.sb("kT", [P, 2, PAIRS, GK])
        z = m.sb("z", [C, 2, DEC_S + GK])
        sp_ = m.sb("sp", [C, 2, DEC_S + GK])
        S = m.sb("S", [C, 2, DEC_S + GK])
        a = m.sb("a", [C, 2, DEC_S + GK])
        aT = m.sb("aT", [P, 2, (GP + 1) * C])
        o_own = m.sb("o_own", [C, W])
        o_row = m.sb("o_row", [DEC_S, W])
        ps_T = m.ps("ps_T", [P, 2, 512])
        Z = m.ps("Z", [P, 2, 512])
        Z_new = m.ps("Z_new", [P, 512])
        AT = m.ps("AT", [P, 512])
        O = m.ps("O", [P, 512])
        R = m.ps("R", [P, 512])

        consts = m.sem("consts")
        zeroed = m.sem("zeroed")
        q_turned = m.sem("q_turned")
        q_copied = m.sem("q_copied")
        padded = m.sem("padded")
        k_loaded = m.sems("k_loaded", RING)
        v_loaded = m.sems("v_loaded", RING)
        k_turned = m.sem("k_turned")
        kT_even = m.sem("kT_even")
        kT_odd = m.sem("kT_odd")
        scored = m.sem("scored")
        z_done = m.sem("z_done")
        exp_done = m.sem("exp_done")
        cut_done = m.sem("cut_done")
        ln_done = m.sem("ln_done")
        sp_done = m.sem("sp_done")
        S_done = m.sem("S_done")
        arg_done = m.sem("arg_done")
        a_done = m.sem("a_done")
        a_turned = m.sem("a_turned")
        aT_copied = m.sem("aT_copied")
        av_done = m.sem("av_done")
        sp_fresh = m.sem("sp_fresh")
        arg_fresh = m.sem("arg_fresh")
        a_fresh = m.sem("a_fresh")
        v_set = m.sem("v_set")
        o_masked = m.sem("o_masked")
        picked = m.sem("picked")
        row_copied = m.sem("row_copied")
        stored = m.sem("stored")

        NCONST = 8 + H

        def is0(b):
            return isinstance(b, int) and b == 0

        def back(b, g, lag):
            if g >= lag:
                return b, g - lag
            return None if is0(b) else (b - 1, NG + g - lag)

        def at(b, g):
            return NG * b + g

        def early(b, g, n):
            return is0(b) and g < n

        def run(eng, step):
            for g in range(NG):
                step(0, g)
            with eng.Fori(1, DEC_B) as b:
                for g in range(NG):
                    step(b, g)
            step(DEC_B, 0)
            step(DEC_B, 1)

        def over(b):
            return isinstance(b, int) and b == DEC_B

        block = ctx.enter_context(nc.Block())

        def load_pages(eng, pages, ring, loaded, used, per_group, then):
            cache = pages[0].rearrange("n s h d -> n s (h d)")

            def body(b):
                for g in range(NG):
                    if not early(b, g, RING):
                        hold(eng, used, per_group * (at(b, g) - RING + 1))
                    for i in range(GP):
                        r = GP * g + i
                        n = eng.value_load(table[0:1, bass.ds(PAGES * b + PAGES - 1 - r, 1)], min_val=0,
                                           max_val=pages.shape[1] - 1)
                        eng.dma_start(ring[:, g % RING, i, :], cache[bass.ds(n, 1), :, :].rearrange("a s c -> (a s) c")) \
                            .then_inc(loaded[g % RING], 16)
                    if g == NG - 4 and not is0(b):
                        then(b - 1)
            body(0)
            with eng.Fori(1, DEC_B) as b:
                body(b)

        @block.sync
        def _(sp):
            sp.dma_start(table[:, :], t["page_table"].rearrange("b n -> (b n)").rearrange("(a n) -> a n", a=1)) \
                .then_inc(consts, 16)
            for buf, n in ((ident, "ident"), (valid, "valid_new"), (own, "own_head"), (pick, "pick")):
                sp.dma_start(buf[:, :], t[n][:, :]).then_inc(consts, 16)
            for i, src in enumerate((t["q_sb_s"], flat(t["k_sb_s"]))):
                sp.dma_start(qk_new[:, i, :], src).then_inc(consts, 16)
            sp.dma_start(v_new[:, :, :], flat(t["v_sb_s"]).rearrange("(b s) c -> s b c", s=DEC_S)).then_inc(consts, 16)
            for h in range(H):
                sp.dma_start(bias[h * DEC_S:(h + 1) * DEC_S, :], t["sb_bias"][0:1, h:h + 1].to_broadcast([DEC_S, 1])) \
                    .then_inc(consts, 16)
            sp.wait_ge(consts, 16 * NCONST)

            def store(b):
                hold(sp, row_copied, b + 1)
                sp.dma_start(t["o_sb_s"][bass.ds(b * DEC_S, DEC_S), :], o_row[:, :]).then_inc(stored, 16)

            load_pages(sp, t["cache_k_sb"], k_ring, k_loaded, k_turned, GP, store)
            store(DEC_B - 1)
            sp.wait_ge(stored, 16 * DEC_B)

        @block.gpsimd
        def _(pool):
            pool.wait_ge(consts, 16 * NCONST)
            load_pages(pool, t["cache_v_sb"], v_ring, v_loaded, av_done, 1, lambda b: None)

        @block.vector
        def _(dve):
            nc.vector.memset(q_pad[:, :], 0.0).then_inc(zeroed, 1)
            nc.vector.memset(ones[:, :], 1.0).then_inc(zeroed, 1)
            dve.wait_ge(consts, 16 * NCONST)
            dve.wait_ge(q_turned, 1)
            nc.vector.tensor_copy(qT[:, :, :], ps_T[:, 0, 0:PAIRS * NS].rearrange("p (a n) -> p a n", n=NS)).then_inc(q_copied, 1)
            nc.vector.tensor_copy(kT_new[:, :, :], ps_T[:, 1, 0:PAIRS * NS].rearrange("p (a n) -> p a n", n=NS)) \
                .then_inc(q_copied, 1)
            dve.wait_ge(zeroed, 2)
            dve.wait_ge(q_copied, 2)

            def copy_page(b, g, i):
                dve.wait_ge(k_turned, GP * at(b, g) + i + 1)
                if not early(b, g, 2):
                    dve.wait_ge(scored, at(b, g) - 1)
                nc.vector.tensor_copy(kT[:, g % 2, :, (GP - 1 - i) * PAGE:(GP - i) * PAGE],
                                      ps_T[:, 1, :].rearrange("p (a n) -> p a n", a=PAIRS)).then_inc(kT_odd, 1)

            def step(b, g):
                s, now = g % 2, not over(b)
                if g == 0 and now:
                    if not is0(b):
                        dve.wait_ge(scored, at(b, 0))
                    for h in range(2):
                        r = slice(h * DH, (h + 1) * DH)
                        dst = q_pad[r, :].rearrange("p (a x) -> p a x", a=PAIRS)[:, :, h * DEC_S:(h + 1) * DEC_S]
                        pd = nc.vector.tensor_copy(dst, qT[r, :, bass.ds(b * DEC_S, DEC_S)])
                    pd.then_inc(padded, 1)
                one = back(b, g, 1)
                if one and not (over(b) and g > 0):
                    B, G = one
                    n, s = at(B, G), G % 2
                    c = 0 if G == 0 else DEC_S
                    cols = slice(c, DEC_S + GK)
                    dve.wait_ge(scored, n + 1)
                    if not early(B, G, 2):
                        dve.wait_ge(arg_done, n - 1)
                    if G == 0:
                        nc.vector.tensor_scalar(z[:, s, 0:DEC_S], Z_new[0:C, 0:DEC_S][:, ::-1], bias[:, 0:1], None, ALU.add)
                    nc.vector.tensor_scalar(z[:, s, DEC_S:DEC_S + GK], Z[0:C, s, :][:, ::-1], bias[:, 0:1], None, ALU.add) \
                        .then_inc(z_done, 1)
                    dve.wait_ge(exp_done, n + 1)
                    nc.vector.tensor_scalar(sp_[:, s, cols], sp_[:, s, cols], BIG, None, ALU.min).then_inc(cut_done, 1)
                if now:
                    copy_page(b, g, 1)
                if one and not (over(b) and g > 0):
                    dve.wait_ge(ln_done, n + 1)
                    nc.vector.tensor_tensor(sp_[:, s, cols], sp_[:, s, cols], z[:, s, cols], ALU.max).then_inc(sp_done, 1)
                    dve.wait_ge(sp_done, n + 1)
                    if G == 0:
                        nc.vector.tensor_tensor(sp_[:, s, 0:DEC_S], sp_[:, s, 0:DEC_S], valid[:, ::-1], ALU.mult) \
                            .then_inc(sp_fresh, 1)
                        dve.wait_ge(sp_fresh, B + 1)
                    if not early(B, G, 1):
                        dve.wait_ge(S_done, n)
                        dve.wait_ge(arg_done, n)
                    nc.vector.tensor_tensor_scan(S[:, s, cols], ones[:, cols], sp_[:, s, cols],
                                                 0.0 if G == 0 else S[:, 1 - s, DEC_S + GK - 1:DEC_S + GK], ALU.mult,
                                                 ALU.add).then_inc(S_done, 1)
                    dve.wait_ge(S_done, n + 1)
                    if not early(B, G, 2):
                        dve.wait_ge(a_turned, n - 1)
                    if G == 0:
                        nc.vector.tensor_tensor(a[:, s, 0:DEC_S], z[:, s, 0:DEC_S][:, ::-1], S[:, s, 0:DEC_S][:, ::-1],
                                                ALU.subtract).then_inc(arg_fresh, 1)
                        dve.wait_ge(arg_fresh, 2 * B + 1)
                        nc.vector.tensor_scalar(a[:, s, 0:DEC_S], a[:, s, 0:DEC_S], 0.0, None, ALU.min).then_inc(arg_fresh, 1)
                    keys = slice(DEC_S, DEC_S + GK)
                    nc.vector.tensor_tensor(a[:, s, keys], z[:, s, keys][:, ::-1], S[:, s, keys][:, ::-1], ALU.subtract) \
                        .then_inc(arg_done, 1)
                    if G == 0:
                        dve.wait_ge(a_done, n + 1)
                        nc.vector.tensor_tensor(a[:, s, 0:DEC_S], a[:, s, 0:DEC_S], valid[:, :], ALU.mult).then_inc(a_fresh, 1)
                if now:
                    copy_page(b, g, 3)
                if g == 1 and not is0(b):
                    dve.wait_ge(av_done, at(b, 0))
                    if not (isinstance(b, int) and b == 1):
                        dve.wait_ge(picked, b - 1)
                    nc.vector.tensor_tensor(o_own[:, :], O[0:C, :], own[:, :], ALU.mult).then_inc(o_masked, 1)

            run(dve, step)

        @block.scalar
        def _(act):
            load_exp_ln_table(nc, act)
            act.wait_ge(consts, 16 * NCONST)

            def copy_page(b, g, i):
                act.wait_ge(k_turned, GP * at(b, g) + i + 1)
                if not early(b, g, 2):
                    act.wait_ge(scored, at(b, g) - 1)
                nc.scalar.activation(kT[:, g % 2, :, (GP - 1 - i) * PAGE:(GP - i) * PAGE],
                                     ps_T[:, 0, :].rearrange("p (a n) -> p a n", a=PAIRS), ACT.Copy).then_inc(kT_even, 1)

            def step(b, g):
                now, one, two = not over(b), back(b, g, 1), back(b, g, 2)
                if two:
                    B, G = two
                    act.wait_ge(a_turned, at(B, G) + 1)
                    if not early(B, G, 2):
                        act.wait_ge(av_done, at(B, G) - 1)
                    if G == 0:
                        nc.scalar.activation(aT[0:DEC_S, G % 2, GP * C:(GP + 1) * C], AT[0:DEC_S, GP * C:(GP + 1) * C], ACT.Copy)
                    nc.scalar.activation(aT[:, G % 2, 0:GP * C], AT[:, 0:GP * C], ACT.Copy).then_inc(aT_copied, 1)
                if one and not (over(b) and g > 0):
                    B, G = one
                    n, s = at(B, G), G % 2
                    cols = slice(0 if G == 0 else DEC_S, DEC_S + GK)
                    act.wait_ge(z_done, n + 1)
                    if not early(B, G, 2):
                        act.wait_ge(S_done, n - 1)
                    nc.scalar.activation(sp_[:, s, cols], z[:, s, cols], ACT.Exp).then_inc(exp_done, 1)
                if now:
                    copy_page(b, g, 0)
                if one and not (over(b) and g > 0):
                    act.wait_ge(cut_done, n + 1)
                    nc.scalar.activation(sp_[:, s, cols], sp_[:, s, cols], ACT.Ln, bias=1.0).then_inc(ln_done, 1)
                if now:
                    copy_page(b, g, 2)
                if one and not (over(b) and g > 0):
                    act.wait_ge(arg_done, n + 1)
                    if G == 0:
                        act.wait_ge(arg_fresh, 2 * B + 2)
                    nc.scalar.activation(a[:, s, cols], a[:, s, cols], ACT.Exp).then_inc(a_done, 1)
                if g == 0 and now:
                    if not is0(b):
                        act.wait_ge(av_done, at(b - 1, 1))
                    nc.scalar.activation(v_now[:, :], v_new[:, bass.ds(b, 1), :].rearrange("p a c -> p (a c)"), ACT.Copy) \
                        .then_inc(v_set, 1)
                if g == 2 and not is0(b):
                    copy_rows(b)

            def copy_rows(b):
                act.wait_ge(picked, b)
                if not (isinstance(b, int) and b == 1):
                    act.wait_ge(stored, 16 * b - 16)
                nc.scalar.activation(o_row[:, :], R[0:DEC_S, :], ACT.Copy).then_inc(row_copied, 1)

            run(act, step)
            copy_rows(DEC_B)

        @block.tensor
        def _(pe):
            pe.wait_ge(consts, 16 * NCONST)
            for i in range(2):
                for pr in range(PAIRS):
                    tr = nc.tensor.transpose(ps_T[:, i, pr * NS:(pr + 1) * NS], qk_new[:, i, pr * P:(pr + 1) * P],
                                             ident[0:NS, 0:NS])
            tr.then_inc(q_turned, 1)
            pe.wait_ge(q_copied, 2)

            def turn_weights(B, G):
                n, s = at(B, G), G % 2
                pe.wait_ge(a_done, n + 1)
                if G == 0:
                    pe.wait_ge(a_fresh, B + 1)
                if not early(B, G, 1):
                    hold(pe, aT_copied, n)
                if G == 0:
                    nc.tensor.transpose(AT[0:DEC_S, GP * C:(GP + 1) * C], a[:, s, 0:DEC_S], ident[0:C, 0:C])
                for i in range(GP):
                    c = DEC_S + (GP - 1 - i) * PAGE
                    tr = nc.tensor.transpose(AT[:, i * C:(i + 1) * C], a[:, s, c:c + PAGE], ident[0:C, 0:C])
                tr.then_inc(a_turned, 1)

            def turn_page(b, g, i):
                if i == 0:
                    pe.wait_ge(k_loaded[g % RING], 16 * GP * ((NG // RING) * b + g // RING + 1))
                if not (early(b, g, 1) and i < 2):
                    pe.wait_ge(kT_odd if i % 2 else kT_even, 2 * at(b, g) + i // 2)
                for pr in range(PAIRS):
                    tr = nc.tensor.transpose(ps_T[:, i % 2, pr * P:(pr + 1) * P], k_ring[:, g % RING, i, pr * P:(pr + 1) * P],
                                             ident[:, :])
                tr.then_inc(k_turned, 1)

            def weigh(B, G, i):
                n, s = at(B, G), G % 2
                if i == 0:
                    pe.wait_ge(v_loaded[G % RING], 16 * GP * ((NG // RING) * B + G // RING + 1))
                    if G == 0:
                        if not is0(B):
                            hold(pe, o_masked, B)
                        hold(pe, aT_copied, n + 1)
                        hold(pe, v_set, B + 1)
                        nc.tensor.matmul(O[0:C, :], aT[0:DEC_S, s, GP * C:(GP + 1) * C], v_now[:, :], start=True, stop=False)
                    pe.wait_ge(aT_copied, n + 1)
                mm = nc.tensor.matmul(O[0:C, :], aT[:, s, i * C:(i + 1) * C], v_ring[:, G % RING, i, :], start=False,
                                      stop=(G == NG - 1 and i == GP - 1))
                if i == GP - 1:
                    mm.then_inc(av_done, 1)

            def score(b, g):
                if not early(b, g, 2):
                    pe.wait_ge(z_done, at(b, g) - 1)
                pe.wait_ge(kT_even, 2 * at(b, g) + 2)
                pe.wait_ge(kT_odd, 2 * at(b, g) + 2)
                if g == 0:
                    pe.wait_ge(padded, b + 1)
                    for pr in range(PAIRS):
                        nc.tensor.matmul(Z_new[0:C, 0:DEC_S], q_pad[:, pr * C:(pr + 1) * C],
                                         kT_new[:, pr, bass.ds(b * DEC_S, DEC_S)], start=(pr == 0), stop=(pr == PAIRS - 1))
                for pr in range(PAIRS):
                    mm = nc.tensor.matmul(Z[0:C, g % 2, :], q_pad[:, pr * C:(pr + 1) * C], kT[:, g % 2, pr, :],
                                          start=(pr == 0), stop=(pr == PAIRS - 1))
                mm.then_inc(scored, 1)

            def pick_rows(b):
                hold(pe, o_masked, b)
                if not (isinstance(b, int) and b == 1):
                    hold(pe, row_copied, b - 1)
                nc.tensor.matmul(R[0:DEC_S, :], pick[:, :], o_own[:, :], start=True, stop=True).then_inc(picked, 1)

            def step(b, g):
                now, two = not over(b), back(b, g, 2)
                if two:
                    turn_weights(*two)
                for i in range(GP):
                    if now:
                        turn_page(b, g, i)
                    if two:
                        weigh(*two, i)
                if now:
                    score(b, g)
                if g == 2 and not is0(b):
                    pick_rows(b)

            run(pe, step)
            pick_rows(DEC_B)


def dilated_sample(nc, t):
    C = H * DEC_S
    NA = 512 // P
    NT = NA + DEC_S
    KEYS = 2 * 512 + DEC_S
    ctx = ExitStack()
    with ctx:
        m = Mem(nc, ctx, "dls")
        ident = m.sb("ident", [P, P])
        mask = m.sb("mask", [C, KEYS])
        count = m.sb("count", [C, KEYS])
        own = m.sb("own", [C, W])
        pick = m.sb("pick", [C, DEC_S])
        qk_new = m.sb("qk_new", [NS, 2, W])
        q_pad = m.sb("q_pad", [P, 2, PAIRS * (C + 8)])
        qT = m.sb("qT", [P, PAIRS, NS])
        kT_new = m.sb("kT_new", [P, PAIRS, NS])
        k_in = m.sb("k_in", [P, 2, NT, W])
        v_in = m.sb("v_in", [P, 2, NT, W])
        v_new = m.sb("v_new", [DEC_S, 2, W])
        kT = m.sb("kT", [P, PAIRS, NT * P])
        s = m.sb("s", [C, 2, KEYS])
        stat = m.sb("stat", [C, 2, 4])
        pT = m.sb("pT", [P, 2, NT + 1, C])
        o_own = m.sb("o_own", [C, 2, W])
        o_row = m.sb("o_row", [DEC_S, 2, W])
        ps_T = m.ps("ps_T", [P, 2, 512])
        Sc = m.ps("Sc", [P, 3, 512])
        O = m.ps("O", [P, 2, 512])
        R = m.ps("R", [P, 512])

        consts = m.sem("consts")
        zeroed = m.sem("zeroed")
        q_turned = m.sem("q_turned")
        q_copied = m.sem("q_copied")
        k_loaded = m.sems("k_loaded", 2)
        v_loaded = m.sems("v_loaded", 2)
        padded = m.sem("padded")
        turned = m.sem("turned")
        copied = m.sems("copied", 2)
        scored = m.sem("scored")
        masked = m.sem("masked")
        max_done = m.sem("max_done")
        exp_done = m.sem("exp_done")
        counted = m.sem("counted")
        summed = m.sem("summed")
        inv_done = m.sem("inv_done")
        p_turned = m.sem("p_turned")
        p_copied = m.sem("p_copied")
        av_done = m.sem("av_done")
        o_masked = m.sem("o_masked")
        picked = m.sem("picked")
        row_copied = m.sem("row_copied")
        stored = m.sems("stored", 2)

        def entries(eng, scores, output):
            scores(0, 0, 0)
            scores(1, 1, 0)
            output(0, 0, 0)
            with eng.Fori(1, DEC_B // 2) as o:
                scores(2 * o, 0, o)
                output(2 * o - 1, 1, o - 1)
                scores(2 * o + 1, 1, o)
                output(2 * o, 0, o)
            output(DEC_B - 1, 1, DEC_B // 2 - 1)

        def early(b, n):
            return isinstance(b, int) and b < n

        k_c, v_c = (t[n][0].rearrange("b s h d -> b s (h d)") for n in ("cache_k_win", "cache_v_win"))
        k_new, v_new_d = (t[n][0].rearrange("b s h d -> b s (h d)")[:, WIN - DEC_S:WIN, :] for n in ("k_win_s", "v_win_s"))
        block = ctx.enter_context(nc.Block())

        @block.sync
        def _(sp):
            sp.dma_start(ident[:, :], t["ident"][:, :]).then_inc(consts, 16)
            for buf, n in ((mask, "win_mask"), (count, "win_count"), (own, "own_head"), (pick, "pick")):
                sp.dma_start(buf[:, :], t[n][:, :]).then_inc(consts, 16)
            sp.dma_start(qk_new[:, 0, :], t["q_dl_s"]).then_inc(consts, 16)
            sp.dma_start(qk_new[:, 1, :], k_new).then_inc(consts, 16)

            def rows(src, b):
                return src[bass.ds(b, 1), :, :].rearrange("a s c -> (a s) c")

            def load(b, slot, use):
                if not early(b, 2):
                    hold(sp, turned, NT * (b - 2) + NT)
                for buf, src, sem in ((k_in, k_c, k_loaded), (v_in, v_c, v_loaded)):
                    if buf is v_in and not early(b, 2):
                        hold(sp, av_done, b - 1)
                    sp.dma_start(buf[:, slot, 0:NA, :], rows(src, b)[WIN - 512:WIN, :].rearrange("(n p) c -> p n c", p=P)) \
                        .then_inc(sem[slot], 16)
                    sp.dma_start(buf[:, slot, NA:NT, :], rows(src, b).rearrange("(p r) c -> p r c", r=16)[:, 0:DEC_S, :]) \
                        .then_inc(sem[slot], 16)
                sp.dma_start(v_new[:, slot, :], rows(v_new_d, b)).then_inc(v_loaded[slot], 16)

            def store(b, slot, use):
                hold(sp, row_copied, b + 1)
                sp.dma_start(t["o_dl_s"][bass.ds(b * DEC_S, DEC_S), :], o_row[:, slot, :]).then_inc(stored[slot], 16)

            entries(sp, load, store)
            for slot in range(2):
                sp.wait_ge(stored[slot], 16 * (DEC_B // 2))

        @block.vector
        def _(dve):
            nc.vector.memset(q_pad[:, :, :], 0.0).then_inc(zeroed, 1)
            dve.wait_ge(consts, 16 * 7)
            dve.wait_ge(q_turned, 1)
            nc.vector.tensor_copy(qT[:, :, :], ps_T[:, 0, 0:PAIRS * NS].rearrange("p (a n) -> p a n", n=NS)).then_inc(q_copied, 1)
            nc.vector.tensor_copy(kT_new[:, :, :], ps_T[:, 1, 0:PAIRS * NS].rearrange("p (a n) -> p a n", n=NS)) \
                .then_inc(q_copied, 1)
            dve.wait_ge(zeroed, 1)
            dve.wait_ge(q_copied, 2)

            def scores(b, slot, use):
                if not early(b, 2):
                    dve.wait_ge(scored, b - 1)
                for h in range(2):
                    r = slice(h * DH, (h + 1) * DH)
                    dst = q_pad[r, slot, :].rearrange("p (a x) -> p a x", a=PAIRS)[:, :, h * DEC_S:(h + 1) * DEC_S]
                    pd = nc.vector.tensor_copy(dst, qT[r, :, bass.ds(b * DEC_S, DEC_S)])
                pd.then_inc(padded, 1)
                for x in range(1, NT, 2):
                    dve.wait_ge(turned, NT * b + x + 1)
                    if not early(b, 1):
                        dve.wait_ge(scored, b)
                    nc.vector.tensor_copy(kT[:, :, x * P:(x + 1) * P], ps_T[:, 1, :].rearrange("p (a n) -> p a n", a=PAIRS)) \
                        .then_inc(copied[1], 1)
                dve.wait_ge(scored, b + 1)
                if not early(b, 2):
                    dve.wait_ge(p_turned, b - 1)
                for x in range(2):
                    cols = slice(x * 512, (x + 1) * 512)
                    nc.vector.tensor_tensor(s[:, slot, cols], Sc[0:C, x, :], mask[:, cols], ALU.add)
                nc.vector.tensor_tensor(s[:, slot, 1024:KEYS], Sc[0:C, 2, 0:DEC_S], mask[:, 1024:KEYS], ALU.add).then_inc(masked, 1)
                dve.wait_ge(masked, b + 1)
                nc.vector.tensor_reduce(stat[:, slot, 0:1], s[:, slot, :], AX.X, ALU.max, negate=True).then_inc(max_done, 1)
                dve.wait_ge(exp_done, b + 1)
                nc.vector.tensor_tensor(s[:, slot, :], s[:, slot, :], count[:, :], ALU.mult).then_inc(counted, 1)
                dve.wait_ge(counted, b + 1)
                nc.vector.tensor_reduce(stat[:, slot, 1:2], s[:, slot, :], AX.X, ALU.add).then_inc(summed, 1)
                dve.wait_ge(summed, b + 1)
                nc.vector.reciprocal(stat[:, slot, 2:3], stat[:, slot, 1:2]).then_inc(inv_done, 1)

            def output(b, slot, use):
                dve.wait_ge(av_done, b + 1)
                dve.wait_ge(inv_done, b + 1)
                if not early(b, 2):
                    dve.wait_ge(picked, b - 1)
                nc.vector.scalar_tensor_tensor(out=o_own[:, slot, :], in0=O[0:C, slot, :], scalar=stat[:, slot, 2:3],
                                               in1=own[:, :], op0=ALU.mult, op1=ALU.mult).then_inc(o_masked, 1)

            entries(dve, scores, output)

        @block.scalar
        def _(act):
            load_exp_ln_table(nc, act)

            def scores(b, slot, use):
                for x in range(0, NT, 2):
                    act.wait_ge(turned, NT * b + x + 1)
                    if not early(b, 1):
                        act.wait_ge(scored, b)
                    nc.scalar.activation(kT[:, :, x * P:(x + 1) * P], ps_T[:, 0, :].rearrange("p (a n) -> p a n", a=PAIRS),
                                         ACT.Copy).then_inc(copied[0], 1)
                act.wait_ge(max_done, b + 1)
                nc.scalar.activation(s[:, slot, :], s[:, slot, :], ACT.Exp, bias=stat[:, slot, 0:1]).then_inc(exp_done, 1)

            def output(b, slot, use):
                act.wait_ge(p_turned, b + 1)
                nc.scalar.activation(pT[:, slot, 0:NT, :], ps_T[:, 0, 0:NT * C].rearrange("p (n c) -> p n c", c=C), ACT.Copy)
                nc.scalar.activation(pT[0:DEC_S, slot, NT, :], ps_T[0:DEC_S, 1, 0:C], ACT.Copy).then_inc(p_copied, 1)
                act.wait_ge(picked, b + 1)
                if not early(b, 2):
                    act.wait_ge(stored[slot], 16 * use)
                nc.scalar.activation(o_row[:, slot, :], R[0:DEC_S, :], ACT.Copy).then_inc(row_copied, 1)

            entries(act, scores, output)

        @block.tensor
        def _(pe):
            pe.wait_ge(consts, 16 * 7)
            for i in range(2):
                for pr in range(PAIRS):
                    tr = nc.tensor.transpose(ps_T[:, i, pr * NS:(pr + 1) * NS], qk_new[:, i, pr * P:(pr + 1) * P],
                                             ident[0:NS, 0:NS])
            tr.then_inc(q_turned, 1)
            pe.wait_ge(q_copied, 2)

            def scores(b, slot, use):
                pe.wait_ge(k_loaded[slot], 32 * use + 32)
                if not early(b, 2):
                    pe.wait_ge(p_copied, b - 1)
                for x in range(NT):
                    if not (early(b, 1) and x < 2):
                        pe.wait_ge(copied[x % 2], (NT // 2) * b + x // 2)
                    for pr in range(PAIRS):
                        tr = nc.tensor.transpose(ps_T[:, x % 2, pr * P:(pr + 1) * P], k_in[:, slot, x, pr * P:(pr + 1) * P],
                                                 ident[:, :])
                    tr.then_inc(turned, 1)
                for x in range(2):
                    pe.wait_ge(copied[x], (NT // 2) * b + NT // 2)
                pe.wait_ge(padded, b + 1)
                if not early(b, 1):
                    pe.wait_ge(masked, b)
                for x in range(2):
                    for pr in range(PAIRS):
                        nc.tensor.matmul(Sc[0:C, x, :], q_pad[:, slot, pr * C:(pr + 1) * C], kT[:, pr, x * 512:(x + 1) * 512],
                                         start=(pr == 0), stop=(pr == PAIRS - 1))
                for pr in range(PAIRS):
                    mm = nc.tensor.matmul(Sc[0:C, 2, 0:DEC_S], q_pad[:, slot, pr * C:(pr + 1) * C],
                                          kT_new[:, pr, bass.ds(b * DEC_S, DEC_S)], start=(pr == 0), stop=(pr == PAIRS - 1))
                mm.then_inc(scored, 1)

            def output(b, slot, use):
                hold(pe, summed, b + 1)
                for x in range(NT):
                    nc.tensor.transpose(ps_T[:, 0, x * C:(x + 1) * C], s[:, slot, x * P:(x + 1) * P], ident[0:C, 0:C])
                nc.tensor.transpose(ps_T[0:DEC_S, 1, 0:C], s[:, slot, 1024:KEYS], ident[0:C, 0:C]).then_inc(p_turned, 1)
                hold(pe, v_loaded[slot], 48 * use + 48)
                hold(pe, p_copied, b + 1)
                if not early(b, 2):
                    hold(pe, o_masked, b - 1)
                nc.tensor.matmul(O[0:C, slot, :], pT[0:DEC_S, slot, NT, :], v_new[:, slot, :], start=True, stop=False)
                for x in range(NT):
                    mm = nc.tensor.matmul(O[0:C, slot, :], pT[:, slot, x, :], v_in[:, slot, x, :], start=False,
                                          stop=(x == NT - 1))
                mm.then_inc(av_done, 1)
                hold(pe, o_masked, b + 1)
                if not early(b, 1):
                    hold(pe, row_copied, b)
                nc.tensor.matmul(R[0:DEC_S, :], pick[:, :], o_own[:, slot, :], start=True, stop=True).then_inc(picked, 1)

            entries(pe, scores, output)


def merge(nc, t):
    PC = PLE // P
    ctx = ExitStack()
    with ctx:
        m = Mem(nc, ctx, "merge")
        wo_hi, wo_lo = (m.sb(f"wo_{x}", [P, KC, D], F32R) for x in ("hi", "lo"))
        wg_hi, wg_lo = (m.sb(f"wg_{x}", [P, KC, D], F32R) for x in ("hi", "lo"))
        wp_hi, wp_lo = (m.sb(f"wp_{x}", [P, PC, D], F32R) for x in ("hi", "lo"))
        yT_hi, yT_lo = (m.sb(f"yT_{x}", [P, KC, P], F32R) for x in ("hi", "lo"))
        xT_hi, xT_lo = (m.sb(f"xT_{x}", [P, KC, P], F32R) for x in ("hi", "lo"))
        pT_hi, pT_lo = (m.sb(f"pT_{x}", [P, PC, P], F32R) for x in ("hi", "lo"))
        x = m.sb("x", [P, 2, D])
        work = m.sb("work", [P, 2, D])
        z = m.sb("z", [P, D])
        o = m.sb("o", [P, 4, W])
        lse = m.sb("lse", [P, 3, H])
        top = m.sb("top", [P, H])
        share = m.sb("share", [P, 3, H])
        total = m.sb("total", [P, H])
        p_in = m.sb("p_in", [P, PLE])
        junk = m.sb("junk", [P, W])
        stat = m.sb("stat", [P, 3, 2])
        mhalf = m.sb("mhalf", [P, 2])
        g_out = m.sb("g_out", [P, KC])
        ident = m.sb("ident", [P, P])
        T = m.ps("T", [P, 2, 512])
        Out = m.ps("Out", [P, 2, 512])
        Gate = m.ps("Gate", [P, 2, 512])
        Ple = m.ps("Ple", [P, 2, 512])

        consts = m.sem("consts")
        mhalf_set = m.sem("mhalf_set")
        w_loaded = m.sems("w_loaded", 2)
        w_hi_done = m.sem("w_hi_done")
        w_split = m.sem("w_split")
        in_loaded = m.sem("in_loaded")
        x_loaded = m.sems("x_loaded", 2)
        p_loaded = m.sem("p_loaded")
        share_step = m.sem("share_step")
        share_exp = m.sem("share_exp")
        z_exp = m.sem("z_exp")
        silu_step = m.sem("silu_step")
        squared = m.sem("squared")
        mean_done = m.sem("mean_done")
        rms_done = m.sem("rms_done")
        y_done = m.sem("y_done")
        y_turned, y_hi, y_split = m.sem("y_turned"), m.sem("y_hi"), m.sem("y_split")
        x1_turned, x1_hi, x1_split = m.sem("x1_turned"), m.sem("x1_hi"), m.sem("x1_split")
        p_turned, p_hi, p_split = m.sem("p_turned"), m.sem("p_hi"), m.sem("p_split")
        out_done = m.sem("out_done")
        x1_done = m.sem("x1_done")
        gate_done = m.sem("gate_done")
        gate_exp = m.sem("gate_exp")
        ple_done = m.sem("ple_done")
        final_step = m.sem("final_step")
        stored = m.sem("stored")

        SH, FS = 10, 4

        def rows_of(item):
            return NS if first(item) else P

        def before(item, slot, use):
            return item - 1, 1 - slot, use - (1 - slot)

        def pipeline(eng, enter, body, leave):
            enter()
            steps(eng, body)
            leave()

        sets = [(t["w_out"][0], wo_hi, wo_lo, k) for k in range(KC)] \
            + [(t["w_ple"][0], wp_hi, wp_lo, k) for k in range(PC)] \
            + [(t["w_ple_gate"][0], wg_hi, wg_lo, k) for k in range(KC)]
        NW = len(sets)
        x_s, p_s = t["x_sample"].rearrange("b s d -> (b s) d"), t["p_sample"][0].rearrange("b s d -> (b s) d")
        y_s = t["y_sample"].rearrange("b s d -> (b s) d")
        block = ctx.enter_context(nc.Block())

        @block.sync
        def _(sp):
            sp.dma_start(ident[:, :], t["ident"][:, :]).then_inc(consts, 16)
            with nc.allow_non_contiguous_dma(reason="the 1024 weights of the norms, once"):
                for i, n in enumerate(("out_norm_sb", "out_norm_dil")):
                    sp.dma_start(g_out[:, 4 * i:4 * i + 4], t[n][0].rearrange("(c p) -> p c", p=P)).then_inc(consts, 16)

            def load_in(item):
                n = rows_of(item)
                rows = slice(0, NS) if first(item) else bass.ts(item - 1, P)
                if first(item):
                    srcs = [t["o_sb_s"]] + [t["o_dl_s"]] * 3
                    zs, ls = [t["z_sb_s"], t["z_dl_s"]], t["lse_one"].rearrange("n (b h) -> n b h", h=H)
                else:
                    srcs = [t["o_sb"][rows, :]] + [t["o_dil"][br][rows, :] for br in range(3)]
                    zs = [t["z_sb"][rows, :], t["z_dl"][rows, :]]
                    ls = t["lse_dil"][:, rows, :].rearrange("b n h -> n b h")
                sp.dma_start(lse[0:n], ls).then_inc(in_loaded, 16)
                for i, src in enumerate(zs):
                    sp.dma_start(z[0:n, i * W:(i + 1) * W], src).then_inc(in_loaded, 16)
                for i, src in enumerate(srcs):
                    sp.dma_start(o[0:n, i, :], src).then_inc(in_loaded, 16)

            def load_x(item, slot):
                n = rows_of(item)
                sp.dma_start(x[0:n, slot, :], x_s if first(item) else t["x_prompt"][0][bass.ts(item - 1, P), :]) \
                    .then_inc(x_loaded[slot], 16)

            def load_p(item):
                n = rows_of(item)
                sp.dma_start(p_in[0:n, :], p_s if first(item) else t["p_prompt"][0, 0][bass.ts(item - 1, P), :]) \
                    .then_inc(p_loaded, 16)

            def store(item):
                n = rows_of(item)
                hold(sp, final_step, FS * item + FS)
                dst = y_s if first(item) else t["y_prompt"][0][bass.ts(item - 1, P), :]
                sp.dma_start(dst, work[0:n, 1, :]).then_inc(stored, 16)

            def enter():
                for c, (src, hi, lo, k) in enumerate(sets):
                    if c >= 2:
                        sp.wait_ge(w_split, c - 1)
                    sp.dma_start(work[:, c % 2, :], src[k * P:(k + 1) * P, :]).then_inc(w_loaded[c % 2], 16)
                    if c == 1:
                        load_in(0)
                        load_x(0, 0)
                        load_p(0)
                hold(sp, y_done, 2)
                load_in(1)

            def body(item, slot, use):
                if not last(item):
                    if not (isinstance(item, int) and item == 0):
                        hold(sp, final_step, FS * item)
                    load_x(item + 1, 1 - slot)
                if not (isinstance(item, int) and item >= TILES - 1):
                    hold(sp, y_done, 2 * item + 4)
                    load_in(item + 2)
                if not first(item):
                    hold(sp, p_turned, item)
                    load_p(item)
                    store(item - 1)

            pipeline(sp, enter, body, lambda: store(TILES))
            sp.wait_ge(stored, 16 * (TILES + 1))

        @block.gpsimd
        def _(pool):
            nc.gpsimd.memset(mhalf[:, :], -0.5).then_inc(mhalf_set, 1)
            hold(pool, mhalf_set, 1)

            def rms(item):
                n = rows_of(item)
                hold(pool, squared, 2 * item + 2)
                if not first(item):
                    hold(pool, y_done, 2 * item)
                nc.gpsimd.tensor_scalar(stat[0:n, 1, :], stat[0:n, 0, :], 1.0 / W, EPS, ALU.mult, ALU.add) \
                    .then_inc(mean_done, 1)
                hold(pool, mean_done, item + 1)
                nc.gpsimd.tensor_tensor(stat[0:n, 2, :], stat[0:n, 1, :], mhalf[0:n, :], ALU.pow).then_inc(rms_done, 1)

            def body(item, slot, use):
                if not last(item):
                    rms(item + 1)

            rms(0)
            steps(pool, body)

        @block.vector
        def _(dve):
            def enter():
                for c, (src, hi, lo, k) in enumerate(sets):
                    dve.wait_ge(w_hi_done, c + 1)
                    if c < KC:
                        nc.vector.scalar_tensor_tensor(out=lo[:, k, :], in0=work[:, c % 2, :], scalar=g_out[:, k:k + 1],
                                                       in1=hi[:, k, :].bitcast(F32), op0=ALU.mult, op1=ALU.subtract) \
                            .then_inc(w_split, 1)
                    else:
                        nc.vector.tensor_tensor(lo[:, k, :], work[:, c % 2, :], hi[:, k, :].bitcast(F32), ALU.subtract) \
                            .then_inc(w_split, 1)
                prepare(0)
                low(0, "y")

            def prepare(item):
                n = rows_of(item)
                s = SH * item
                dve.wait_ge(in_loaded, 16 * 7 * item + 16 * 7)
                nc.vector.tensor_tensor(top[0:n], lse[0:n, 0], lse[0:n, 1], ALU.max).then_inc(share_step, 1)
                dve.wait_ge(share_step, s + 1)
                nc.vector.tensor_tensor(top[0:n], top[0:n], lse[0:n, 2], ALU.max).then_inc(share_step, 1)
                dve.wait_ge(share_step, s + 2)
                nc.vector.tensor_tensor(share[0:n], lse[0:n], top[0:n].unsqueeze(1).to_broadcast([n, 3, H]), ALU.subtract) \
                    .then_inc(share_step, 1)
                dve.wait_ge(z_exp, item + 1)
                nc.vector.tensor_scalar(work[0:n, 0, :], work[0:n, 0, :], 1.0, None, ALU.add).then_inc(silu_step, 1)
                dve.wait_ge(share_exp, item + 1)
                nc.vector.tensor_tensor(total[0:n], share[0:n, 0], share[0:n, 1], ALU.add).then_inc(share_step, 1)
                dve.wait_ge(share_step, s + 4)
                nc.vector.tensor_tensor(total[0:n], total[0:n], share[0:n, 2], ALU.add).then_inc(share_step, 1)
                dve.wait_ge(share_step, s + 5)
                nc.vector.reciprocal(total[0:n], total[0:n]).then_inc(share_step, 1)
                dve.wait_ge(share_step, s + 6)
                nc.vector.tensor_tensor(share[0:n], share[0:n], total[0:n].unsqueeze(1).to_broadcast([n, 3, H]), ALU.mult) \
                    .then_inc(share_step, 1)
                dve.wait_ge(share_step, s + 7)
                nc.vector.tensor_tensor(o[0:n, 1:4, :].rearrange("p b (h d) -> p (b h) d", d=DH),
                                        o[0:n, 1:4, :].rearrange("p b (h d) -> p (b h) d", d=DH),
                                        share[0:n].rearrange("p b h -> p (b h)").unsqueeze(2).to_broadcast([n, 3 * H, DH]),
                                        ALU.mult).then_inc(share_step, 1)
                dve.wait_ge(share_step, s + 8)
                nc.vector.tensor_tensor(o[0:n, 1, :], o[0:n, 1, :], o[0:n, 2, :], ALU.add).then_inc(share_step, 1)
                dve.wait_ge(share_step, s + 9)
                nc.vector.tensor_tensor(o[0:n, 1, :], o[0:n, 1, :], o[0:n, 3, :], ALU.add).then_inc(share_step, 1)
                dve.wait_ge(silu_step, 3 * item + 1)
                nc.vector.reciprocal(work[0:n, 0, :], work[0:n, 0, :]).then_inc(silu_step, 1)
                dve.wait_ge(silu_step, 3 * item + 2)
                nc.vector.tensor_tensor(work[0:n, 0, :], work[0:n, 0, :], z[0:n, :], ALU.mult).then_inc(silu_step, 1)
                dve.wait_ge(rms_done, item + 1)
                dve.wait_ge(silu_step, 3 * item + 3)
                for i in range(2):
                    cols = slice(i * W, (i + 1) * W)
                    nc.vector.scalar_tensor_tensor(out=work[0:n, 0, cols], in0=o[0:n, i, :], scalar=stat[0:n, 2, i:i + 1],
                                                   in1=work[0:n, 0, cols], op0=ALU.mult, op1=ALU.mult).then_inc(y_done, 1)

            def low(item, what):
                n = rows_of(item)
                hi, lo, hi_done, split = {"y": (yT_hi, yT_lo, y_hi, y_split), "x1": (xT_hi, xT_lo, x1_hi, x1_split)}[what]
                for b in range(2):
                    dve.wait_ge(hi_done, 2 * item + b + 1)
                    src = T[:, b, :].rearrange("p (c r) -> p c r", r=P)[:, :, 0:n]
                    nc.vector.tensor_tensor(lo[:, 4 * b:4 * b + 4, 0:n], src, hi[:, 4 * b:4 * b + 4, 0:n].bitcast(F32),
                                            ALU.subtract).then_inc(split, 1)

            def low_p(item):
                n = rows_of(item)
                dve.wait_ge(p_hi, item + 1)
                src = T[:, 0, 0:PC * P].rearrange("p (c r) -> p c r", r=P)[:, :, 0:n]
                nc.vector.tensor_tensor(pT_lo[:, :, 0:n], src, pT_hi[:, :, 0:n].bitcast(F32), ALU.subtract).then_inc(p_split, 1)

            def residual(item, slot, use):
                n = rows_of(item)
                dve.wait_ge(x_loaded[slot], 16 * use + 16)
                for g in range(2):
                    dve.wait_ge(out_done, 2 * item + g + 1)
                    cols = slice(g * 512, (g + 1) * 512)
                    nc.vector.tensor_tensor(x[0:n, slot, cols], x[0:n, slot, cols], Out[0:n, g, :], ALU.add) \
                        .then_inc(x1_done, 1)

            def final(item, slot, use):
                n = rows_of(item)
                f = FS * item
                out = work[0:n, 1, :]
                dve.wait_ge(gate_exp, 2 * item + 2)
                nc.vector.tensor_scalar(out, out, 1.0, None, ALU.add).then_inc(final_step, 1)
                dve.wait_ge(final_step, f + 1)
                nc.vector.reciprocal(out, out).then_inc(final_step, 1)
                dve.wait_ge(ple_done, item + 1)
                dve.wait_ge(final_step, f + 2)
                nc.vector.tensor_tensor(out, out, Ple[0:n, :, :].rearrange("p a c -> p (a c)"), ALU.mult).then_inc(final_step, 1)
                dve.wait_ge(final_step, f + 3)
                nc.vector.tensor_tensor(out, out, x[0:n, slot, :], ALU.add).then_inc(final_step, 1)

            def body(item, slot, use):
                if not first(item):
                    low(item - 1, "x1")
                if not last(item):
                    prepare(item + 1)
                if not first(item):
                    low_p(item - 1)
                residual(item, slot, use)
                if not last(item):
                    low(item + 1, "y")
                if not first(item):
                    final(*before(item, slot, use))

            def leave():
                low(TILES, "x1")
                low_p(TILES)
                final(TILES, 0, TILES // 2)

            pipeline(dve, enter, body, leave)

        @block.scalar
        def _(act):
            load_exp_ln_table(nc, act)

            def enter():
                act.wait_ge(consts, 48)
                for c, (src, hi, lo, k) in enumerate(sets):
                    act.wait_ge(w_loaded[c % 2], 16 * (c // 2 + 1))
                    nc.scalar.activation(hi[:, k, :], work[:, c % 2, :], ACT.Copy,
                                         scale=g_out[:, k:k + 1] if c < KC else 1.0).then_inc(w_hi_done, 1)
                act.wait_ge(w_split, NW)
                prepare(0)
                high(0, "y")

            def prepare(item):
                n = rows_of(item)
                act.wait_ge(in_loaded, 16 * 7 * item + 16 * 7)
                if not first(item):
                    act.wait_ge(y_turned, 2 * item)
                    act.wait_ge(squared, 2 * item)
                    act.wait_ge(mean_done, item)
                nc.scalar.activation(work[0:n, 0, :], z[0:n, :], ACT.Exp, scale=-1.0).then_inc(z_exp, 1)
                nc.scalar.activation(junk[0:n, :], o[0:n, 0, :], ACT.Square, accum_out=stat[0:n, 0, 0:1]).then_inc(squared, 1)
                act.wait_ge(share_step, SH * item + 3)
                nc.scalar.activation(share[0:n], share[0:n], ACT.Exp).then_inc(share_exp, 1)
                act.wait_ge(share_step, SH * item + 10)
                act.wait_ge(squared, 2 * item + 1)
                nc.scalar.activation(junk[0:n, :], o[0:n, 1, :], ACT.Square, accum_out=stat[0:n, 0, 1:2]).then_inc(squared, 1)

            def high(item, what):
                n = rows_of(item)
                hi, hi_done, turned = {"y": (yT_hi, y_hi, y_turned), "x1": (xT_hi, x1_hi, x1_turned)}[what]
                for b in range(2):
                    act.wait_ge(turned, 2 * item + b + 1)
                    src = T[:, b, :].rearrange("p (c r) -> p c r", r=P)[:, :, 0:n]
                    nc.scalar.activation(hi[:, 4 * b:4 * b + 4, 0:n], src, ACT.Copy).then_inc(hi_done, 1)

            def high_p(item):
                n = rows_of(item)
                act.wait_ge(p_turned, item + 1)
                src = T[:, 0, 0:PC * P].rearrange("p (c r) -> p c r", r=P)[:, :, 0:n]
                nc.scalar.activation(pT_hi[:, :, 0:n], src, ACT.Copy).then_inc(p_hi, 1)

            def gate(item):
                n = rows_of(item)
                if first(item):
                    act.wait_ge(w_split, NW)
                else:
                    act.wait_ge(stored, 16 * item)
                for g in range(2):
                    act.wait_ge(gate_done, 2 * item + g + 1)
                    nc.scalar.activation(work[0:n, 1, g * 512:(g + 1) * 512], Gate[0:n, g, :], ACT.Exp, scale=-1.0) \
                        .then_inc(gate_exp, 1)

            def body(item, slot, use):
                if not first(item):
                    high(item - 1, "x1")
                if not last(item):
                    prepare(item + 1)
                if not first(item):
                    high_p(item - 1)
                if not last(item):
                    high(item + 1, "y")
                if not first(item):
                    gate(item - 1)

            def leave():
                high(TILES, "x1")
                high_p(TILES)
                gate(TILES)

            pipeline(act, enter, body, leave)

        @block.tensor
        def _(pe):
            def split_product(dst, n, xh, xl, wh, wl, chunks, g):
                cols = slice(g * 512, (g + 1) * 512)
                for k in range(chunks):
                    nc.tensor.matmul(dst[0:n, g, :], xh[:, k, 0:n], wh[:, k, cols], start=(k == 0), stop=False)
                    nc.tensor.matmul(dst[0:n, g, :], xh[:, k, 0:n], wl[:, k, cols], start=False, stop=False)
                    mm = nc.tensor.matmul(dst[0:n, g, :], xl[:, k, 0:n], wh[:, k, cols], start=False, stop=(k == chunks - 1))
                return mm

            def turn(src, n, b, chunks, turned):
                for c in range(chunks):
                    k = 4 * b + c
                    tr = nc.tensor.transpose(T[:, b, c * P:c * P + n], src[:, k * P:(k + 1) * P], ident[0:n, 0:n])
                tr.then_inc(turned, 1)

            def turn_y(item):
                n = rows_of(item)
                for b in range(2):
                    pe.wait_ge(y_done, 2 * item + b + 1)
                    if not first(item):
                        if isinstance(item, int) and item == 1:
                            pe.wait_ge(y_split, b + 1)
                        elif b == 0:
                            pe.wait_ge(p_split, item - 1)
                        else:
                            pe.wait_ge(x1_split, 2 * item - 2)
                    turn(work[0:n, 0, :], n, b, 4, y_turned)

            def turn_x1(item, slot, use):
                n = rows_of(item)
                pe.wait_ge(x1_done, 2 * item + 2)
                for b in range(2):
                    if not last(item):
                        pe.wait_ge(y_split, 2 * item + 3 + b)
                    elif b == 0:
                        pe.wait_ge(p_split, item)
                    else:
                        pe.wait_ge(x1_split, 2 * item)
                    turn(x[0:n, slot, :], n, b, 4, x1_turned)

            def turn_p(item):
                n = rows_of(item)
                pe.wait_ge(p_loaded, 16 * item + 16)
                pe.wait_ge(x1_split, 2 * item + 1)
                turn(p_in[0:n, :], n, 0, PC, p_turned)

            def project_out(item, g):
                n = rows_of(item)
                if g == 0:
                    pe.wait_ge(y_split, 2 * item + 2)
                if not first(item):
                    pe.wait_ge(x1_done, 2 * item - 1 + g)
                split_product(Out, n, yT_hi, yT_lo, wo_hi, wo_lo, KC, g).then_inc(out_done, 1)

            def gate_ple(item):
                n = rows_of(item)
                pe.wait_ge(x1_split, 2 * item + 2)
                for g in range(2):
                    if not first(item):
                        pe.wait_ge(gate_exp, 2 * item - 1 + g)
                    split_product(Gate, n, xT_hi, xT_lo, wg_hi, wg_lo, KC, g).then_inc(gate_done, 1)
                pe.wait_ge(p_split, item + 1)
                if not first(item):
                    pe.wait_ge(final_step, FS * item - 1)
                for g in range(2):
                    mm = split_product(Ple, n, pT_hi, pT_lo, wp_hi, wp_lo, PC, g)
                mm.then_inc(ple_done, 1)

            def enter():
                pe.wait_ge(consts, 48)
                turn_y(0)

            def body(item, slot, use):
                if not first(item):
                    turn_x1(*before(item, slot, use))
                project_out(item, 0)
                if not first(item):
                    turn_p(item - 1)
                project_out(item, 1)
                if not last(item):
                    turn_y(item + 1)
                if not first(item):
                    gate_ple(item - 1)

            def leave():
                turn_x1(TILES, 0, TILES // 2)
                turn_p(TILES)
                gate_ple(TILES)

            pipeline(pe, enter, body, leave)


def build(nc, t):
    for name, shape in (("q_sb", [SEQ, W]), ("z_sb", [SEQ, W]), ("q_dl", [SEQ, W]), ("z_dl", [SEQ, W]),
                        ("q_sb_s", [NS, W]), ("z_sb_s", [NS, W]), ("q_dl_s", [NS, W]), ("z_dl_s", [NS, W]),
                        ("o_sb", [SEQ, W]), ("o_dil", [3, SEQ, W]), ("lse_dil", [3, SEQ, H]),
                        ("o_sb_s", [NS, W]), ("o_dl_s", [NS, W])):
        t[name] = nc.dram_tensor(f"scratch_{name}", shape, F32).ap()
    with nc.semaphore("tick") as tick:
        TICK[0] = tick
        project(nc, t, 0)
        project(nc, t, 1)
        stick_breaking_prompt(nc, t)
        dilated_prompt(nc, t)
        stick_breaking_sample(nc, t)
        dilated_sample(nc, t)
        merge(nc, t)


INPUTS = ["x_prompt", "x_sample", "cache_k_sb", "cache_v_sb", "cache_k_win", "cache_v_win", "page_table",
          "p_prompt", "p_sample", "attn_norm", "w_in", "sb_bias", "q_norm_dil", "k_norm_dil", "out_norm_sb",
          "out_norm_dil", "w_out", "w_ple", "w_ple_gate"]
OUTPUTS = [("y_prompt", (1, SEQ, D)), ("y_sample", (DEC_B, DEC_S, D)),
           ("k_sb_p", (1, 1, SEQ, H, DH)), ("v_sb_p", (1, 1, SEQ, H, DH)),
           ("k_sb_s", (1, DEC_B, DEC_S, H, DH)), ("v_sb_s", (1, DEC_B, DEC_S, H, DH)),
           ("k_win_p", (1, 1, SEQ, H, DH)), ("v_win_p", (1, 1, SEQ, H, DH)),
           ("k_win_s", (1, DEC_B, WIN, H, DH)), ("v_win_s", (1, DEC_B, WIN, H, DH))]


def shape_constants():
    import numpy as np
    f32 = np.float32
    k, q = np.arange(P)[:, None], np.arange(P)[None, :]
    inv = np.power(f32(500000.0), -(np.arange(ROT // 2, dtype=f32) * f32(2.0) / f32(ROT))).astype(f32)
    pos = np.concatenate([np.resize(PAGES * PAGE + np.arange(DEC_S), P), np.arange(SEQ)]).astype(f32)
    ang = (pos[:, None] * inv[None, :]).astype(f32)
    rope = np.concatenate([np.cos(ang), np.sin(ang)], 1).astype(f32).reshape(TILES + 1, P, ROT)
    out = {"ident": np.eye(P, dtype=f32), "rope": rope}
    out["suffix"] = np.stack([-(k >= q).astype(f32), -np.ones((P, P), f32)])
    q, k = np.arange(P)[:, None], np.arange(P)[None, :]
    own = np.where(k <= q, 0.0, NEG)
    before = np.where(k >= q, 0.0, NEG)
    never = np.full((P, P), NEG)
    out["masks"] = np.stack([np.concatenate([own, never, before, own], 1),
                             np.concatenate([before, own, before, own], 1),
                             np.concatenate([own, own, own, own], 1)]).astype(f32)
    tok = (np.arange(H * DEC_S) % DEC_S)[:, None]
    dist = 512 + tok - np.arange(512)[None, :]
    recent = (dist <= 128).astype(f32) + ((dist % 4 == 0) & (dist <= 512))
    strided = np.broadcast_to(tok == np.repeat(np.arange(DEC_S), P)[None, :], (H * DEC_S, 512))
    fresh = (np.arange(DEC_S)[None, :] <= tok) + 2 * (np.arange(DEC_S)[None, :] == tok)
    out["win_count"] = np.concatenate([recent, strided, fresh], 1).astype(f32)
    out["win_mask"] = np.where(out["win_count"] > 0, 0.0, NEG).astype(f32)
    out["own_head"] = (np.arange(H * DEC_S)[:, None] // DEC_S == np.arange(W)[None, :] // DH).astype(f32)
    out["valid_new"] = (np.arange(DEC_S)[None, :] < tok).astype(f32)
    out["pick"] = (tok == np.arange(DEC_S)[None, :]).astype(f32)
    out["lse_one"] = np.repeat(np.array([[0.0, -1e30, -1e30]]), NS, 0).repeat(H, 1).astype(f32)
    return out


def kernel(**inputs):
    import numpy as np
    import concourse.bacc as bacc
    from concourse.bass_utils import run_bass_kernel_spmd as run

    nc = bacc.Bacc("TRN2", target_bir_lowering=False, num_devices=1)
    arrays, t = {}, {}
    for name in INPUTS:
        arrays[f"in_{name}"] = np.ascontiguousarray(inputs[name])
    for name, a in shape_constants().items():
        arrays[f"in_{name}"] = a
    for name, a in arrays.items():
        t[name[3:]] = nc.dram_tensor(name, a.shape, mybir.dt.from_np(a.dtype), kind="ExternalInput").ap()
    for name, shape in OUTPUTS:
        t[name] = nc.dram_tensor(f"out_{name}", shape, F32, kind="ExternalOutput").ap()
    build(nc, t)
    r = run(nc, [arrays], core_ids=[0])
    return tuple(r.results[0][f"out_{name}"] for name, _ in OUTPUTS)
```
